# Optimizing a Trainium2 kernel written in Bass

```python
import math
import jax, jax.numpy as jnp
from jax import lax
import numpy as np

D_MODEL = 1024
BATCH = 1
SEQ = 256
DEPTH = 1

HEAD_DIM = 64
BLOCK = 128
RMS_EPS = 1e-6
SUBLN_EPS = 1e-5
A_HEADS = 4
A_QK = A_HEADS * 2 * HEAD_DIM
A_WIDTH = A_HEADS * 2 * HEAD_DIM
B_HEADS = 8
B_KV_HEADS = 2
B_GROUP = B_HEADS // B_KV_HEADS
B_WIDTH = B_HEADS * HEAD_DIM
B_KV = B_KV_HEADS * HEAD_DIM
WINDOW = 128
C_HEADS = 8
C_WIDTH = C_HEADS * HEAD_DIM
N_BRANCH = 3
SPLITS = (A_QK, A_QK, A_WIDTH, A_WIDTH,
          B_WIDTH, B_KV, B_KV, B_WIDTH,
          C_WIDTH, C_WIDTH, C_WIDTH, C_HEADS, C_WIDTH,
          N_BRANCH * D_MODEL)
D_IN = sum(SPLITS)


def rms_norm(x, gain, eps):
    xf = x.astype(jnp.float32)
    y = xf * lax.rsqrt(jnp.mean(xf * xf, axis=-1, keepdims=True) + eps)
    return (y * gain.astype(jnp.float32)).astype(x.dtype)

def alibi_slopes(n_heads):
    return 2.0 ** (-8.0 * jnp.arange(1, n_heads + 1, dtype=jnp.float32) / n_heads)

def diff_attention(q, k, v, lam, slopes):
    B, S, H, _, d = q.shape
    nb = S // BLOCK
    scale = d ** -0.5
    qb = jnp.moveaxis(q.reshape(B, nb, BLOCK, H, 2, d), 1, 0)
    k_pos = jnp.arange(S)

    def one_block(args):
        qblk, start = args
        s = jnp.einsum('bqhmd,bkhmd->bhmqk', qblk, k).astype(jnp.float32) * scale
        dist = (start + jnp.arange(BLOCK))[:, None] - k_pos[None, :]
        bias = jnp.where(dist >= 0, -slopes[:, None, None] * dist.astype(jnp.float32), -jnp.inf)
        p = jax.nn.softmax(s + bias[None, :, None], axis=-1)
        w = p[:, :, 0] - lam * p[:, :, 1]
        return jnp.einsum('bhqk,bkhe->bqhe', w.astype(v.dtype), v)

    out = lax.map(one_block, (qb, jnp.arange(nb) * BLOCK))
    return jnp.moveaxis(out, 0, 1).reshape(B, S, H, v.shape[-1])

def sliding_window_attention(q, k, v, sinks, slopes):
    B, S, HQ, d = q.shape
    KV = k.shape[2]
    G = HQ // KV
    nb = S // BLOCK
    scale = d ** -0.5
    qb = q.reshape(B, nb, BLOCK, KV, G, d)

    def banded(t):
        tb = t.reshape(B, nb, BLOCK, KV, d)
        prev = jnp.concatenate([jnp.zeros_like(tb[:, :1]), tb[:, :-1]], axis=1)
        return jnp.concatenate([prev, tb], axis=2)

    kb, vb = banded(k), banded(v)
    s = jnp.einsum('bnqhgd,bnkhd->bnhgqk', qb, kb).astype(jnp.float32) * scale
    i = jnp.arange(BLOCK)[:, None]
    j = jnp.arange(2 * BLOCK)[None, :]
    dist = i - j + BLOCK
    key_pos = jnp.arange(nb)[:, None, None] * BLOCK + j - BLOCK
    valid = (dist >= 0) & (dist < WINDOW) & (key_pos >= 0)
    bias = -slopes.reshape(KV, G)[:, :, None, None] * dist.astype(jnp.float32)
    s = jnp.where(valid[None, :, None, None], s + bias[None, None], -jnp.inf)
    sink = sinks.astype(jnp.float32).reshape(KV, G)[None, None, :, :, None, None]
    m = jnp.maximum(jnp.max(s, axis=-1, keepdims=True), sink)
    e = jnp.exp(s - m)
    p = e / (jnp.sum(e, axis=-1, keepdims=True) + jnp.exp(sink - m))
    out = jnp.einsum('bnhgqk,bnkhd->bnqhgd', p.astype(v.dtype), vb)
    return out.reshape(B, S, HQ * d)

def forgetting_attention(q, k, v, logf):
    B, S, H, d = q.shape
    nb = S // BLOCK
    scale = d ** -0.5
    c = jnp.cumsum(logf, axis=1)
    c_k = jnp.transpose(c, (0, 2, 1))
    qb = jnp.moveaxis(q.reshape(B, nb, BLOCK, H, d), 1, 0)
    cb = jnp.moveaxis(c.reshape(B, nb, BLOCK, H), 1, 0)
    k_pos = jnp.arange(S)

    def one_block(args):
        qblk, cblk, start = args
        s = jnp.einsum('bqhd,bkhd->bhqk', qblk, k).astype(jnp.float32) * scale
        decay = jnp.transpose(cblk, (0, 2, 1))[:, :, :, None] - c_k[:, :, None, :]
        dist = (start + jnp.arange(BLOCK))[:, None] - k_pos[None, :]
        s = jnp.where((dist >= 0)[None, None], s + decay, -jnp.inf)
        p = jax.nn.softmax(s, axis=-1)
        return jnp.einsum('bhqk,bkhd->bqhd', p.astype(v.dtype), v)

    out = lax.map(one_block, (qb, cb, jnp.arange(nb) * BLOCK))
    return jnp.moveaxis(out, 0, 1).reshape(B, S, H * d)

def first_inputs(seed: int = 0) -> dict:
    key = jax.random.key(seed)
    ks = jax.random.split(key, 16)
    f32 = jnp.float32
    nrm = lambda k, shape: jax.random.normal(k, shape, dtype=f32)
    return {
        "x": nrm(ks[0], (BATCH, SEQ, D_MODEL)),
        "norm_gain": 1.0 + 0.05 * nrm(ks[1], (DEPTH, D_MODEL)),
        "w_in": nrm(ks[2], (DEPTH, D_MODEL, D_IN)) * D_MODEL ** -0.5,
        "b_forget": 0.1 * nrm(ks[3], (DEPTH, C_HEADS)),
        "lambda_q1": 0.1 * nrm(ks[4], (DEPTH, HEAD_DIM)),
        "lambda_k1": 0.1 * nrm(ks[5], (DEPTH, HEAD_DIM)),
        "lambda_q2": 0.1 * nrm(ks[6], (DEPTH, HEAD_DIM)),
        "lambda_k2": 0.1 * nrm(ks[7], (DEPTH, HEAD_DIM)),
        "subln_gain": 1.0 + 0.05 * nrm(ks[8], (DEPTH, 2 * HEAD_DIM)),
        "sinks": 0.5 * nrm(ks[9], (DEPTH, B_HEADS)),
        "w_up_a": nrm(ks[10], (DEPTH, A_WIDTH, D_MODEL)) * A_WIDTH ** -0.5,
        "w_up_b": nrm(ks[11], (DEPTH, B_WIDTH, D_MODEL)) * B_WIDTH ** -0.5,
        "w_up_c": nrm(ks[12], (DEPTH, C_WIDTH, D_MODEL)) * C_WIDTH ** -0.5,
        "w_o": nrm(ks[13], (DEPTH, D_MODEL, D_MODEL)) * D_MODEL ** -0.5,
        "final_gain": 1.0 + 0.05 * nrm(ks[14], (D_MODEL,)),
    }

def first_block(x, norm_gain, w_in, b_forget, lambda_q1, lambda_k1, lambda_q2, lambda_k2,
              subln_gain, sinks, w_up_a, w_up_b, w_up_c, w_o, final_gain):
    B, S, D = x.shape
    offsets = np.cumsum(SPLITS)[:-1].tolist()
    slopes_a = alibi_slopes(A_HEADS)
    slopes_b = alibi_slopes(B_HEADS)
    for l in range(DEPTH):
        h = rms_norm(x, norm_gain[l], RMS_EPS)
        proj = jnp.einsum('bsd,de->bse', h, w_in[l])
        (qa, ka, va, ga, qb, kb, vb, gb,
         qc, kc, vc, fc, gc, gm) = jnp.split(proj, offsets, axis=-1)

        lam_init = 0.8 - 0.6 * math.exp(-0.3 * l)
        lam = (jnp.exp(jnp.sum(lambda_q1[l].astype(jnp.float32) * lambda_k1[l].astype(jnp.float32)))
               - jnp.exp(jnp.sum(lambda_q2[l].astype(jnp.float32) * lambda_k2[l].astype(jnp.float32)))
               + lam_init)
        ya = diff_attention(qa.reshape(B, S, A_HEADS, 2, HEAD_DIM),
                            ka.reshape(B, S, A_HEADS, 2, HEAD_DIM),
                            va.reshape(B, S, A_HEADS, 2 * HEAD_DIM), lam, slopes_a)
        ya = (rms_norm(ya, subln_gain[l], SUBLN_EPS) * (1.0 - lam_init)).reshape(B, S, A_WIDTH)

        yb = sliding_window_attention(qb.reshape(B, S, B_HEADS, HEAD_DIM),
                                      kb.reshape(B, S, B_KV_HEADS, HEAD_DIM),
                                      vb.reshape(B, S, B_KV_HEADS, HEAD_DIM),
                                      sinks[l], slopes_b)

        logf = jax.nn.log_sigmoid(fc.astype(jnp.float32) + b_forget[l].astype(jnp.float32))
        yc = forgetting_attention(qc.reshape(B, S, C_HEADS, HEAD_DIM),
                                  kc.reshape(B, S, C_HEADS, HEAD_DIM),
                                  vc.reshape(B, S, C_HEADS, HEAD_DIM), logf)

        ua = jnp.einsum('bse,ed->bsd', ya * jax.nn.silu(ga), w_up_a[l])
        ub = jnp.einsum('bse,ed->bsd', yb * jax.nn.silu(gb), w_up_b[l])
        uc = jnp.einsum('bse,ed->bsd', yc * jax.nn.silu(gc), w_up_c[l])
        gates = jax.nn.sigmoid(gm.reshape(B, S, N_BRANCH, D))
        merged = gates[:, :, 0] * ua + gates[:, :, 1] * ub + gates[:, :, 2] * uc
        x = x + jnp.einsum('bsd,de->bse', merged, w_o[l])
    return rms_norm(x, final_gain, RMS_EPS)


DEPTH_2 = 2

GRID_W = 64
CTX_LEN = 256
EPS = 1e-6

NA_HEADS = 8
NA_HEAD_DIM = 64
NA_WIDTH = NA_HEADS * NA_HEAD_DIM
NA_KH = 8
NA_KW = 16

HG_HEADS = 4
HG_KEY_DIM = 128
HG_VAL_DIM = 128
HG_KEY = HG_HEADS * HG_KEY_DIM
HG_VAL = HG_HEADS * HG_VAL_DIM
HG_CHUNK = 32

D_FF = 2816
CONV_W = 3

N_EVEN = (DEPTH_2 + 1) // 2
N_ODD = DEPTH_2 // 2
EV_SIZES = [NA_WIDTH, NA_WIDTH, NA_WIDTH, HG_KEY, HG_KEY, HG_KEY, HG_VAL, HG_VAL]
EV_IN = sum(EV_SIZES)
EV_SPLITS = [int(s) for s in np.cumsum(EV_SIZES)[:-1]]
EV_MIX = NA_WIDTH + HG_VAL


def rms_norm_2(x, w):
    xf = x.astype(jnp.float32)
    y = xf * lax.rsqrt(jnp.mean(xf * xf, axis=-1, keepdims=True) + EPS)
    return (y * w.astype(jnp.float32)).astype(x.dtype)

def modulate(h, shift, scale):
    return h * (1.0 + scale[:, None, :]) + shift[:, None, :]

def dwconv3(h, w, b):
    hp = jnp.pad(h, ((0, 0), (1, 1), (0, 0)))
    return hp[:, :-2] * w[0] + hp[:, 1:-1] * w[1] + hp[:, 2:] * w[2] + b

def neighbourhood_attention(q, k, v, k_ctx, v_ctx, rpb):
    b, s, h, d = q.shape
    rows = s // GRID_W
    kh = min(NA_KH, rows)
    kw = NA_KW
    scale = d ** -0.5
    cols = np.arange(GRID_W)
    col_start = np.clip(cols - kw // 2, 0, GRID_W - kw)
    col_idx = col_start[:, None] + np.arange(kw)[None, :]
    col_rel = col_idx - cols[:, None] + (NA_KW - 1)
    rpb_c = rpb.astype(jnp.float32)[:, :, col_rel]
    qg = q.reshape(b, rows, GRID_W, h, d)
    kg = k.reshape(b, rows, GRID_W, h, d)
    vg = v.reshape(b, rows, GRID_W, h, d)

    def row_block(args):
        r, q_row = args
        r0 = jnp.clip(r - kh // 2, 0, rows - kh)
        k_rows = lax.dynamic_slice_in_dim(kg, r0, kh, axis=1)
        v_rows = lax.dynamic_slice_in_dim(vg, r0, kh, axis=1)
        k_nb = k_rows[:, :, col_idx]
        v_nb = v_rows[:, :, col_idx]
        row_rel = r0 + jnp.arange(kh) - r + (NA_KH - 1)
        bias = rpb_c[:, row_rel].transpose(0, 2, 1, 3)
        s_loc = jnp.einsum('bqhd,brqwhd->bhqrw', q_row, k_nb).astype(jnp.float32) * scale + bias[None]
        s_ctx = jnp.einsum('bqhd,bkhd->bhqk', q_row, k_ctx).astype(jnp.float32) * scale
        logits = jnp.concatenate([s_loc.reshape(b, h, GRID_W, kh * kw), s_ctx], axis=-1)
        p = jax.nn.softmax(logits, axis=-1).astype(v.dtype)
        p_loc = p[..., :kh * kw].reshape(b, h, GRID_W, kh, kw)
        p_ctx = p[..., kh * kw:]
        return (jnp.einsum('bhqrw,brqwhd->bqhd', p_loc, v_nb)
                + jnp.einsum('bhqk,bkhd->bqhd', p_ctx, v_ctx))

    out = lax.map(row_block, (jnp.arange(rows), qg.transpose(1, 0, 2, 3, 4)))
    return out.transpose(1, 0, 2, 3, 4).reshape(b, s, h, d)

def context_attention(q, k, v):
    s = jnp.einsum('bqhd,bkhd->bhqk', q, k).astype(jnp.float32) * (q.shape[-1] ** -0.5)
    p = jax.nn.softmax(s, axis=-1).astype(v.dtype)
    return jnp.einsum('bhqk,bkhd->bqhd', p, v)

def hgrn2_scan(q, k, v, log_f, s0):
    b, h, l, _ = q.shape
    n = l // HG_CHUNK

    def to_chunks(t):
        return t.reshape(b, h, n, HG_CHUNK, t.shape[-1]).transpose(2, 0, 1, 3, 4)

    causal_in_chunk = jnp.tril(jnp.ones((HG_CHUNK, HG_CHUNK), dtype=bool))

    def step(state, inp):
        qc, kc, vc, gc = inp
        bcum = jnp.cumsum(gc, axis=2)
        btot = bcum[:, :, -1:]
        qe = qc * jnp.exp(bcum)
        ke = kc * jnp.exp(-bcum)
        att = jnp.where(causal_in_chunk, jnp.einsum('bhtk,bhsk->bhts', qe, ke), 0.0)
        o = jnp.einsum('bhtk,bhkv->bhtv', qe, state) + jnp.einsum('bhts,bhsv->bhtv', att, vc)
        kd = kc * jnp.exp(btot - bcum)
        new_state = jnp.exp(btot)[:, :, 0, :, None] * state + jnp.einsum('bhsk,bhsv->bhkv', kd, vc)
        return new_state, o

    s_end, o = lax.scan(step, s0, (to_chunks(q), to_chunks(k), to_chunks(v), to_chunks(log_f)))
    return o.transpose(1, 2, 0, 3, 4).reshape(b, h, l, v.shape[-1]), s_end

def hgrn2_final_state(k, v, log_f):
    bcum = jnp.cumsum(log_f, axis=2)
    return jnp.einsum('bhtk,bhtv->bhkv', k * jnp.exp(bcum[:, :, -1:] - bcum), v)

def _heads(a, dh):
    b, l, _ = a.shape
    return a.astype(jnp.float32).reshape(b, l, -1, dh).transpose(0, 2, 1, 3)

def _hg_gates(f_pres, i, lb):
    v = _heads(i, HG_VAL_DIM)
    dirs = []
    for d, f_pre in enumerate(f_pres):
        lbd = lb[d].astype(jnp.float32).reshape(HG_HEADS, 1, HG_KEY_DIM)
        fg = lbd + (1.0 - lbd) * jax.nn.sigmoid(_heads(f_pre, HG_KEY_DIM))
        dirs.append((1.0 - fg, jnp.log(fg)))
    return v, dirs

def _hg_readout(o, g, norm_w):
    b, _, l, _ = o.shape
    o = o * lax.rsqrt(jnp.mean(o * o, axis=-1, keepdims=True) + EPS)
    o = o * norm_w.astype(jnp.float32).reshape(HG_HEADS, 1, HG_VAL_DIM)
    o = o.transpose(0, 2, 1, 3).reshape(b, l, HG_VAL)
    return (o * jax.nn.silu(g.astype(jnp.float32))).astype(g.dtype)

def hgrn2_mixer(q, fs, i, g, cq, cfs, ci, cg, lb, norm_w, with_ctx_out):
    v, dirs = _hg_gates(fs, i, lb)
    vc, dirs_c = _hg_gates(cfs, ci, lb)
    qh = jax.nn.silu(_heads(q, HG_KEY_DIM))
    if with_ctx_out:
        cqh = jax.nn.silu(_heads(cq, HG_KEY_DIM))
    b = q.shape[0]
    zero_state = jnp.zeros((b, HG_HEADS, HG_KEY_DIM, HG_VAL_DIM), jnp.float32)
    o_lat = jnp.zeros_like(qh[..., :HG_VAL_DIM])
    o_ctx = None
    for d in range(2):
        tr = (lambda a: jnp.flip(a, axis=2)) if d == 1 else (lambda a: a)
        k, lf = dirs[d]
        kc, lfc = dirs_c[d]
        if with_ctx_out:
            oc, s_ctx = hgrn2_scan(tr(cqh), tr(kc), tr(vc), tr(lfc), zero_state)
            o_ctx = tr(oc) if o_ctx is None else o_ctx + tr(oc)
        else:
            s_ctx = hgrn2_final_state(tr(kc), tr(vc), tr(lfc))
        ol, _ = hgrn2_scan(tr(qh), tr(k), tr(v), tr(lf), s_ctx)
        o_lat = o_lat + tr(ol)
    y = _hg_readout(o_lat, g, norm_w)
    y_ctx = _hg_readout(o_ctx, cg, norm_w) if with_ctx_out else None
    return y, y_ctx

def even_mixer(h, h_ctx, w_in, w_out, rpb, lb, hg_norm_w, with_ctx_out):
    b, s, _ = h.shape
    na_q, na_k, na_v, hg_q, hg_ff, hg_fb, hg_i, hg_g = jnp.split(h @ w_in, EV_SPLITS, axis=-1)
    cna_q, cna_k, cna_v, chg_q, chg_ff, chg_fb, chg_i, chg_g = jnp.split(h_ctx @ w_in, EV_SPLITS, axis=-1)

    def nh(a):
        return a.reshape(a.shape[0], a.shape[1], NA_HEADS, NA_HEAD_DIM)

    a_lat = neighbourhood_attention(nh(na_q), nh(na_k), nh(na_v), nh(cna_k), nh(cna_v), rpb)
    g_lat, g_ctx = hgrn2_mixer(hg_q, (hg_ff, hg_fb), hg_i, hg_g,
                               chg_q, (chg_ff, chg_fb), chg_i, chg_g, lb, hg_norm_w, with_ctx_out)
    y = jnp.concatenate([a_lat.reshape(b, s, NA_WIDTH), g_lat], axis=-1) @ w_out
    y_ctx = None
    if with_ctx_out:
        a_ctx = context_attention(nh(cna_q), nh(cna_k), nh(cna_v))
        y_ctx = jnp.concatenate([a_ctx.reshape(b, h_ctx.shape[1], NA_WIDTH), g_ctx], axis=-1) @ w_out
    return y, y_ctx

def short_conv_mixer(h, w_in, conv_w, conv_b, w_out):
    gate_b, gate_c, u = jnp.split(h @ w_in, 3, axis=-1)
    return (gate_b * dwconv3(gate_c * u, conv_w, conv_b)) @ w_out

def conv_ffn(h, w_up, conv_w, conv_b, w_down):
    a, val = jnp.split(h @ w_up, 2, axis=-1)
    return (jax.nn.gelu(dwconv3(a, conv_w, conv_b), approximate=False) * val) @ w_down

def second_inputs(seed: int = 0) -> dict:
    key = jax.random.key(seed)
    ks = jax.random.split(key, 24)
    f32 = jnp.float32
    nrm = lambda k, shape, s: jax.random.normal(k, shape, f32) * s
    D = D_MODEL
    return {
        "x": nrm(ks[0], (BATCH, SEQ, D), 1.0),
        "c": nrm(ks[1], (BATCH, D), 1.0),
        "ctx": nrm(ks[2], (BATCH, CTX_LEN, D), 1.0),
        "c_ctx": nrm(ks[3], (D,), 1.0),
        "ada_w": nrm(ks[4], (DEPTH_2, D, 6 * D), 0.5 * D ** -0.5),
        "ada_b": nrm(ks[5], (DEPTH_2, 6 * D), 0.02),
        "norm_mix_w": 1.0 + nrm(ks[6], (DEPTH_2, D), 0.02),
        "norm_ffn_w": 1.0 + nrm(ks[7], (DEPTH_2, D), 0.02),
        "ev_w_in": nrm(ks[8], (N_EVEN, D, EV_IN), D ** -0.5),
        "ev_w_out": nrm(ks[9], (N_EVEN, EV_MIX, D), EV_MIX ** -0.5),
        "na_rpb": nrm(ks[10], (N_EVEN, NA_HEADS, 2 * NA_KH - 1, 2 * NA_KW - 1), 0.1),
        "hg_lb_logits": nrm(ks[11], (N_EVEN + 1, 2, HG_KEY), 0.1),
        "hg_norm_w": 1.0 + nrm(ks[12], (N_EVEN, HG_VAL), 0.02),
        "od_w_in": nrm(ks[13], (N_ODD, D, 3 * D), D ** -0.5),
        "od_conv_w": nrm(ks[14], (N_ODD, CONV_W, D), CONV_W ** -0.5),
        "od_conv_b": nrm(ks[15], (N_ODD, D), 0.02),
        "od_w_out": nrm(ks[16], (N_ODD, D, D), D ** -0.5),
        "ffn_w_up": nrm(ks[17], (DEPTH_2, D, 2 * D_FF), D ** -0.5),
        "ffn_conv_w": nrm(ks[18], (DEPTH_2, CONV_W, D_FF), CONV_W ** -0.5),
        "ffn_conv_b": nrm(ks[19], (DEPTH_2, D_FF), 0.02),
        "ffn_w_down": nrm(ks[20], (DEPTH_2, D_FF, D), D_FF ** -0.5),
        "final_norm_w": 1.0 + nrm(ks[21], (D,), 0.02),
    }

def second_block(x, c, ctx, c_ctx, ada_w, ada_b, norm_mix_w, norm_ffn_w, ev_w_in, ev_w_out,
              na_rpb, hg_lb_logits, hg_norm_w, od_w_in, od_conv_w, od_conv_b, od_w_out,
              ffn_w_up, ffn_conv_w, ffn_conv_b, ffn_w_down, final_norm_w):
    lb_all = jnp.cumsum(jax.nn.softmax(hg_lb_logits.astype(jnp.float32), axis=0), axis=0)[:N_EVEN]
    silu_c = jax.nn.silu(c)
    silu_cc = jax.nn.silu(c_ctx)[None]
    xc = ctx
    for layer in range(DEPTH_2):
        j = layer // 2
        is_even = layer % 2 == 0
        ctx_feeds_later = any(l % 2 == 0 for l in range(layer + 1, DEPTH_2))
        mod = silu_c @ ada_w[layer] + ada_b[layer]
        shift_m, scale_m, gate_m, shift_f, scale_f, gate_f = jnp.split(mod, 6, axis=-1)
        if is_even or ctx_feeds_later:
            mod_c = silu_cc @ ada_w[layer] + ada_b[layer]
            cshift_m, cscale_m, cgate_m, cshift_f, cscale_f, cgate_f = jnp.split(mod_c, 6, axis=-1)
            h_ctx = modulate(rms_norm_2(xc, norm_mix_w[layer]), cshift_m, cscale_m)
        h = modulate(rms_norm_2(x, norm_mix_w[layer]), shift_m, scale_m)
        if is_even:
            y, y_ctx = even_mixer(h, h_ctx, ev_w_in[j], ev_w_out[j], na_rpb[j], lb_all[j],
                                  hg_norm_w[j], ctx_feeds_later)
        else:
            y = short_conv_mixer(h, od_w_in[j], od_conv_w[j], od_conv_b[j], od_w_out[j])
            y_ctx = (short_conv_mixer(h_ctx, od_w_in[j], od_conv_w[j], od_conv_b[j], od_w_out[j])
                     if ctx_feeds_later else None)
        x = x + gate_m[:, None, :] * y
        h = modulate(rms_norm_2(x, norm_ffn_w[layer]), shift_f, scale_f)
        x = x + gate_f[:, None, :] * conv_ffn(h, ffn_w_up[layer], ffn_conv_w[layer],
                                              ffn_conv_b[layer], ffn_w_down[layer])
        if ctx_feeds_later:
            xc = xc + cgate_m[:, None, :] * y_ctx
            hc = modulate(rms_norm_2(xc, norm_ffn_w[layer]), cshift_f, cscale_f)
            xc = xc + cgate_f[:, None, :] * conv_ffn(hc, ffn_w_up[layer], ffn_conv_w[layer],
                                                     ffn_conv_b[layer], ffn_w_down[layer])
    return rms_norm_2(x, final_norm_w)


def setup_inputs(seed=0):
    out = dict(first_inputs(seed))
    for name, value in second_inputs(seed + 1).items():
        if name != "x":
            out[name + "_2"] = value
    return out


def reference(
    x, norm_gain, w_in, b_forget, lambda_q1, lambda_k1, lambda_q2, lambda_k2, subln_gain, sinks,
    w_up_a, w_up_b, w_up_c, w_o, final_gain, c_2, ctx_2, c_ctx_2, ada_w_2, ada_b_2,
    norm_mix_w_2, norm_ffn_w_2, ev_w_in_2, ev_w_out_2, na_rpb_2, hg_lb_logits_2, hg_norm_w_2,
    od_w_in_2, od_conv_w_2, od_conv_b_2, od_w_out_2, ffn_w_up_2, ffn_conv_w_2, ffn_conv_b_2,
    ffn_w_down_2, final_norm_w_2,
):
    x = first_block(
        x, norm_gain, w_in, b_forget, lambda_q1, lambda_k1, lambda_q2, lambda_k2, subln_gain,
        sinks, w_up_a, w_up_b, w_up_c, w_o, final_gain,
    )
    return second_block(
        x, c_2, ctx_2, c_ctx_2, ada_w_2, ada_b_2, norm_mix_w_2, norm_ffn_w_2, ev_w_in_2,
        ev_w_out_2, na_rpb_2, hg_lb_logits_2, hg_norm_w_2, od_w_in_2, od_conv_w_2, od_conv_b_2,
        od_w_out_2, ffn_w_up_2, ffn_conv_w_2, ffn_conv_b_2, ffn_w_down_2, final_norm_w_2,
    )


_drawn_inputs = setup_inputs


def setup_inputs(seed=0):
    import zlib

    import numpy as np

    out = dict(_drawn_inputs(seed))
    spreads = {}
    factors = {'b_forget': 4.962,
     'lambda_k1': 6.157,
     'lambda_q2': 6.471,
     'subln_gain': 3.796,
     'sinks': 6.484,
     'norm_mix_w_2': 4.522,
     'norm_ffn_w_2': 5.856,
     'na_rpb_2': 8.0,
     'hg_lb_logits_2': 8.0,
     'hg_norm_w_2': 8.0,
     'od_conv_b_2': 63.948,
     'ffn_conv_b_2': 8.0,
     'final_norm_w_2': 8.192}
    for name, (base, spread) in spreads.items():
        noise = np.random.default_rng([zlib.crc32(name.encode()), seed]).standard_normal(out[name].shape)
        drawn = base * np.exp(spread * noise) if base else spread * noise
        out[name] = __import__('jax').numpy.asarray(drawn.astype(out[name].dtype))
    for name, factor in factors.items():
        out[name] = (out[name] * factor).astype(out[name].dtype)
    return out
```

```python
from contextlib import ExitStack
import math

import concourse.bass as bass
from concourse import mybir

F32 = mybir.dt.float32
F32R = mybir.dt.float32r
I32 = mybir.dt.int32
U32 = mybir.dt.uint32
ALU = mybir.AluOpType
ACT = mybir.ActivationFunctionType
AX = mybir.AxisListType

P = 128
D = 1024
KT = D // P
S = 256
NT = S // P
HD = 64
SCALE = HD ** -0.5
EPS = 1e-6
SUBLN_EPS = 1e-5
LAM_INIT = 0.8 - 0.6 * math.exp(-0.3 * 0)
FAR = 1e30
RAW = 4
WRING = 4
HALF = 1024
CH = 32
NCH = S // CH
FF = 2816
FT = FF // P
TABLES = "natural_log_exp_and_others"

O_QA, O_KA, O_VA, O_GA = 0, 512, 1024, 1536
O_QB, O_KB, O_GB = 2048, 2560, 2816
O_QC, O_KC, O_VC, O_FC, O_GC, O_GM = 3328, 3840, 4352, 4864, 4872, 5384
E_NQ, E_NK, E_NV, E_HQ, E_HF, E_HB, E_HI, E_HG = [512 * i for i in range(8)]

C_NG, C_FG, C_MIX, C_FFN, C_HGN, C_LB, C_C, C_CC, C_ODW, C_ODB, C_FN, C_SUB = (
    0, 8, 16, 32, 48, 52, 68, 76, 84, 108, 116, 124)
C_ADAB, C_FCW, C_FCB = 128, 256, 256 + 66


def plan_units():
    units, spans = [], {}

    def section(name, kind, src, col0, n, width=256, step=None, k0=0):
        spans[name] = range(len(units), len(units) + n)
        for i in range(n):
            units.append((kind, src, k0, col0 + i * (width if step is None else step), width))

    def ada(layer, sections):
        for s in sections:
            section(f"ada{layer}.{s}", "A", f"ada{layer}", s * D, 4)

    section("qa", "F", "w_in", O_QA, 2)
    section("ka", "F", "w_in", O_KA, 2)
    section("va", "T", "w_in", O_VA, 2)
    section("qb", "B", "w_in", O_QB, 2, step=128)
    section("kvb", "M", "w_in", O_KB, 1)
    section("qc", "F", "w_in", O_QC, 2)
    section("kc", "F", "w_in", O_KC, 2)
    section("vc", "T", "w_in", O_VC, 2)
    section("fc", "C", "w_in", O_FC, 1, width=128)
    section("ga", "F", "w_in", O_GA, 2)
    section("gb", "B", "w_in", O_GB, 2, step=128)
    section("gc", "F", "w_in", O_GC, 2)
    ada(0, range(6))
    section("gm", "F", "w_in", O_GM, 12)
    for i in range(4):
        for br in "abc":
            section(f"up_{br}{i}", "U" if br != "b" else "V", f"w_up_{br}", i * 256, 1)
    section("wo", "F", "w_o", 0, 4)
    for name, kind, off in (("cnk", "F", E_NK), ("cnv", "T", E_NV), ("chi", "T", E_HI),
                            ("chf", "F", E_HF), ("chb", "F", E_HB),
                            ("nq", "F", E_NQ), ("nk", "F", E_NK), ("nv", "T", E_NV),
                            ("hq", "F", E_HQ), ("hi", "T", E_HI), ("hf", "F", E_HF), ("hb", "F", E_HB),
                            ("hg", "F", E_HG)):
        section(name, kind, "ev_w_in", off, 2)
    ada(1, range(6))
    section("evo", "F", "ev_w_out", 0, 4)

    def ffn(layer):
        for i in range(FT // 2):
            section(f"fa{layer}.{i}", "F", f"ffn_up{layer}", i * 256, 1)
            section(f"fv{layer}.{i}", "F", f"ffn_up{layer}", FF + i * 256, 1)
        for i in range(FT // 2):
            section(f"fd{layer}.{i}", "D", f"ffn_down{layer}", 0, 1, width=D, k0=2 * i)

    ffn(0)
    for i in range(4):
        section(f"odc{i}", "F", "od_w_in", D + i * 256, 1)
        section(f"odu{i}", "F", "od_w_in", 2 * D + i * 256, 1)
        section(f"odb{i}", "F", "od_w_in", i * 256, 1)
    section("odo", "F", "od_w_out", 0, 4)
    ffn(1)
    return units, spans


def build(nc, x, norm_gain, w_in, b_forget, lambda_q1, lambda_k1, lambda_q2, lambda_k2, subln_gain, sinks,
          w_up_a, w_up_b, w_up_c, w_o, final_gain, c_2, ctx_2, c_ctx_2, ada_w_2, ada_b_2,
          norm_mix_w_2, norm_ffn_w_2, ev_w_in_2, ev_w_out_2, na_rpb_2, hg_lb_logits_2, hg_norm_w_2,
          od_w_in_2, od_conv_w_2, od_conv_b_2, od_w_out_2, ffn_w_up_2, ffn_conv_w_2, ffn_conv_b_2,
          ffn_w_down_2, final_norm_w_2, out, stop_at=None, probe=None):
    UNITS, SPAN = plan_units()
    NU = len(UNITS)
    SRC = {"w_in": w_in[0], "w_up_a": w_up_a[0], "w_up_b": w_up_b[0], "w_up_c": w_up_c[0], "w_o": w_o[0],
           "ada0": ada_w_2[0], "ada1": ada_w_2[1], "ev_w_in": ev_w_in_2[0], "ev_w_out": ev_w_out_2[0],
           "od_w_in": od_w_in_2[0], "od_w_out": od_w_out_2[0],
           "ffn_up0": ffn_w_up_2[0], "ffn_up1": ffn_w_up_2[1],
           "ffn_down0": ffn_w_down_2[0], "ffn_down1": ffn_w_down_2[1]}

    halves = {"A": 0, "C": 1, "U": 1, "V": 1}
    NH = [halves.get(k[0], 2) for k in UNITS]
    H0 = [sum(NH[:u]) for u in range(NU)]
    loads = {"B": 2, "V": 2}
    LD = [loads.get(k[0], 1) for k in UNITS]
    LANDED = [16 * sum(LD[v] for v in range(u % RAW, u + 1, RAW)) for u in range(NU)]
    NA_ = [int(k[0] == "A") for k in UNITS]
    A0 = [sum(NA_[:u]) for u in range(NU)]
    banked = [int(k[0] not in "AD") for k in UNITS]
    B0 = [sum(banked[:u]) for u in range(NU)]
    split_order = [u for u in range(NU) if NH[u]]
    after = {u: u + 1 for u in split_order[:-1] if NH[u + 1]}

    with ExitStack() as ctx:
        def sb(name, shape, dt=F32):
            return ctx.enter_context(nc.sbuf_tensor(name, shape, dt))

        def sem(name):
            return ctx.enter_context(nc.semaphore(name))

        raw = sb("raw", [P, RAW, 2 * HALF])
        whi = sb("whi", [P, WRING, HALF], F32R)
        wlo = sb("wlo", [P, WRING, HALF], F32R)
        xT = sb("xT", [P, KT, S])
        Hhi = sb("Hhi", [P, KT, S], F32R)
        Hlo = sb("Hlo", [P, KT, S], F32R)
        tok = sb("tok", [P, NT, D])
        rn = sb("rn", [P, 2, S])
        ident = sb("ident", [P, P])
        ones = sb("ones", [P, S])
        pcol = sb("pcol", [P, 4 * P])
        eps = sb("eps", [P, 2])
        mod = sb("mod", [P, 2, 48, 2])
        cm = sb("cm", [P, 5, KT])
        cs = sb("cs", [P, KT, 2])
        cse = sb("cse", [P, 2 * KT])
        stat = sb("stat", [P, 6, 4])
        vt = sb("vt", [P, 2, S])
        prow = vt[:, :, :].rearrange("p a (b c) -> p (a b) c", c=P)
        sctx = sb("sctx", [P, 2, 4, P])

        with ExitStack() as a1:
            def s1(name, shape, dt=F32):
                return a1.enter_context(nc.sbuf_tensor(name, shape, dt))
            dist = s1("dist", [P, 384])
            distw = s1("distw", [P, 384])
            cmask = s1("cmask", [P, 384])
            distI = s1("distI", [P, 384], I32)
            sel = s1("sel", [8, 8, P])
            sinkb = s1("sinkb", [P, 4, 2, 2])
            smallr = s1("smallr", [P, 16])
            lam4 = s1("lam4", [HD, 4])
            lamp = s1("lamp", [P, 8])
            negc = s1("negc", [8, S])
            bfc = s1("bfc", [8, 1])
            sg = s1("sg", [P, 12, S])
            Mhi = s1("Mhi", [P, 12, S], F32R)
            Mlo = s1("Mlo", [P, 12, S], F32R)
            e2 = s1("e2", [P, 2, S])
            with ExitStack() as a1a:
                def s2(name, shape, dt=F32):
                    return a1a.enter_context(nc.sbuf_tensor(name, shape, dt))
                qaT, kaT = s2("qaT", [P, 4, S]), s2("kaT", [P, 4, S])
                qbT, kbT = s2("qbT", [P, 4, S]), s2("kbT", [P, S])
                qcT, kcT = s2("qcT", [P, 4, S]), s2("kcT", [P, 4, S])
                va, vb, vc = s2("va", [P, NT, 512]), s2("vb", [P, NT, P]), s2("vc", [P, NT, 512])
                pr = s2("pr", [P, 2, 2, 384])
                pT = s2("pT", [P, 2, 2, 384])
                yA = s2("yA", [P, 4, S])
                fcw = yA[0:8, :, :]
            with ExitStack() as a1b:
                gate = a1b.enter_context(nc.sbuf_tensor("gate", [P, 24, S], F32))
                merged = a1b.enter_context(nc.sbuf_tensor("merged", [P, KT, S], F32))
                mt = a1b.enter_context(nc.sbuf_tensor("mt", [P, 2, S], F32))
        with ExitStack() as a2:
            def s3(name, shape, dt=F32):
                return a2.enter_context(nc.sbuf_tensor(name, shape, dt))
            naq, nak, cnk = s3("naq", [P, 4, S]), s3("nak", [P, 4, S]), s3("cnk", [P, 4, S])
            nav, cnv = s3("nav", [P, NT, 512]), s3("cnv", [P, NT, 512])
            Yhi, Ylo = s3("Yhi", [P, KT, S], F32R), s3("Ylo", [P, KT, S], F32R)
            lbc = s3("lbc", [P, 3, 8])
            with ExitStack() as a2a:
                def s4(name, shape, dt=F32):
                    return a2a.enter_context(nc.sbuf_tensor(name, shape, dt))
                hq, hv = s4("hq", [P, 4, S]), s4("hv", [P, NT, 512])
                kk = s4("kk", [P, 2, 4, S])
                lg = s4("lg", [P, 2, 4, S])
                bc = s4("bc", [P, 4, S])
                qe, ke, kd = s4("qe", [P, 4, S]), s4("ke", [P, 4, S]), s4("kd", [P, 4, S])
                kdt = s4("kdt", [P, 2, P])
                attm = s4("attm", [P, 2, P])
                vbd = s4("vbd", [P, NT, 4, P])
                sq = s4("sq", [P, NCH, P])
                oT = s4("oT", [P, 4, S])
                smask = s4("smask", [P, 2, P])
                reset = s4("reset", [P, S])
                hgt = s4("hgt", [P, 2, S])
                sgh = s4("sgh", [P, 4, S])
                dec = s4("dec", [P, 4 * NCH])
            with ExitStack() as a2b:
                def s5(name, shape, dt=F32):
                    return a2b.enter_context(nc.sbuf_tensor(name, shape, dt))
                rpad = s5("rpad", [120, P])
                rrev = s5("rrev", [120, P])
                nb = s5("nb", [P, 8, 6, HD])
                pn = s5("pn", [P, 2, NT, 512])
                pnT = s5("pnT", [P, 4, 512])
        with ExitStack() as a3:
            def s6(name, shape, dt=F32):
                return a3.enter_context(nc.sbuf_tensor(name, shape, dt))
            Ghi, Glo = s6("Ghi", [P, FT, S], F32R), s6("Glo", [P, FT, S], F32R)
            fa = s6("fa", [P, 2, 2, S])
            fz = s6("fz", [P, 2, 2, S])
        cxT = kk[:, :, :, :].rearrange("p d h s -> p (d h) s")
        sqv = tok[:, :, :].rearrange("p t (k s) -> p (t k) s", s=S)
        headr = tok[:, 1, :].rearrange("p (a b) -> p a b", a=2)
        rscr = nc.dram_tensor("rpb_rows", (120, P), F32, kind="Internal").ap()

        psG = ctx.enter_context(nc.psum_tensor("psG", [P, 2, 512], F32))
        psS = ctx.enter_context(nc.psum_tensor("psS", [P, 4, 512], F32))
        psX = ctx.enter_context(nc.psum_tensor("psX", [P, 512], F32))
        psY = ctx.enter_context(nc.psum_tensor("psY", [P, 512], F32))

        raw_landed = [sem(f"raw_landed{i}") for i in range(RAW)]
        hi_split, lo_split = sem("hi_split"), sem("lo_split")
        half_used, ada_used, ada_kept = sem("half_used"), sem("ada_used"), sem("ada_kept")
        bank_free = [sem("bank_free0"), sem("bank_free1")]
        acts, dves, pools = sem("act_step"), sem("dve_step"), sem("pool_step")
        tok_in, par_in, misc_in, scr_out, nb_in, out_done = [sem(n) for n in (
            "tok_in", "par_in", "misc_in", "scr_out", "nb_in", "out_done")]
        consts, ones_set = sem("consts"), sem("ones_set")
        turned, turned_kept = sem("turned"), sem("turned_kept")
        squares, sums, rms_inv, H_ready, norm_done = [sem(n) for n in (
            "squares", "sums", "rms_inv", "H_ready", "norm_done")]
        kept = sem("kept")
        silu_e = sem("silu_e")
        c_silu, c_exp = sem("c_silu"), sem("c_exp")
        small_mm, small_ev, small_ex = sem("small_mm"), sem("small_ev"), sem("small_ex")
        forget, forget_a = sem("forget"), sem("forget_a")
        scored, biased, exped, probs, turnedP, pT_kept, yed, y_kept = [sem(n) for n in (
            "scored", "biased", "exped", "probs", "turnedP", "pT_kept", "yed", "y_kept")]
        yA_kept = sem("yA_kept")
        sub_sq, sub_sum, sub_inv = sem("sub_sq"), sem("sub_sum"), sem("sub_inv")
        M_ready = sem("M_ready")
        gate_e = sem("gate_e")
        merge_ready = sem("merge_ready")
        x_ready = sem("x_ready")
        lb_e, lb_set = sem("lb_e"), sem("lb_set")
        f_e, f_set, f_ln, f_cum, f_exp, f_mul = [sem(n) for n in (
            "f_e", "f_set", "f_ln", "f_cum", "f_exp", "f_mul")]
        vbd_set, kd_turned, kd_kept, kv_done, att_done, att_set, st_set, o_done, o_kept = [sem(n) for n in (
            "vbd_set", "kd_turned", "kd_kept", "kv_done", "att_done", "att_set", "st_set", "o_done", "o_kept")]
        ctx_state, ctx_kept = sem("ctx_state"), sem("ctx_kept")
        nb_set, rpad_set = sem("nb_set"), sem("rpad_set")
        conv_a, gelu_in, gelu_out, G_ready, down_done = [sem(n) for n in (
            "conv_a", "gelu_in", "gelu_out", "G_ready", "down_done")]
        cu_set, c_kept = sem("cu_set"), sem("c_kept")
        out_turned, out_kept = sem("out_turned"), sem("out_kept")

        block = ctx.enter_context(nc.Block())

        def bank(u):
            return psG[:, B0[u] % 2, :]

        def y_bank(g):
            return psG[:, 1, 0:S] if g % 2 else psY[:, 0:S]

        def na_y_bank(j):
            return psG[:, 0, 0:S] if j % 2 else psY[:, 0:S]

        def na_x_bank(n):
            return psG[:, 1, :] if n % 2 else psX[:, :]

        def token_bank(n):
            return psX[:, :] if n % 2 else psY[:, :]

        adaP = psG[:, 0, 0:16]
        attP = psG[:, 1, 0:S]

        def half(ring, h):
            return ring[:, h % WRING, :]

        def raw_half(u, i):
            kind = UNITS[u][0]
            r = raw[:, u % RAW, :]
            if kind in "FM":
                return r.rearrange("p (k n) -> p k n", k=KT)[:, :, i * P:(i + 1) * P], KT
            if kind == "B":
                return r.rearrange("p (k i j r) -> p k i j r", k=KT, i=2, j=2)[:, :, :, i, :], KT
            if kind == "C":
                return r[:, 0:HALF], 1
            if kind in "UV":
                return r[:, 0:HALF], 1
            return r[:, i * HALF:(i + 1) * HALF], 1

        def ring_half(ring, u, i):
            kind = UNITS[u][0]
            a = half(ring, H0[u] + i)
            if kind in "FM":
                return a.rearrange("p (k n) -> p k n", k=KT)
            if kind == "B":
                return a.rearrange("p (k i r) -> p k i r", k=KT, i=2)
            return a

        GROUPS = [("A", h) for h in range(4)] + [("B", j) for j in range(4)] + [("C", j) for j in range(4)]
        NG = len(GROUPS)
        TSETS = [1 if b == "A" else 2 for b, _ in GROUPS]
        T0 = [sum(TSETS[:g]) for g in range(NG)]
        NT0 = T0[-1] + TSETS[-1]
        COLS = [(0, P), (P, 384)]
        ADA0 = [u for s in range(6) for u in SPAN[f"ada0.{s}"]]
        ADA1 = [u for s in range(6) for u in SPAN[f"ada1.{s}"]]
        KEPT = {"kc": 13, "vc": 15}
        col = lambda ap: ap.rearrange("a (k p) -> (a k) p", p=P)
        PAR_ROWS = [(col(norm_gain), C_NG, 8), (final_gain.rearrange("(k p) -> k p", p=P), C_FG, 8),
                    (col(norm_mix_w_2), C_MIX, 16), (col(norm_ffn_w_2), C_FFN, 16), (col(hg_norm_w_2), C_HGN, 4),
                    (hg_lb_logits_2.rearrange("n d (k p) -> (n d k) p", p=P), C_LB, 16), (col(c_2), C_C, 8),
                    (c_ctx_2.rearrange("(k p) -> k p", p=P), C_CC, 8),
                    (od_conv_w_2.rearrange("a t (k p) -> (a t k) p", p=P), C_ODW, 24), (col(od_conv_b_2), C_ODB, 8),
                    (final_norm_w_2.rearrange("(k p) -> k p", p=P), C_FN, 8), (subln_gain, C_SUB, 1),
                    (col(ada_b_2), C_ADAB, 96)]
        for l in range(2):
            PAR_ROWS += [(ffn_conv_w_2[l].rearrange("t (k p) -> (t k) p", p=P), C_FCW + P * l, 66),
                         (ffn_conv_b_2[l:l + 1, :].rearrange("t (k p) -> (t k) p", p=P), C_FCB + P * l, 22)]
        PARS, MISC = len(PAR_ROWS), 6
        F = {n: i for i, n in enumerate(["h1", "fin1", "ctx", "mix0", "ffn0", "mix1", "ffn1", "last"])}
        H_COUNT = {"h1": 1, "ctx": 2, "mix0": 3, "ffn0": 4, "mix1": 5, "ffn1": 6}

        @block.sync
        def _(sp):
            for u, (kind, src, k0, col0, width) in enumerate(UNITS):
                if stop_at is not None and u >= stop_at:
                    break
                slot = u % RAW
                if u >= RAW:
                    v = u - RAW
                    if NH[v]:
                        sp.wait_ge(lo_split, H0[v] + NH[v])
                    else:
                        sp.wait_ge(ada_used, A0[v] + 1)
                w = SRC[src]
                r = raw[:, slot, :]
                if kind == "B":
                    rv = r.rearrange("p (k i n) -> p k i n", k=KT, i=2)
                    for i in range(2):
                        c = col0 + i * 256
                        sp.dma_start(rv[:, :, i, :], w[:, c:c + P].rearrange("(k p) n -> p k n", p=P)
                                     ).then_inc(raw_landed[slot], 16)
                elif kind == "V":
                    for i in range(2):
                        sp.dma_start(r[i * HD:(i + 1) * HD, 0:HALF].rearrange("p (k n) -> p k n", k=4),
                                     w[i * 256:(i + 1) * 256, col0:col0 + width].rearrange("(k p) n -> p k n", p=HD)
                                     ).then_inc(raw_landed[slot], 16)
                elif kind == "D":
                    sp.dma_start(r.rearrange("p (k n) -> p k n", k=2),
                                 w[k0 * P:(k0 + 2) * P, :].rearrange("(k p) n -> p k n", p=P)
                                 ).then_inc(raw_landed[slot], 16)
                else:
                    kt = 4 if kind == "U" else KT
                    sp.dma_start(r[:, 0:kt * width].rearrange("p (k n) -> p k n", k=kt),
                                 w[:, col0:col0 + width].rearrange("(k p) n -> p k n", p=P)
                                 ).then_inc(raw_landed[slot], 16)
            ov = out.rearrange("b (t p) d -> p (b t) d", p=P)
            for t in range(NT):
                sp.wait_ge(out_kept, 2 * (t + 1))
                sp.dma_start(ov[:, t, :], tok[:, t, :]).then_inc(out_done, 16)
            sp.wait_ge(out_done, 16 * NT)

        @block.tensor
        def _(pe):
            mm = nc.tensor.matmul

            def product(o, a_hi, a_lo, b_hi, b_lo, first, last, shared=False):
                mm(o, a_hi, b_lo, start=first, stop=False, skip_group_check=shared)
                mm(o, a_lo, b_hi, start=False, stop=False, skip_group_check=shared)
                return mm(o, a_hi, b_hi, start=False, stop=last, skip_group_check=shared)

            def open_bank(u):
                n = B0[u] // 2
                if n:
                    pe.wait_ge(bank_free[B0[u] % 2], n)

            def project(u, ahi, alo, ready=None, base=0, scale_ready=1):
                kind = UNITS[u][0]
                open_bank(u)
                o = bank(u)
                h = H0[u]

                def pair(k):
                    if ready is not None and k % 2 == 0:
                        pe.wait_ge(ready[0], ready[1] + k // 2 + 1)
                if kind in "FBC":
                    for n in range(NH[u]):
                        pe.wait_ge(lo_split, h + n + 1)
                        wh = half(whi, h + n).rearrange("p (k n) -> p k n", k=KT)
                        wl = half(wlo, h + n).rearrange("p (k n) -> p k n", k=KT)
                        for k in range(KT):
                            if n == 0:
                                pair(k)
                            last = product(o[:, n * S:(n + 1) * S], wh[:, k, :], wl[:, k, :],
                                           ahi[:, base + k, :], alo[:, base + k, :], k == 0, k == KT - 1)
                        last.then_inc(half_used, 1)
                elif kind == "T":
                    for t in range(NT):
                        for k in range(KT):
                            if t == 0:
                                pair(k)
                            if t == 0 and k % 4 == 0:
                                pe.wait_ge(lo_split, h + k // 4 + 1)
                            q, n = k // 4, k % 4
                            last = product(o[:, t * 256:(t + 1) * 256],
                                           ahi[:, base + k, t * P:(t + 1) * P], alo[:, base + k, t * P:(t + 1) * P],
                                           half(whi, h + q)[:, n * 256:(n + 1) * 256],
                                           half(wlo, h + q)[:, n * 256:(n + 1) * 256], k == 0, k == KT - 1)
                            if t == NT - 1 and k % 4 == 3:
                                last.then_inc(half_used, 1)
                elif kind == "M":
                    for n in range(2):
                        pe.wait_ge(lo_split, h + n + 1)
                        wh = half(whi, h + n).rearrange("p (k n) -> p k n", k=KT)
                        wl = half(wlo, h + n).rearrange("p (k n) -> p k n", k=KT)
                        for t in range(1 if n == 0 else NT):
                            for k in range(KT):
                                if n == 0:
                                    last = product(o[:, 0:S], wh[:, k, :], wl[:, k, :], ahi[:, k, :], alo[:, k, :],
                                                   k == 0, k == KT - 1)
                                else:
                                    last = product(o[:, S + t * P:S + (t + 1) * P],
                                                   ahi[:, k, t * P:(t + 1) * P], alo[:, k, t * P:(t + 1) * P],
                                                   wh[:, k, :], wl[:, k, :], k == 0, k == KT - 1)
                        last.then_inc(half_used, 1)
                else:
                    pe.wait_ge(lo_split, h + 1)
                    wh = half(whi, h).rearrange("p (k n) -> p k n", k=4)
                    wl = half(wlo, h).rearrange("p (k n) -> p k n", k=4)
                    for n in range(2):
                        for k in range(4):
                            last = product(o[:, n * S:(n + 1) * S], wh[:, k, n * P:(n + 1) * P],
                                           wl[:, k, n * P:(n + 1) * P], ahi[:, base + k, :], alo[:, base + k, :],
                                           k == 0, k == 3)
                    last.then_inc(half_used, 1)

            def ada(u):
                pe.wait_ge(raw_landed[u % RAW], LANDED[u])
                a = A0[u]
                if a == 0:
                    pe.wait_ge(c_silu, 1)
                if a % 4 == 0 and a >= 4:
                    pe.wait_ge(ada_kept, a // 4)
                w = raw[:, u % RAW, :].rearrange("p (k n) -> p k n", k=KT)
                for n in range(2):
                    c = 2 * (2 * (a % 4) + n)
                    for k in range(KT):
                        last = mm(adaP[:, c:c + 2], w[:, k, n * P:(n + 1) * P], cs[:, k, :],
                                  start=(k == 0), stop=(k == KT - 1))
                last.then_inc(ada_used, 1)

            def sum_squares(i):
                for k in range(KT):
                    if k % 2 == 0:
                        pe.wait_ge(squares, 4 * i + k // 2 + 1)
                    last = mm(psY[:, 0:S], ones[:, 0:P], sqv[:, k, :], start=(k == 0), stop=(k == KT - 1))
                last.then_inc(sums, 1)


            def turn_tokens(i):
                pe.wait_ge(tok_in, 16 * NT * (i + 1))
                for k4 in range(4):
                    if k4 >= 2:
                        pe.wait_ge(turned_kept, 4 * i + k4 - 1)
                    for kk_ in range(2):
                        k = 2 * k4 + kk_
                        for t in range(NT):
                            last = nc.tensor.transpose(token_bank(k4)[:, kk_ * S + t * P:kk_ * S + (t + 1) * P],
                                                       tok[:, t, k * P:(k + 1) * P], ident[:, :])
                    last.then_inc(turned, 1)

            pe.wait_ge(consts, 1)
            pe.wait_ge(ones_set, 1)
            pe.wait_ge(par_in, 16 * PARS)
            for i, rows in enumerate((125, 96, 88, 88)):
                last = nc.tensor.transpose(psX[:, i * P:i * P + rows], prow[0:rows, i, :], ident[0:rows, 0:rows])
            last.then_inc(small_mm, 1)
            pe.wait_ge(misc_in, 16 * MISC)
            pe.wait_ge(small_ev, 2)
            mm(psX[:, 0:2], ones[0:HD, 0:P], lamp[0:HD, 0:2], start=True, stop=True)
            mm(psX[:, 8:16], ones[0:1, 0:P], smallr[0:1, 0:8], start=True, stop=True).then_inc(small_mm, 1)
            pe.wait_ge(small_ex, 1)
            turn_tokens(0)
            sum_squares(F["h1"])

            for name in ("qa", "ka", "va", "qb", "kvb", "qc", "kc", "vc", "fc", "ga", "gb", "gc"):
                for u in SPAN[name]:
                    project(u, Hhi, Hlo, ready=(H_ready, 0) if u == 0 else None)

            def scores(g):
                br, j = GROUPS[g]
                if g == 0:
                    pe.wait_ge(kept, KEPT["kc"])
                if g >= 2:
                    pe.wait_ge(exped, g - 1)
                if br == "C" and j == 0:
                    pe.wait_ge(forget, 1)
                for i in range(2):
                    q = (qaT, qbT, qcT)["ABC".index(br)][i * HD:(i + 1) * HD, j, :]
                    k = kaT[i * HD:(i + 1) * HD, j, :] if br == "A" else (
                        kbT[i * HD:(i + 1) * HD, :] if br == "B" else kcT[i * HD:(i + 1) * HD, j, :])
                    for t in range(NT):
                        o = psS[:, 2 * (g % 2) + i, COLS[t][0]:COLS[t][1]]
                        last = mm(o, q[:, t * P:(t + 1) * P], k[:, 0:(t + 1) * P], start=True, stop=(br != "C"))
                        if br == "C":
                            last = mm(o, sel[0:8, 2 * j + i, :], negc[0:8, 0:(t + 1) * P], start=False, stop=True)
                last.then_inc(scored, 1)

            def turn_probs(g, i):
                n = T0[g] + i
                pe.wait_ge(probs, g + 1)
                if n >= 1:
                    pe.wait_ge(pT_kept, n)
                for b in range(3):
                    last = nc.tensor.transpose(psX[:, b * P:(b + 1) * P], pr[:, g % 2, i, b * P:(b + 1) * P],
                                               ident[:, :])
                last.then_inc(turnedP, 1)

            def weigh(g):
                br, j = GROUPS[g]
                pe.wait_ge(pT_kept, T0[g] + TSETS[g])
                if g == 0:
                    pe.wait_ge(kept, KEPT["vc"])
                if 2 <= g < 6:
                    pe.wait_ge(yA_kept, g - 1)
                elif g >= 6:
                    pe.wait_ge(y_kept, g - 5)
                for i in range(TSETS[g]):
                    if br == "A":
                        rows, v = slice(0, P), va[:, :, j * P:(j + 1) * P]
                    elif br == "B":
                        rows, v = slice(i * HD, (i + 1) * HD), vb[:, :, i * HD:(i + 1) * HD]
                    else:
                        rows, v = slice(i * HD, (i + 1) * HD), vc[:, :, (2 * j + i) * HD:(2 * j + i + 1) * HD]
                    y = y_bank(g)
                    mm(y[rows, :], v[:, 0, :], pT[:, g % 2, i, 0:S], start=True, stop=False)
                    last = mm(y[rows, P:S], v[:, 1, :], pT[:, g % 2, i, S:384], start=False, stop=True)
                last.then_inc(yed, 1)

            for b in range(2):
                pe.wait_ge(bank_free[b], (B0[SPAN["gc"][1]] + 2 - b) // 2)
            for g in range(NG + 2):
                if g < NG:
                    scores(g)
                if 1 <= g <= NG:
                    turn_probs(g - 1, 0)
                for u in ADA0[2 * g:2 * g + 1]:
                    ada(u)
                if 1 <= g <= NG and TSETS[g - 1] == 2:
                    turn_probs(g - 1, 1)
                for u in ADA0[2 * g + 1:2 * g + 2]:
                    ada(u)
                if g >= 2:
                    weigh(g - 2)
            pe.wait_ge(sub_sq, 1)
            for i in range(2):
                last = mm(psS[:, i, :], ones[:, 0:P], sqv[:, 2 * i:2 * i + 2, :], start=True, stop=True)
            last.then_inc(sub_sum, 1)

            pe.wait_ge(ada_kept, 6)
            pe.wait_ge(y_kept, 8)
            for u in SPAN["gm"]:
                project(u, Hhi, Hlo)
            for i in range(4):
                for b, br in enumerate("abc"):
                    for u in SPAN[f"up_{br}{i}"]:
                        if i == 0:
                            pe.wait_ge(M_ready, (9, 4, 8)[b])
                        project(u, Mhi, Mlo, base=4 * b)
            for u in SPAN["wo"]:
                if u == SPAN["wo"][0]:
                    pe.wait_ge(merge_ready, 1)
                project(u, Hhi, Hlo)
            sum_squares(F["fin1"])

            pe.wait_ge(rms_inv, F["fin1"] + 1)
            turn_tokens(1)
            sum_squares(F["ctx"])
            for name in ("cnk", "cnv", "chi", "chf", "chb"):
                for u in SPAN[name]:
                    project(u, Hhi, Hlo, ready=(H_ready, 4) if u == SPAN["cnk"][0] else None)

            def turn_kd(n, j):
                if n >= 1:
                    pe.wait_ge(kd_kept, n)
                for t in range(NT):
                    last = nc.tensor.transpose(psX[:, t * P:(t + 1) * P],
                                               kd[:, j, t * P:(t + 1) * P], ident[:, :])
                last.then_inc(kd_turned, 1)

            for d in range(2):
                for j in range(4):
                    n = 4 * d + j
                    pe.wait_ge(f_mul, d + 1)
                    turn_kd(n, j)
                    pe.wait_ge(kd_kept, n + 1)
                    if n >= 1:
                        pe.wait_ge(ctx_kept, n)
                    for t in range(NT):
                        last = mm(psS[:, 0, 0:P], kdt[:, t, :], hv[:, t, j * P:(j + 1) * P],
                                  start=(t == 0), stop=(t == NT - 1))
                    last.then_inc(ctx_state, 1)

            sum_squares(F["mix0"])
            for name in ("nq", "nk", "nv", "hq", "hi", "hf", "hb", "hg"):
                for u in SPAN[name]:
                    project(u, Hhi, Hlo, ready=(H_ready, 8) if u == SPAN["nq"][0] else None)

            for b in range(2):
                pe.wait_ge(bank_free[b], (B0[SPAN["hg"][1]] + 2 - b) // 2)
            adas = iter(ADA1)
            for d in range(2):
                for j in range(4):
                    n = 4 * d + j
                    pe.wait_ge(f_mul, 3 + d)
                    turn_kd(8 + n, j)
                    if n:
                        pe.wait_ge(att_set, n)
                    for t in range(NT):
                        last = mm(attP[:, t * P:(t + 1) * P],
                                  ke[:, j, t * P:(t + 1) * P], qe[:, j, t * P:(t + 1) * P], start=True, stop=True)
                    last.then_inc(att_done, 1)
                    ada(next(adas))
                    pe.wait_ge(kd_kept, 8 + n + 1)
                    pe.wait_ge(vbd_set, n + 1)
                    if n >= 1:
                        pe.wait_ge(st_set, n)
                    for t in range(NT):
                        last = mm(psS[:, t, :], kdt[:, t, :], vbd[:, t, :, :], start=True, stop=True)
                    last.then_inc(kv_done, 1)
                    pe.wait_ge(att_set, n + 1)
                    if n >= 1:
                        pe.wait_ge(o_kept, n)
                    ada(next(adas))
                    pe.wait_ge(st_set, n + 1)
                    for t in range(NT):
                        mm(psY[:, t * P:(t + 1) * P], hv[:, t, j * P:(j + 1) * P], attm[:, t, :],
                           start=True, stop=False)
                        for c in range(4):
                            cc = 4 * t + c
                            last = mm(psY[:, cc * CH:(cc + 1) * CH], sq[:, cc, :], qe[:, j, cc * CH:(cc + 1) * CH],
                                      start=False, stop=(c == 3))
                    last.then_inc(o_done, 1)
            pe.wait_ge(sub_sq, 2)
            for i in range(2):
                last = mm(psS[:, 2 + i, :], ones[:, 0:P], sqv[:, 2 * i:2 * i + 2, :], start=True, stop=True)
            last.then_inc(sub_sum, 1)

            def na_scores(h):
                j, i = h // 2, h % 2
                if h >= 2:
                    pe.wait_ge(exped, NG + h - 1)
                elif h == 1:
                    pe.wait_ge(sub_inv, 2)
                for t in range(NT):
                    q = naq[i * HD:(i + 1) * HD, j, t * P:(t + 1) * P]
                    o = psS[:, 2 * (h % 2) + t, :]
                    mm(o[:, 0:S], q, nak[i * HD:(i + 1) * HD, j, :], start=True, stop=True)
                    last = mm(o[:, S:512], q, cnk[i * HD:(i + 1) * HD, j, :], start=True, stop=True)
                last.then_inc(scored, 1)



            def na_turn(h, t):
                n = 2 * h + t
                if n == 0:
                    pe.wait_ge(ada_kept, 10)
                pe.wait_ge(probs, NG + h + 1)
                if n >= 2:
                    pe.wait_ge(pT_kept, NT0 + n - 1)
                for b in range(4):
                    last = nc.tensor.transpose(na_x_bank(n)[:, b * P:(b + 1) * P], pn[:, h % 2, t, b * P:(b + 1) * P],
                                               ident[:, :])
                last.then_inc(turnedP, 1)

            def na_weigh(h):
                j, i = h // 2, h % 2
                pe.wait_ge(pT_kept, NT0 + 2 * h + 2)
                if h % 2 == 0 and j >= 2:
                    pe.wait_ge(y_kept, 8 + j - 1)
                for t in range(NT):
                    for b in range(4):
                        v = (nav if b < 2 else cnv)[:, b % 2, h * HD:(h + 1) * HD]
                        last = mm(na_y_bank(j)[i * HD:(i + 1) * HD, t * P:(t + 1) * P], v, pnT[:, (2 * h + t) % 4, b * P:(b + 1) * P],
                                  start=(b == 0), stop=(b == 3))
                last.then_inc(yed, 1)

            for h in range(8 + 2):
                if h < 8:
                    na_scores(h)
                if 1 <= h <= 8:
                    na_turn(h - 1, 0)
                    na_turn(h - 1, 1)
                if h >= 2:
                    na_weigh(h - 2)
            pe.wait_ge(M_ready, 14)
            for u in ADA1[16:]:
                ada(u)
            pe.wait_ge(ada_kept, 12)
            for u in SPAN["evo"]:
                project(u, Yhi, Ylo)

            def feed_forward(layer):
                sum_squares(F[f"ffn{layer}"])
                for i in range(FT // 2):
                    for part in ("fa", "fv"):
                        u = SPAN[f"{part}{layer}.{i}"][0]
                        project(u, Hhi, Hlo, ready=(H_ready, 12 + 8 * layer) if part == "fa" and i == 0 else None)
                for i in range(FT // 2):
                    u = SPAN[f"fd{layer}.{i}"][0]
                    pe.wait_ge(G_ready, (FT // 2 + 4) * layer + i + 1)
                    for q in range(2):
                        k = 2 * i + q
                        h = H0[u] + q
                        pe.wait_ge(lo_split, h + 1)
                        for n in range(KT):
                            last = product(psS[:, n // 2, (n % 2) * S:(n % 2 + 1) * S],
                                           half(whi, h)[:, n * P:(n + 1) * P], half(wlo, h)[:, n * P:(n + 1) * P],
                                           Ghi[:, k, :], Glo[:, k, :], k == 0 and n % 2 == 0, k == FT - 1, shared=True)
                        last.then_inc(half_used, 1)

            feed_forward(0)
            sum_squares(F["mix1"])
            for i in range(4):
                for part in "cub":
                    u = SPAN[f"od{part}{i}"][0]
                    project(u, Hhi, Hlo, ready=(H_ready, 16) if part == "c" and i == 0 else None)
            pe.wait_ge(G_ready, FT // 2 + 4)
            for u in SPAN["odo"]:
                project(u, Ghi, Glo)
            feed_forward(1)
            sum_squares(F["last"])

            pe.wait_ge(norm_done, 2)
            for t in range(NT):
                for k4 in range(2):
                    n = 2 * t + k4
                    if n >= 2:
                        pe.wait_ge(out_kept, n - 1)
                    for q in range(4):
                        k = 4 * k4 + q
                        last = nc.tensor.transpose(token_bank(n)[:, q * P:(q + 1) * P], xT[:, k, t * P:(t + 1) * P], ident[:, :])
                    last.then_inc(out_turned, 1)

        @block.scalar
        def _(act):
            steps = [0]
            half_at = [0]

            def step(ins):
                steps[0] += 1
                ins.then_inc(acts, 1)
                act.wait_ge(acts, steps[0])

            def split_through(u):
                while half_at[0] < H0[u] + NH[u]:
                    h = half_at[0]
                    v = next(w for w in split_order if H0[w] <= h < H0[w] + NH[w])
                    i = h - H0[v]
                    if i == 0:
                        act.wait_ge(raw_landed[v % RAW], LANDED[v])
                    if h >= WRING:
                        act.wait_ge(half_used, h - WRING + 1)
                    src, _ = raw_half(v, i)
                    nc.scalar.copy(ring_half(whi, v, i), src).then_inc(hi_split, 1)
                    half_at[0] += 1

            def ahead(u):
                if u in after:
                    split_through(after[u])

            def keep(u, dst, scale=None, free=True):
                act.wait_ge(half_used, H0[u] + NH[u])
                src = bank(u)
                nc.scalar.activation(dst, src.rearrange("p (a b) -> p a b", a=2), ACT.Copy,
                                     scale=1.0 if scale is None else scale).then_inc(bank_free[B0[u] % 2], 1)
                act.wait_ge(bank_free[B0[u] % 2], B0[u] // 2 + 1)
                act.sem_inc(kept, 1)

            nc.scalar.preload_act_table_set(TABLES)
            ctxv = ctx_2.rearrange("b (t p) d -> p (b t) d", p=P)
            xv = x.rearrange("b (t p) d -> p (b t) d", p=P)
            for t in range(NT):
                act.dma_start(tok[:, t, :], xv[:, t, :]).then_inc(tok_in, 16)
            act.wait_ge(small_mm, 2)
            step(nc.scalar.activation(lamp[:, 2:4], psX[:, 0:2], ACT.Exp))
            nc.scalar.copy(smallr[:, 8:16], psX[:, 8:16]).then_inc(small_ex, 1)

            act.wait_ge(c_exp, 1)
            nc.scalar.activation(cse[:, :], pcol[:, C_C:C_C + 16], ACT.Exp, scale=-1.0).then_inc(c_exp, 1)
            def turn_keep(i, g, dst):
                act.wait_ge(turned, 4 * i + g + 1)
                nc.scalar.copy(dst, token_bank(g).rearrange("p (a b) -> p a b", a=2)).then_inc(turned_kept, 1)
                act.wait_ge(turned_kept, 4 * i + g + 1)

            def norm(i, src, e):
                for g in range(4):
                    nc.scalar.activation(sqv[:, 2 * g:2 * g + 2, :], src[:, 2 * g:2 * g + 2, :], ACT.Square
                                         ).then_inc(squares, 1)
                inverse(i)

            def inverse(i):
                act.wait_ge(sums, i + 1)
                step(nc.scalar.activation(rn[:, 0, :], psY[:, 0:S], ACT.Ln, bias=eps[:, 0:1], scale=1.0 / D))
                nc.scalar.activation(rn[:, 1, :], rn[:, 0, :], ACT.Exp, scale=-0.5).then_inc(rms_inv, 1)
                act.wait_ge(rms_inv, i + 1)

            act.wait_ge(ones_set, 1)
            split_through(0)
            for g in range(4):
                turn_keep(0, g, xT[:, 2 * g:2 * g + 2, :])
            norm(F["h1"], xT, None)

            for name, dst, sc in (("qa", qaT, SCALE), ("ka", kaT, None)):
                for n, u in enumerate(SPAN[name]):
                    ahead(u)
                    keep(u, dst[:, 2 * n:2 * n + 2, :], sc)

            def keep_values(name, dst):
                for n, u in enumerate(SPAN[name]):
                    ahead(u)
                    keep(u, dst[:, :, n * 256:(n + 1) * 256])

            keep_values("va", va)
            for n, u in enumerate(SPAN["qb"]):
                ahead(u)
                keep(u, qbT[:, 2 * n:2 * n + 2, :], SCALE)
            u = SPAN["kvb"][0]
            ahead(u)
            act.wait_ge(half_used, H0[u] + NH[u])
            step(nc.scalar.copy(kbT[:, :], bank(u)[:, 0:S]))
            nc.scalar.copy(vb[:, :, :], bank(u)[:, S:512].rearrange("p (a b) -> p a b", a=2)
                           ).then_inc(bank_free[B0[u] % 2], 1)
            act.wait_ge(bank_free[B0[u] % 2], B0[u] // 2 + 1)
            act.sem_inc(kept, 1)
            for name, dst, sc in (("qc", qcT, SCALE), ("kc", kcT, None)):
                for n, u in enumerate(SPAN[name]):
                    ahead(u)
                    keep(u, dst[:, 2 * n:2 * n + 2, :], sc)
            keep_values("vc", vc)
            u = SPAN["fc"][0]
            ahead(u)
            act.wait_ge(forget_a, 1)
            step(nc.scalar.activation(fcw[:, 2, :], fcw[:, 1, :], ACT.Exp, scale=-1.0))
            nc.scalar.activation(fcw[:, 3, :], fcw[:, 2, :], ACT.Ln, bias=ones[0:8, 0:1]).then_inc(forget_a, 1)

            def silu_exp(u, n):
                ahead(u)
                act.wait_ge(half_used, H0[u] + NH[u])
                if n >= 1:
                    act.wait_ge(bank_free[(B0[u] - 1) % 2], (B0[u] - 1) // 2 + 1)
                nc.scalar.activation(e2[:, :, :], bank(u).rearrange("p (a b) -> p a b", a=2), ACT.Exp, scale=-1.0
                                     ).then_inc(silu_e, 1)

            n = 0
            for name in ("ga", "gb", "gc"):
                for u in SPAN[name]:
                    silu_exp(u, n)
                    n += 1

            def exps(g, tiles, rows):
                act.wait_ge(biased, g + 1)
                for n, (dst, src) in enumerate(tiles):
                    ins = nc.scalar.activation(dst, src, ACT.Exp, bias=stat[:, 0 + 3 * (g % 2), n:n + 1],
                                               accum_out=stat[:, 1 + 3 * (g % 2), n:n + 1])
                    if n < len(tiles) - 1 or rows:
                        step(ins)
                if rows:
                    ins = nc.scalar.activation(stat[:, 2 + 3 * (g % 2), 0:4], stat[:, 2 + 3 * (g % 2), 0:4], ACT.Exp)
                ins.then_inc(exped, 1)
                act.wait_ge(exped, g + 1)

            for g in range(NG + 2):
                if g < NG:
                    if g >= 2:
                        act.wait_ge(turnedP, T0[g - 2] + TSETS[g - 2])
                    exps(g, [(pr[:, g % 2, i, COLS[t][0]:COLS[t][1]],
                              psS[:, 2 * (g % 2) + i, COLS[t][0]:COLS[t][1]]) for i in range(2) for t in range(2)],
                         GROUPS[g][0] == "B")
                if 1 <= g <= NG:
                    for i in range(TSETS[g - 1]):
                        n = T0[g - 1] + i
                        act.wait_ge(turnedP, n + 1)
                        if g >= 3 and i == 0:
                            act.wait_ge(yed, g - 2)
                        nc.scalar.copy(pT[:, (g - 1) % 2, i, :], psX[:, 0:384]).then_inc(pT_kept, 1)
                        act.wait_ge(pT_kept, n + 1)
                if 2 <= g < 6:
                    act.wait_ge(yed, g - 1)
                    nc.scalar.copy(yA[:, g - 2, :], y_bank(g - 2)).then_inc(yA_kept, 1)
                    act.wait_ge(yA_kept, g - 1)
            nc.scalar.activation(sqv[:, 0:4, :], yA[:, :, :], ACT.Square).then_inc(sub_sq, 1)
            act.wait_ge(sub_sum, 1)
            step(nc.scalar.activation(headr[:, :, :], psS[:, 0:2, :], ACT.Ln, bias=eps[:, 1:2], scale=1.0 / P))
            nc.scalar.activation(headr[:, :, :], headr[:, :, :], ACT.Exp, scale=-0.5).then_inc(sub_inv, 1)
            act.wait_ge(sub_inv, 1)

            split_through(SPAN["gm"][0])
            for n, u in enumerate(SPAN["gm"]):
                ahead(u)
                if n == 0:
                    act.wait_ge(M_ready, 9)
                act.wait_ge(half_used, H0[u] + NH[u])
                nc.scalar.activation(gate[:, 2 * n:2 * n + 2, :], bank(u).rearrange("p (a b) -> p a b", a=2), ACT.Exp,
                                     scale=-1.0).then_inc(bank_free[B0[u] % 2], 1)
                act.wait_ge(bank_free[B0[u] % 2], B0[u] // 2 + 1)
                act.sem_inc(gate_e, 1)
            for i in range(4):
                for br in "abc":
                    ahead(SPAN[f"up_{br}{i}"][0])
            for n, u in enumerate(SPAN["wo"]):
                ahead(u)
            for g in range(4):
                act.wait_ge(x_ready, g + 1)
                nc.scalar.activation(sqv[:, 2 * g:2 * g + 2, :], xT[:, 2 * g:2 * g + 2, :], ACT.Square
                                     ).then_inc(squares, 1)
            inverse(F["fin1"])
            for t in range(NT):
                act.dma_start(tok[:, t, :], ctxv[:, t, :]).then_inc(tok_in, 16)
            for g in range(4):
                turn_keep(1, g, cxT[:, 2 * g:2 * g + 2, :])
            act.wait_ge(norm_done, 1)
            norm(F["ctx"], cxT, None)
            for n, u in enumerate(SPAN["cnk"]):
                ahead(u)
                keep(u, cnk[:, 2 * n:2 * n + 2, :])
            keep_values("cnv", cnv)
            keep_values("chi", hv)

            act.wait_ge(lb_e, 1)
            nc.scalar.activation(lbc[:, 0, :], lbc[:, 0, :], ACT.Exp).then_inc(lb_e, 1)

            def gates_exp(name, n0):
                for n, u in enumerate(SPAN[name]):
                    ahead(u)
                    act.wait_ge(half_used, H0[u] + NH[u])
                    if n0 + n >= 1:
                        act.wait_ge(f_set, n0 + n)
                    nc.scalar.activation(hgt[:, :, :], bank(u).rearrange("p (a b) -> p a b", a=2), ACT.Exp,
                                         scale=-1.0).then_inc(bank_free[B0[u] % 2], 1)
                    act.wait_ge(bank_free[B0[u] % 2], B0[u] // 2 + 1)
                    act.sem_inc(f_e, 1)

            gates_exp("chf", 0)
            gates_exp("chb", 2)
            act.wait_ge(f_set, 4)
            step(nc.scalar.activation(lg[:, :, :, :], lg[:, :, :, :], ACT.Ln))
            act.sem_inc(f_ln, 1)
            for d in range(2):
                act.wait_ge(f_cum, d + 1)
                for j in range(4):
                    tot = bc[:, j, S - 1:S] if d == 0 else bc[:, j, 0:1]
                    step(nc.scalar.activation(kd[:, j, :], bc[:, j, :], ACT.Exp, bias=tot, scale=-1.0))
                act.sem_inc(f_exp, 1)
                for j in range(4):
                    n = 4 * d + j
                    act.wait_ge(kd_turned, n + 1)
                    if n >= 1:
                        act.wait_ge(ctx_state, n)
                    nc.scalar.copy(kdt[:, :, :], psX[:, 0:S].rearrange("p (a b) -> p a b", a=2)).then_inc(kd_kept, 1)
                    act.wait_ge(kd_kept, n + 1)
                    act.wait_ge(ctx_state, n + 1)
                    nc.scalar.copy(sctx[:, d, j, :], psS[:, 0, 0:P]).then_inc(ctx_kept, 1)
                    act.wait_ge(ctx_kept, n + 1)

            act.wait_ge(norm_done, 1)
            norm(F["mix0"], xT, None)
            for name, dst, sc in (("nq", naq, SCALE), ("nk", nak, None)):
                for n, u in enumerate(SPAN[name]):
                    ahead(u)
                    keep(u, dst[:, 2 * n:2 * n + 2, :], sc)
            keep_values("nv", nav)
            for n, u in enumerate(SPAN["hq"]):
                ahead(u)
                act.wait_ge(half_used, H0[u] + NH[u])
                if n >= 1:
                    act.wait_ge(bank_free[(B0[u] - 1) % 2], (B0[u] - 1) // 2 + 1)
                nc.scalar.activation(hgt[:, :, :], bank(u).rearrange("p (a b) -> p a b", a=2), ACT.Exp, scale=-1.0
                                     ).then_inc(silu_e, 1)
            keep_values("hi", hv)
            act.wait_ge(bank_free[(B0[SPAN["hq"][1]]) % 2], (B0[SPAN["hq"][1]]) // 2 + 1)
            gates_exp("hf", 4)
            gates_exp("hb", 6)
            act.wait_ge(f_set, 8)
            step(nc.scalar.activation(lg[:, :, :, :], lg[:, :, :, :], ACT.Ln))
            act.sem_inc(f_ln, 1)
            for n, u in enumerate(SPAN["hg"]):
                ahead(u)
                act.wait_ge(half_used, H0[u] + NH[u])
                if n >= 1:
                    act.wait_ge(bank_free[(B0[u] - 1) % 2], (B0[u] - 1) // 2 + 1)
                nc.scalar.activation(hgt[:, :, :], bank(u).rearrange("p (a b) -> p a b", a=2), ACT.Exp, scale=-1.0
                                     ).then_inc(silu_e, 1)
            for d in range(2):
                act.wait_ge(f_cum, 3 + d)
                step(nc.scalar.activation(qe[:, :, :], bc[:, :, :], ACT.Exp))
                step(nc.scalar.activation(ke[:, :, :], bc[:, :, :], ACT.Exp, scale=-1.0))
                step(nc.scalar.activation(kd[:, :, :], kd[:, :, :], ACT.Exp))
                act.sem_inc(f_exp, 1)
                for j in range(4):
                    n = 4 * d + j
                    act.wait_ge(kd_turned, 8 + n + 1)
                    if n >= 1:
                        act.wait_ge(kv_done, n)
                    nc.scalar.copy(kdt[:, :, :], psX[:, 0:S].rearrange("p (a b) -> p a b", a=2)).then_inc(kd_kept, 1)
                    act.wait_ge(kd_kept, 8 + n + 1)
            act.wait_ge(o_kept, 8)
            nc.scalar.activation(sqv[:, 0:4, :], oT[:, :, :], ACT.Square).then_inc(sub_sq, 1)
            act.wait_ge(sub_sum, 2)
            step(nc.scalar.activation(headr[:, :, :], psS[:, 2:4, :], ACT.Ln, bias=eps[:, 0:1], scale=1.0 / P))
            nc.scalar.activation(headr[:, :, :], headr[:, :, :], ACT.Exp, scale=-0.5).then_inc(sub_inv, 1)
            act.wait_ge(sub_inv, 2)

            for h in range(8 + 2):
                if h < 8:
                    if h >= 2:
                        act.wait_ge(turnedP, NT0 + 2 * (h - 2) + 2)
                    else:
                        act.wait_ge(nb_set, 1)
                    exps(NG + h, [(pn[:, h % 2, t, :], psS[:, 2 * (h % 2) + t, :]) for t in range(NT)], False)
                if 1 <= h <= 8:
                    for t in range(2):
                        n = 2 * (h - 1) + t
                        act.wait_ge(turnedP, NT0 + n + 1)
                        if h >= 3 and t == 0:
                            act.wait_ge(yed, NG + h - 2)
                        nc.scalar.copy(pnT[:, n % 4, :], na_x_bank(n)).then_inc(pT_kept, 1)
                        act.wait_ge(pT_kept, NT0 + n + 1)

            split_through(SPAN["evo"][0])
            for u in SPAN["evo"]:
                ahead(u)

            def squares_of_x(i):
                for g in range(4):
                    act.wait_ge(x_ready, XR[i] + g + 1)
                    nc.scalar.activation(sqv[:, 2 * g:2 * g + 2, :], xT[:, 2 * g:2 * g + 2, :], ACT.Square
                                         ).then_inc(squares, 1)
                inverse(F[i])

            XR = {"ffn0": 4, "mix1": 8, "ffn1": 12, "last": 16}

            def conv_centre(src, n, w, b, z):
                for q in range(2):
                    ins = nc.scalar.activation(z[:, q, :], src[:, q, :], ACT.Identity, scale=pcol[:, w + q:w + q + 1],
                                               bias=pcol[:, b + q:b + q + 1])
                    if q == 0:
                        step(ins)
                ins.then_inc(conv_a, 1)
                act.wait_ge(conv_a, n + 1)

            def feed_forward(layer):
                squares_of_x(f"ffn{layer}")
                n0 = (FT // 2 + 4) * layer
                for i in range(FT // 2):
                    ua, uv = SPAN[f"fa{layer}.{i}"][0], SPAN[f"fv{layer}.{i}"][0]
                    ahead(ua)
                    act.wait_ge(half_used, H0[ua] + NH[ua])
                    if i >= 2:
                        act.wait_ge(G_ready, n0 + i - 1)
                    src = bank(ua).rearrange("p (a b) -> p a b", a=2)
                    nc.scalar.copy(fa[:, i % 2, :, :], src).then_inc(bank_free[B0[ua] % 2], 1)
                    act.wait_ge(bank_free[B0[ua] % 2], B0[ua] // 2 + 1)
                    conv_centre(fa[:, i % 2, :, :], n0 + i, C_FCW + P * layer + FT + 2 * i,
                                C_FCB + P * layer + 2 * i, fz[:, i % 2, :, :])
                    ahead(uv)
                    act.wait_ge(gelu_in, FT // 2 * layer + i + 1)
                    nc.scalar.activation(fz[:, i % 2, :, :], fz[:, i % 2, :, :], ACT.Gelu).then_inc(gelu_out, 1)
                    act.wait_ge(gelu_out, FT // 2 * layer + i + 1)
                for i in range(FT // 2):
                    ahead(SPAN[f"fd{layer}.{i}"][0])

            feed_forward(0)
            nc.scalar.preload_act_table_set(TABLES)
            squares_of_x("mix1")
            for i in range(4):
                uc, uu, ub = [SPAN[f"od{q}{i}"][0] for q in "cub"]
                n = FT // 2 + i
                ahead(uc)
                act.wait_ge(half_used, H0[uc] + NH[uc])
                if i >= 2:
                    act.wait_ge(G_ready, n - 1)
                nc.scalar.copy(fa[:, i % 2, :, :], bank(uc).rearrange("p (a b) -> p a b", a=2)
                               ).then_inc(bank_free[B0[uc] % 2], 1)
                act.wait_ge(bank_free[B0[uc] % 2], B0[uc] // 2 + 1)
                act.sem_inc(c_kept, 1)
                ahead(uu)
                act.wait_ge(cu_set, i + 1)
                conv_centre(fa[:, i % 2, :, :], n, C_ODW + 8 + 2 * i, C_ODB + 2 * i, fz[:, i % 2, :, :])
                ahead(ub)
            for u in SPAN["odo"]:
                ahead(u)
            feed_forward(1)
            nc.scalar.preload_act_table_set(TABLES)
            squares_of_x("last")

            for t in range(NT):
                for k4 in range(2):
                    n = 2 * t + k4
                    act.wait_ge(out_turned, n + 1)
                    nc.scalar.copy(tok[:, t, k4 * 512:(k4 + 1) * 512], token_bank(n)).then_inc(out_kept, 1)
                    act.wait_ge(out_kept, n + 1)

        @block.vector
        def _(dve):
            steps = [0]
            half_at = [0]
            V = nc.vector

            def step(ins):
                steps[0] += 1
                ins.then_inc(dves, 1)
                dve.wait_ge(dves, steps[0])

            def then(ins, s, n):
                ins.then_inc(s, 1)
                dve.wait_ge(s, n)

            def split_through(u):
                while half_at[0] < H0[u] + NH[u]:
                    h = half_at[0]
                    v = next(w for w in split_order if H0[w] <= h < H0[w] + NH[w])
                    dve.wait_ge(hi_split, h + 1)
                    src, _ = raw_half(v, h - H0[v])
                    V.tensor_tensor(ring_half(wlo, v, h - H0[v]), src, ring_half(whi, v, h - H0[v]).bitcast(F32),
                                    ALU.subtract).then_inc(lo_split, 1)
                    half_at[0] += 1

            def ahead(u):
                if u in after:
                    split_through(after[u])

            def split_value(v, hi, lo, s, n):
                step(V.tensor_copy(hi, v))
                then(V.tensor_tensor(lo, v, hi.bitcast(F32), ALU.subtract), s, n)

            then(V.memset(ones[:, :], 1.0), ones_set, 1)
            step(V.memset(eps[:, 0:1], EPS))
            step(V.memset(eps[:, 1:2], SUBLN_EPS))
            dve.wait_ge(small_mm, 1)
            for i, rows in enumerate((125, 96, 88, 88)):
                step(V.tensor_copy(pcol[:, i * P:i * P + rows], psX[:, i * P:i * P + rows]))
            dve.sem_inc(small_ev, 1)
            dve.sem_inc(c_exp, 1)
            dve.wait_ge(misc_in, 16 * MISC)
            then(V.tensor_tensor(lamp[0:HD, 0:2], lam4[:, 0:4:2], lam4[:, 1:4:2], ALU.mult), small_ev, 2)
            dve.wait_ge(small_ex, 1)
            step(V.tensor_tensor(lamp[:, 4:5], lamp[:, 3:4], lamp[:, 2:3], ALU.subtract))
            step(V.tensor_scalar(lamp[:, 5:6], lamp[:, 4:5], -LAM_INIT, None, ALU.add))
            step(V.tensor_scalar(lamp[:, 6:7], pcol[:, C_SUB:C_SUB + 1], 1.0 - LAM_INIT, None, ALU.mult))
            for t in range(2):
                step(V.tensor_copy(sinkb[:, :, :, t], smallr[:, 8:16].rearrange("p (i j) -> p j i", i=2)))
            dve.wait_ge(c_exp, 2)
            step(V.tensor_scalar(cse[:, :], cse[:, :], 1.0, None, ALU.add))
            step(V.reciprocal(cse[:, :], cse[:, :]))
            for i in range(2):
                step(V.tensor_tensor(cs[:, :, i], cse[:, 8 * i:8 * i + 8], pcol[:, C_C + 8 * i:C_C + 8 * i + 8],
                                     ALU.mult))
            dve.sem_inc(c_silu, 1)
            dve.wait_ge(consts, 1)
            step(V.tensor_copy(dist[:, :], distI[:, :]))
            step(V.tensor_copy(distw[:, :], distI[:, :]))
            step(V.memset(cmask[:, :], 0.0))
            dve.sem_inc(consts, 1)
            split_through(0)


            def normed(i, src, g0, shift=None):
                dve.wait_ge(rms_inv, F[i] + 1)
                for g in range(4):
                    for q in range(2):
                        k = 2 * g + q
                        step(V.tensor_tensor(vt[:, q, :], src[:, k, :], rn[:, 1, :], ALU.mult))
                        if shift is None:
                            step(V.tensor_scalar(vt[:, q, :], vt[:, q, :], g0[:, k:k + 1], None, ALU.mult))
                        else:
                            step(V.tensor_scalar(vt[:, q, :], vt[:, q, :], g0[:, k:k + 1], shift[:, k:k + 1],
                                                 ALU.mult, ALU.add))
                    split_value(vt[:, :, :], Hhi[:, 2 * g:2 * g + 2, :], Hlo[:, 2 * g:2 * g + 2, :],
                                H_ready, 4 * (H_COUNT[i] - 1) + g + 1)

            normed("h1", xT, pcol[:, C_NG:C_NG + 8])
            for name in ("qa", "ka", "va", "qb", "kvb", "qc", "kc", "vc"):
                for u in SPAN[name]:
                    ahead(u)
            u = SPAN["fc"][0]
            ahead(u)
            dve.wait_ge(half_used, H0[u] + NH[u])
            then(V.tensor_scalar(fcw[:, 0, :], bank(u)[0:8, 0:S], bfc[:, 0:1], None, ALU.add),
                 bank_free[B0[u] % 2], B0[u] // 2 + 1)
            then(V.scalar_tensor_tensor(fcw[:, 1, :], fcw[:, 0, :], -1.0, fcw[:, 0, :], ALU.mult, ALU.max),
                 forget_a, 1)
            step(V.tensor_scalar(fcw[:, 0, :], fcw[:, 0, :], 0.0, None, ALU.min))
            dve.wait_ge(forget_a, 2)
            step(V.tensor_tensor(fcw[:, 3, :], fcw[:, 3, :], fcw[:, 0, :], ALU.subtract))
            then(V.tensor_tensor_scan(negc[:, :], ones[0:8, 0:S], fcw[:, 3, :], 0.0, ALU.mult, ALU.add), forget, 1)
            

            def silu(u, n, dst, tmp):
                ahead(u)
                dve.wait_ge(silu_e, n + 1)
                step(V.tensor_scalar(tmp, tmp, 1.0, None, ALU.add))
                step(V.reciprocal(tmp, tmp))
                then(V.tensor_tensor(dst, tmp, bank(u).rearrange("p (a b) -> p a b", a=2), ALU.mult),
                     bank_free[B0[u] % 2], B0[u] // 2 + 1)

            n = 0
            for name in ("ga", "gb", "gc"):
                for u in SPAN[name]:
                    silu(u, n, sg[:, 2 * n:2 * n + 2, :], e2[:, :, :])
                    n += 1

            SLOPE_A = [2.0 ** (-8.0 * (h + 1) / 4) for h in range(4)]
            SLOPE_B = [2.0 ** (-8.0 * (h + 1) / 8) for h in range(8)]
            ada_at = [0]

            def keep_ada(limit):
                while ada_at[0] < limit:
                    a = ada_at[0]
                    layer, s = a // 6, a % 6
                    dve.wait_ge(ada_used, 4 * (a + 1))
                    b = pcol[:, C_ADAB + 48 * layer + 8 * s:C_ADAB + 48 * layer + 8 * s + 8]
                    step(V.tensor_copy(vt[:, 0, 0:16], adaP))
                    for i in range(2):
                        ins = V.tensor_tensor(mod[:, layer, 8 * s:8 * s + 8, i],
                                              vt[:, 0, i:16:2], b, ALU.add)
                        if i == 0:
                            step(ins)
                    then(ins, ada_kept, a + 1)
                    ada_at[0] += 1

            def bias_max(g):
                br, j = GROUPS[g]
                st = 3 * (g % 2)
                dve.wait_ge(scored, g + 1)
                if g == 4:
                    dve.wait_ge(consts, 3)
                if g == 0:
                    dve.wait_ge(consts, 3)
                for i in range(2):
                    o = psS[:, 2 * (g % 2) + i, 0:384]
                    if br == "A":
                        step(V.scalar_tensor_tensor(o, dist[:, :], -SLOPE_A[j], o, ALU.mult, ALU.add))
                    elif br == "B":
                        step(V.scalar_tensor_tensor(o, distw[:, :], -SLOPE_B[j + 4 * i], o, ALU.mult, ALU.add))
                    else:
                        step(V.tensor_tensor(o, o, cmask[:, :], ALU.add))
                for t in range(2):
                    ins = V.tensor_reduce(stat[:, st, t:4:2], psS[:, 2 * (g % 2):2 * (g % 2) + 2, COLS[t][0]:COLS[t][1]],
                                          AX.X, ALU.max, negate=(br != "B"))
                    if t == 0 or br == "B":
                        step(ins)
                if br == "B":
                    sk = sinkb[:, j, :, :].rearrange("p i t -> p (i t)")
                    step(V.tensor_tensor(stat[:, st, :], stat[:, st, :], sk, ALU.max))
                    step(V.tensor_scalar(stat[:, st, :], stat[:, st, :], -1.0, None, ALU.mult))
                    ins = V.tensor_tensor(stat[:, st + 2, :], sk, stat[:, st, :], ALU.add)
                then(ins, biased, g + 1)

            def normalise(g):
                br, j = GROUPS[g]
                st = 3 * (g % 2)
                dve.wait_ge(exped, g + 1)
                if br == "B":
                    step(V.tensor_tensor(stat[:, st + 1, :], stat[:, st + 1, :], stat[:, st + 2, :], ALU.add))
                step(V.reciprocal(stat[:, st + 1, :], stat[:, st + 1, :]))
                if br == "A":
                    step(V.tensor_scalar(stat[:, st + 1, 2:4], stat[:, st + 1, 2:4], lamp[:, 5:6], None, ALU.mult))
                for t in range(2):
                    a, b = COLS[t]
                    for i in range(2):
                        v = pr[:, g % 2, i, a:b]
                        if br == "A" and i == 1:
                            ins = V.scalar_tensor_tensor(pr[:, g % 2, 0, a:b], v, stat[:, st + 1, 2 + t:3 + t],
                                                         pr[:, g % 2, 0, a:b], ALU.mult, ALU.add)
                        else:
                            ins = V.tensor_scalar(v, v, stat[:, st + 1, 2 * i + t:2 * i + t + 1], None, ALU.mult)
                        if (t, i) != (1, 1):
                            step(ins)
                then(ins, probs, g + 1)

            def gate_y(g):
                m = g
                dve.wait_ge(yed, g + 1)
                then(V.tensor_tensor(vt[:, 1, :], y_bank(g), sg[:, m, :], ALU.mult),
                     y_kept, g - 4 + 1)
                split_value(vt[:, 1, :], Mhi[:, m, :], Mlo[:, m, :], M_ready, g - 4 + 1)

            for g in range(NG + 3):
                if g < NG:
                    bias_max(g)
                if g >= 7:
                    gate_y(g - 3)
                keep_ada(min(6, g // 2))
                if g < NG:
                    normalise(g)
            keep_ada(6)
            dve.wait_ge(sub_inv, 1)
            for i in range(2):
                v = yA[:, 2 * i:2 * i + 2, :]
                step(V.scalar_tensor_tensor(v, v, lamp[:, 6:7], headr[:, i, :].rearrange("p (a b) -> p a b", a=2),
                                            ALU.mult, ALU.mult))
                step(V.tensor_tensor(v, v, sg[:, 2 * i:2 * i + 2, :], ALU.mult))
            step(V.tensor_copy(Mhi[:, 0:4, :], yA[:, :, :]))
            then(V.tensor_tensor(Mlo[:, 0:4, :], yA[:, :, :], Mhi[:, 0:4, :].bitcast(F32), ALU.subtract), M_ready, 9)

            split_through(SPAN["gm"][0])
            for n, u in enumerate(SPAN["gm"]):
                ahead(u)
                dve.wait_ge(gate_e, n + 1)
                v = gate[:, 2 * n:2 * n + 2, :]
                step(V.tensor_scalar(v, v, 1.0, None, ALU.add))
                step(V.reciprocal(v, v))
            for i in range(4):
                for b, br in enumerate("abc"):
                    u = SPAN[f"up_{br}{i}"][0]
                    ahead(u)
                    dve.wait_ge(half_used, H0[u] + NH[u])
                    gt = gate[:, 8 * b + 2 * i:8 * b + 2 * i + 2, :]
                    dst = merged[:, 2 * i:2 * i + 2, :] if b == 0 else mt[:, :, :]
                    then(V.tensor_tensor(dst, gt, bank(u).rearrange("p (a b) -> p a b", a=2), ALU.mult),
                         bank_free[B0[u] % 2], B0[u] // 2 + 1)
                    if b:
                        step(V.tensor_tensor(merged[:, 2 * i:2 * i + 2, :], merged[:, 2 * i:2 * i + 2, :], mt[:, :, :],
                                             ALU.add))
            step(V.tensor_copy(Hhi[:, :, :], merged[:, :, :]))
            then(V.tensor_tensor(Hlo[:, :, :], merged[:, :, :], Hhi[:, :, :].bitcast(F32), ALU.subtract),
                 merge_ready, 1)
            for n, u in enumerate(SPAN["wo"]):
                ahead(u)
                dve.wait_ge(half_used, H0[u] + NH[u])
                v = xT[:, 2 * n:2 * n + 2, :]
                then(V.tensor_tensor(v, v, bank(u).rearrange("p (a b) -> p a b", a=2), ALU.add),
                     bank_free[B0[u] % 2], B0[u] // 2 + 1)
                dve.sem_inc(x_ready, 1)

            def renorm(i, gain, n):
                dve.wait_ge(rms_inv, F[i] + 1)
                for k in range(KT):
                    step(V.scalar_tensor_tensor(xT[:, k, :], xT[:, k, :], pcol[:, gain + k:gain + k + 1], rn[:, 1, :],
                                                ALU.mult, ALU.mult))
                dve.sem_inc(norm_done, 1)

            renorm("fin1", C_FG, 1)
            for i, (layer, s, who, w) in enumerate(((0, 1, 1, C_MIX), (0, 1, 0, C_MIX), (0, 4, 0, C_FFN))):
                step(V.scalar_tensor_tensor(cm[:, i, :], mod[:, layer, 8 * s:8 * s + 8, who], 1.0, pcol[:, w:w + 8],
                                            ALU.add, ALU.mult))
            step(V.tensor_tensor(lbc[:, 0, :], pcol[:, C_LB + 8:C_LB + 16], pcol[:, C_LB:C_LB + 8], ALU.subtract))
            dve.sem_inc(lb_e, 1)
            normed("ctx", cxT, cm[:, 0, :], mod[:, 0, 0:8, 1])
            for name in ("cnk", "cnv", "chi"):
                for u in SPAN[name]:
                    ahead(u)
            dve.wait_ge(lb_e, 2)
            step(V.tensor_scalar(lbc[:, 0, :], lbc[:, 0, :], 1.0, None, ALU.add))
            step(V.reciprocal(lbc[:, 1, :], lbc[:, 0, :]))
            step(V.tensor_scalar(lbc[:, 2, :], lbc[:, 1, :], -1.0, 1.0, ALU.mult, ALU.add))

            def forget_gates(name, d, n0):
                for n, u in enumerate(SPAN[name]):
                    ahead(u)
                    dve.wait_ge(f_e, n0 + n + 1)
                    v = hgt[:, :, :]
                    step(V.tensor_scalar(v, v, 1.0, None, ALU.add))
                    step(V.reciprocal(v, v))
                    for q in range(2):
                        c = 4 * d + 2 * n + q
                        step(V.tensor_scalar(lg[:, d, 2 * n + q, :], hgt[:, q, :], lbc[:, 2, c:c + 1], lbc[:, 1, c:c + 1],
                                             ALU.mult, ALU.add))
                    then(V.tensor_scalar(kk[:, d, 2 * n:2 * n + 2, :], lg[:, d, 2 * n:2 * n + 2, :], -1.0, 1.0,
                                         ALU.mult, ALU.add), f_set, n0 + n + 1)

            forget_gates("chf", 0, 0)
            forget_gates("chb", 1, 2)
            dve.wait_ge(f_ln, 1)
            for d in range(2):
                if d:
                    dve.wait_ge(ctx_kept, 4)
                for j in range(4):
                    r = slice(None, None, -1) if d else slice(None)
                    ins = V.tensor_tensor_scan(bc[:, j, r], ones[:, 0:S], lg[:, d, j, r], 0.0, ALU.mult, ALU.add)
                    if j < 3:
                        step(ins)
                then(ins, f_cum, d + 1)
                dve.wait_ge(f_exp, d + 1)
                then(V.tensor_tensor(kd[:, :, :], kd[:, :, :], kk[:, d, :, :], ALU.mult), f_mul, d + 1)

            normed("mix0", xT, cm[:, 1, :], mod[:, 0, 0:8, 0])
            for name in ("nq", "nk", "nv"):
                for u in SPAN[name]:
                    ahead(u)
            for n, u in enumerate(SPAN["hq"]):
                silu(u, 6 + n, hq[:, 2 * n:2 * n + 2, :], hgt[:, :, :])
            for u in SPAN["hi"]:
                ahead(u)
            forget_gates("hf", 0, 4)
            forget_gates("hb", 1, 6)
            for n, u in enumerate(SPAN["hg"]):
                silu(u, 8 + n, sgh[:, 2 * n:2 * n + 2, :], hgt[:, :, :])
            dve.wait_ge(f_ln, 2)
            step(V.memset(reset[:, :], 1.0))
            step(V.memset(reset[:, :].rearrange("p (c t) -> p c t", t=CH)[:, :, 0:1], 0.0))
            for t in range(NT):
                step(V.memset(attm[:, t, :], 0.0))
            step(V.memset(vbd[:, :, :, :], 0.0))
            dve.wait_ge(consts, 4)
            for d in range(2):
                r = slice(None, None, -1) if d else slice(None)
                if d:
                    dve.wait_ge(o_done, 4)
                    for t in range(NT):
                        step(V.memset(attm[:, t, :], 0.0))
                for j in range(4):
                    step(V.tensor_tensor_scan(bc[:, j, r], reset[:, :], lg[:, d, j, r], 0.0, ALU.mult, ALU.add))
                b3 = bc[:, :, :].rearrange("p h (c t) -> p (h c) t", t=CH)
                tot = (b3[:, :, 0:1] if d else b3[:, :, CH - 1:CH]).to_broadcast([P, 4 * NCH, CH])
                then(V.tensor_tensor(kd[:, :, :].rearrange("p h (c t) -> p (h c) t", t=CH), tot, b3, ALU.subtract),
                     f_cum, 3 + d)
                dve.wait_ge(f_exp, 3 + d)
                q3 = qe[:, :, :].rearrange("p h (c t) -> p (h c) t", t=CH)
                step(V.tensor_copy(dec[:, :].rearrange("p (c o) -> p c o", o=1), q3[:, :, 0:1] if d else q3[:, :, CH - 1:CH]))
                step(V.tensor_tensor(qe[:, :, :], qe[:, :, :], hq[:, :, :], ALU.mult))
                step(V.tensor_tensor(ke[:, :, :], ke[:, :, :], kk[:, d, :, :], ALU.mult))
                then(V.tensor_tensor(kd[:, :, :], kd[:, :, :], kk[:, d, :, :], ALU.mult), f_mul, 3 + d)
                for j in range(4):
                    n = 4 * d + j
                    keep_ada(6 + n // 2)
                    if n >= 1:
                        dve.wait_ge(kv_done, n)
                    for c in range(4):
                        for t in range(NT):
                            a = slice(c * CH, (c + 1) * CH)
                            step(V.tensor_copy(vbd[a, t, c, :], hv[a, t, j * P:(j + 1) * P]))
                    dve.sem_inc(vbd_set, 1)
                    dve.wait_ge(att_done, n + 1)
                    if n >= 1:
                        dve.wait_ge(o_done, n)
                    for t in range(NT):
                        src = attP[:, t * P:(t + 1) * P]
                        ins = V.copy_predicated(attm[:, t, :], smask[:, d, :].bitcast(U32), src)
                        if t == 0:
                            step(ins)
                    then(ins, att_set, n + 1)
                    first = NCH - 1 if d else 0
                    step(V.tensor_copy(sq[:, first, :], sctx[:, d, j, :]))
                    dve.wait_ge(kv_done, n + 1)
                    order = list(range(NCH - 1, -1, -1)) if d else list(range(NCH))
                    for a, b in zip(order[:-1], order[1:]):
                        step(V.scalar_tensor_tensor(sq[:, b, :], sq[:, a, :], dec[:, NCH * j + a:NCH * j + a + 1],
                                                    psS[:, a // 4, (a % 4) * P:(a % 4 + 1) * P], ALU.mult, ALU.add))
                    dve.sem_inc(st_set, 1)
                    dve.wait_ge(o_done, n + 1)
                    if d == 0:
                        ins = V.tensor_copy(oT[:, j, :], psY[:, 0:S])
                    else:
                        ins = V.tensor_tensor(oT[:, j, :], oT[:, j, :], psY[:, 0:S], ALU.add)
                    then(ins, o_kept, n + 1)
            keep_ada(10)
            dve.wait_ge(sub_inv, 2)
            for j in range(4):
                step(V.scalar_tensor_tensor(oT[:, j, :], oT[:, j, :], pcol[:, C_HGN + j:C_HGN + j + 1],
                                            headr[:, j // 2, (j % 2) * S:(j % 2 + 1) * S], ALU.mult, ALU.mult))
            step(V.tensor_tensor(oT[:, :, :], oT[:, :, :], sgh[:, :, :], ALU.mult))
            step(V.tensor_copy(Yhi[:, 4:8, :], oT[:, :, :]))
            then(V.tensor_tensor(Ylo[:, 4:8, :], oT[:, :, :], Yhi[:, 4:8, :].bitcast(F32), ALU.subtract),
                 M_ready, 10)
            dve.sem_inc(rpad_set, 1)
            dve.wait_ge(nb_set, 1)
            for h in range(8 + 3):
                if h < 8:
                    st = 3 * (h % 2)
                    dve.wait_ge(scored, NG + h + 1)
                    for t in range(NT):
                        o = psS[:, 2 * (h % 2) + t, 0:S].rearrange("p (a b) -> p a b", a=4)
                        step(V.tensor_tensor(o, o, nb[:, h, 2 - 2 * t:6 - 2 * t, ::-1], ALU.add))
                    then(V.tensor_reduce(stat[:, st, 0:2], psS[:, 2 * (h % 2):2 * (h % 2) + 2, :], AX.X, ALU.max,
                                         negate=True), biased, NG + h + 1)
                if h >= 3 and h % 2 == 0:
                    j = (h - 4) // 2
                    dve.wait_ge(yed, NG + 2 * j + 2)
                    src = na_y_bank(j)
                    then(V.tensor_copy(vt[:, 1, :], src), y_kept, 8 + j + 1)
                    split_value(vt[:, 1, :], Yhi[:, j, :], Ylo[:, j, :], M_ready, 10 + j + 1)
                if h < 8:
                    dve.wait_ge(exped, NG + h + 1)
                    step(V.reciprocal(stat[:, st + 1, 0:2], stat[:, st + 1, 0:2]))
                    for t in range(NT):
                        v = pn[:, h % 2, t, :]
                        ins = V.tensor_scalar(v, v, stat[:, st + 1, t:t + 1], None, ALU.mult)
                        if t == 0:
                            step(ins)
                    then(ins, probs, NG + h + 1)
            keep_ada(12)
            for i, (layer, s, who, w) in enumerate(((1, 1, 0, C_MIX + 8), (1, 4, 0, C_FFN + 8))):
                step(V.scalar_tensor_tensor(cm[:, 3 + i, :], mod[:, layer, 8 * s:8 * s + 8, who], 1.0,
                                            pcol[:, w:w + 8], ALU.add, ALU.mult))

            def add_gated(u, n, layer, s):
                dve.wait_ge(half_used, H0[u] + NH[u])
                for q in range(2):
                    k = 2 * n + q
                    ins = V.scalar_tensor_tensor(xT[:, k, :], bank(u)[:, q * S:(q + 1) * S],
                                                 mod[:, layer, 8 * s + k, 0:1], xT[:, k, :], ALU.mult, ALU.add)
                    if q == 0:
                        step(ins)
                then(ins, bank_free[B0[u] % 2], B0[u] // 2 + 1)
                dve.sem_inc(x_ready, 1)

            split_through(SPAN["evo"][0])
            for n, u in enumerate(SPAN["evo"]):
                ahead(u)
                add_gated(u, n, 0, 2)

            def conv_sides(z, src, w, n):
                dve.wait_ge(conv_a, n + 1)
                for q in range(2):
                    step(V.scalar_tensor_tensor(z[:, q, 1:S], src[:, q, 0:S - 1], pcol[:, w[0] + q:w[0] + q + 1],
                                                z[:, q, 1:S], ALU.mult, ALU.add))
                    ins = V.scalar_tensor_tensor(z[:, q, 0:S - 1], src[:, q, 1:S], pcol[:, w[1] + q:w[1] + q + 1],
                                                 z[:, q, 0:S - 1], ALU.mult, ALU.add)
                    if q == 0:
                        step(ins)
                return ins

            def feed_forward(layer):
                normed(f"ffn{layer}", xT, cm[:, 2 + 2 * layer, :], mod[:, layer, 24:32, 0])
                n0 = (FT // 2 + 4) * layer
                for i in range(FT // 2):
                    ua, uv = SPAN[f"fa{layer}.{i}"][0], SPAN[f"fv{layer}.{i}"][0]
                    ahead(ua)
                    z, src = fz[:, i % 2, :, :], fa[:, i % 2, :, :]
                    c = C_FCW + P * layer + 2 * i
                    then(conv_sides(z, src, (c, c + 2 * FT), n0 + i), gelu_in, FT // 2 * layer + i + 1)
                    ahead(uv)
                    dve.wait_ge(gelu_out, FT // 2 * layer + i + 1)
                    dve.wait_ge(half_used, H0[uv] + NH[uv])
                    then(V.tensor_tensor(z, z, bank(uv).rearrange("p (a b) -> p a b", a=2), ALU.mult),
                         bank_free[B0[uv] % 2], B0[uv] // 2 + 1)
                    split_value(z, Ghi[:, 2 * i:2 * i + 2, :], Glo[:, 2 * i:2 * i + 2, :], G_ready, n0 + i + 1)
                for i in range(FT // 2):
                    ahead(SPAN[f"fd{layer}.{i}"][0])
                u = SPAN[f"fd{layer}.{FT // 2 - 1}"][0]
                dve.wait_ge(half_used, H0[u] + NH[u])
                for k in range(KT):
                    step(V.scalar_tensor_tensor(xT[:, k, :], psS[:, k // 2, (k % 2) * S:(k % 2 + 1) * S],
                                                mod[:, layer, 40 + k, 0:1], xT[:, k, :], ALU.mult, ALU.add))
                    if k % 2:
                        dve.sem_inc(x_ready, 1)

            feed_forward(0)
            normed("mix1", xT, cm[:, 3, :], mod[:, 1, 0:8, 0])
            for i in range(4):
                uc, uu, ub = [SPAN[f"od{q}{i}"][0] for q in "cub"]
                n = FT // 2 + i
                z, src = fz[:, i % 2, :, :], fa[:, i % 2, :, :]
                ahead(uc)
                ahead(uu)
                dve.wait_ge(c_kept, i + 1)
                dve.wait_ge(half_used, H0[uu] + NH[uu])
                then(V.tensor_tensor(src, src, bank(uu).rearrange("p (a b) -> p a b", a=2), ALU.mult),
                     bank_free[B0[uu] % 2], B0[uu] // 2 + 1)
                dve.sem_inc(cu_set, 1)
                ahead(ub)
                step(conv_sides(z, src, (C_ODW + 2 * i, C_ODW + 16 + 2 * i), n))
                dve.wait_ge(half_used, H0[ub] + NH[ub])
                then(V.tensor_tensor(z, z, bank(ub).rearrange("p (a b) -> p a b", a=2), ALU.mult),
                     bank_free[B0[ub] % 2], B0[ub] // 2 + 1)
                split_value(z, Ghi[:, 2 * i:2 * i + 2, :], Glo[:, 2 * i:2 * i + 2, :], G_ready, n + 1)
            for n, u in enumerate(SPAN["odo"]):
                ahead(u)
                add_gated(u, n, 1, 2)
            feed_forward(1)
            renorm("last", C_FN, 2)

        @block.gpsimd
        def _(pool):
            G = nc.gpsimd
            steps = [0]

            def step(ins):
                steps[0] += 1
                ins.then_inc(pools, 1)
                pool.wait_ge(pools, steps[0])

            def rows(dst0, n, tile_, src):
                pool.dma_start(prow[dst0:dst0 + n, tile_, :], src).then_inc(par_in, 16)
            for src, at, n in PAR_ROWS:
                rows(at % P, n, at // P, src)
            for i, v in enumerate((lambda_q1, lambda_k1, lambda_q2, lambda_k2)):
                pool.dma_start(lam4[:, i:i + 1], v.rearrange("a d -> d a")).then_inc(misc_in, 16)
            pool.dma_start(smallr[0:1, 0:8], sinks).then_inc(misc_in, 16)
            pool.dma_start(bfc[:, :], b_forget.rearrange("a h -> h a")).then_inc(misc_in, 16)
            step(G.memset(ident[:, :], 0.0))
            step(G.affine_select(out=ident[:, :], in_=ident[:, :], compare_op=ALU.not_equal, fill=1.0, base=0,
                                 pattern=[[-1, P]], channel_multiplier=1))
            step(G.memset(sel[:, :, :], 0.0))
            step(G.affine_select(out=sel[:, :, :], in_=sel[:, :, :], compare_op=ALU.not_equal, fill=1.0, base=0,
                                 pattern=[[-1, 8], [0, P]], channel_multiplier=1))
            step(G.iota(distI[:, 0:P], pattern=[[-1, P]], base=0, channel_multiplier=1))
            step(G.iota(distI[:, P:384], pattern=[[-1, S]], base=P, channel_multiplier=1))
            pool.sem_inc(consts, 1)
            pool.wait_ge(consts, 2)
            for tile_, fill in ((dist, FAR), (distw, FAR), (cmask, -FAR)):
                for a, b, base in ((0, P, 0), (P, 384, P)):
                    step(G.affine_select(out=tile_[:, a:b], in_=tile_[:, a:b], compare_op=ALU.is_ge, fill=fill,
                                         base=base, pattern=[[-1, b - a]], channel_multiplier=1))
            step(G.affine_select(out=distw[:, P:384], in_=distw[:, P:384], compare_op=ALU.is_ge, fill=FAR,
                                 base=-1, pattern=[[1, S]], channel_multiplier=-1))
            pool.sem_inc(consts, 1)
            pool.wait_ge(norm_done, 1)
            step(G.memset(smask[:, :, :], 1.0))
            step(G.affine_select(out=smask[:, 0, :], in_=smask[:, 0, :], compare_op=ALU.is_ge, fill=0.0, base=0,
                                 pattern=[[1, P]], channel_multiplier=-1))
            step(G.affine_select(out=smask[:, 0, :], in_=smask[:, 0, :], compare_op=ALU.is_ge, fill=0.0, base=0,
                                 pattern=[[-CH, 4], [0, CH]], channel_multiplier=1))
            step(G.affine_select(out=smask[:, 1, :], in_=smask[:, 1, :], compare_op=ALU.is_ge, fill=0.0, base=0,
                                 pattern=[[-1, P]], channel_multiplier=1))
            step(G.affine_select(out=smask[:, 1, :], in_=smask[:, 1, :], compare_op=ALU.is_ge, fill=0.0, base=CH - 1,
                                 pattern=[[CH, 4], [0, CH]], channel_multiplier=-1))
            pool.sem_inc(consts, 1)
            pool.wait_ge(rpad_set, 1)
            step(G.memset(rpad[:, :], 0.0))
            pool.dma_start(rpad[:, 48:79], na_rpb_2.rearrange("a h r c -> (a h r) c")).then_inc(scr_out, 16)
            pool.wait_ge(scr_out, 16)
            step(G.memset(rrev[:, :], 0.0))
            step(G.tensor_copy(rrev[:, 0:127], rpad[:, 126::-1]))
            pool.dma_start(rscr, rrev[:, :]).then_inc(scr_out, 16)
            pool.wait_ge(scr_out, 32)
            for half_ in range(2):
                for h in range(8):
                    src = bass.AP(rscr.tensor, (h * 15 + 5 - half_) * P, [[1, HD], [P, 6], [1, HD]])
                    pool.dma_start(nb[half_ * HD:(half_ + 1) * HD, h, :, :], src).then_inc(nb_in, 16)
            pool.wait_ge(nb_in, 16 * 16)
            for half_ in range(2):
                a = slice(half_ * HD, (half_ + 1) * HD)
                v = nb[a, :, :, :].rearrange("p h j c -> p (h j) c")
                step(G.affine_select(out=v[:, :, 0:48], in_=v[:, :, 0:48], compare_op=ALU.is_ge, fill=-FAR,
                                     base=7 - 63, pattern=[[0, 48], [1, 48]], channel_multiplier=1))
                step(G.affine_select(out=v[:, :, 16:64], in_=v[:, :, 16:64], compare_op=ALU.is_ge, fill=-FAR,
                                     base=63 + 8 - 16, pattern=[[0, 48], [-1, 48]], channel_multiplier=-1))
            pool.sem_inc(nb_set, 1)


_INS = ['x', 'norm_gain', 'w_in', 'b_forget', 'lambda_q1', 'lambda_k1', 'lambda_q2', 'lambda_k2', 'subln_gain',
        'sinks', 'w_up_a', 'w_up_b', 'w_up_c', 'w_o', 'final_gain', 'c_2', 'ctx_2', 'c_ctx_2', 'ada_w_2', 'ada_b_2',
        'norm_mix_w_2', 'norm_ffn_w_2', 'ev_w_in_2', 'ev_w_out_2', 'na_rpb_2', 'hg_lb_logits_2', 'hg_norm_w_2',
        'od_w_in_2', 'od_conv_w_2', 'od_conv_b_2', 'od_w_out_2', 'ffn_w_up_2', 'ffn_conv_w_2', 'ffn_conv_b_2',
        'ffn_w_down_2', 'final_norm_w_2']
_OUTS = [((1, 256, 1024), 'float32')]


def kernel(**inputs):
    import numpy as _np
    import concourse.bacc as _bacc
    from concourse import mybir as _mybir
    from concourse.bass_utils import run_bass_kernel_spmd as _run

    nc = _bacc.Bacc("TRN2", target_bir_lowering=False, num_devices=1)
    arrays, args = {}, []
    for name in _INS:
        a = _np.ascontiguousarray(inputs[name])
        arrays[f"in_{name}_dram"] = a
        args.append(nc.dram_tensor(f"in_{name}_dram", a.shape, _mybir.dt.from_np(a.dtype), kind="ExternalInput").ap())
    for i, (shape, dtype) in enumerate(_OUTS):
        dt = _mybir.dt.from_np(_np.dtype(dtype))
        args.append(nc.dram_tensor(f"out_{i}_dram", shape, dt, kind="ExternalOutput").ap())
    build(nc, *args)
    r = _run(nc, [arrays], core_ids=[0])
    return r.results[0]["out_0_dram"]
```

```python
from contextlib import ExitStack
import math

import concourse.bass as bass
from concourse import mybir

F32 = mybir.dt.float32
F32R = mybir.dt.float32r
I32 = mybir.dt.int32
U32 = mybir.dt.uint32
ALU = mybir.AluOpType
ACT = mybir.ActivationFunctionType
AX = mybir.AxisListType

P = 128
D = 1024
KT = D // P
S = 256
NT = S // P
HD = 64
SCALE = HD ** -0.5
EPS = 1e-6
SUBLN_EPS = 1e-5
LAM_INIT = 0.8 - 0.6 * math.exp(-0.3 * 0)
FAR = 1e30
AW = 3
RAW = 4
WRING = 4
HALF = 1024
CH = 32
NCH = S // CH
FF = 2816
FT = FF // P
TABLES = "natural_log_exp_and_others"

O_QA, O_KA, O_VA, O_GA = 0, 512, 1024, 1536
O_QB, O_KB, O_GB = 2048, 2560, 2816
O_QC, O_KC, O_VC, O_FC, O_GC, O_GM = 3328, 3840, 4352, 4864, 4872, 5384
E_NQ, E_NK, E_NV, E_HQ, E_HF, E_HB, E_HI, E_HG = [512 * i for i in range(8)]

C_NG, C_FG, C_MIX, C_FFN, C_HGN, C_LB, C_C, C_CC, C_ODW, C_ODB, C_FN, C_SUB = (
    0, 8, 16, 32, 48, 52, 68, 76, 84, 108, 116, 124)
C_ADAB, C_FCW, C_FCB = 128, 256, 256 + 66


def plan_units():
    units, spans = [], {}

    def section(name, kind, src, col0, n, width=256, step=None, k0=0):
        spans[name] = range(len(units), len(units) + n)
        for i in range(n):
            units.append((kind, src, k0, col0 + i * (width if step is None else step), width))

    section("qa", "F", "w_in", O_QA, 2)
    section("ka", "F", "w_in", O_KA, 2)
    section("va", "T", "w_in", O_VA, 2)
    section("qb", "B", "w_in", O_QB, 2, step=128)
    section("kvb", "M", "w_in", O_KB, 1)
    section("qc", "F", "w_in", O_QC, 2)
    section("kc", "F", "w_in", O_KC, 2)
    section("vc", "T", "w_in", O_VC, 2)
    section("fc", "C", "w_in", O_FC, 1, width=128)
    section("ga", "F", "w_in", O_GA, 2)
    section("gb", "B", "w_in", O_GB, 2, step=128)
    section("gc", "F", "w_in", O_GC, 2)
    for i in range(4):
        for br in "bca":
            section(f"gm_{br}{i}", "F", "w_in", O_GM + D * "abc".index(br) + 256 * i, 1)
            section(f"up_{br}{i}", "U" if br != "b" else "V", f"w_up_{br}", i * 256, 1)
    section("wo", "F", "w_o", 0, 4)
    for name, kind, off in (("cnk", "F", E_NK), ("cnv", "T", E_NV), ("chi", "T", E_HI),
                            ("chf", "F", E_HF), ("chb", "F", E_HB),
                            ("nq", "F", E_NQ), ("nk", "F", E_NK), ("nv", "T", E_NV),
                            ("hq", "F", E_HQ), ("hi", "T", E_HI), ("hf", "F", E_HF), ("hb", "F", E_HB),
                            ("hg", "F", E_HG)):
        section(name, kind, "ev_w_in", off, 2)
    section("evo", "F", "ev_w_out", 0, 4)

    def ffn(layer):
        for i in range(FT // 2):
            section(f"fa{layer}.{i}", "F", f"ffn_up{layer}", i * 256, 1)
            section(f"fv{layer}.{i}", "F", f"ffn_up{layer}", FF + i * 256, 1)
        for i in range(FT // 2):
            section(f"fd{layer}.{i}", "D", f"ffn_down{layer}", 0, 1, width=D, k0=2 * i)

    ffn(0)
    for i in range(4):
        section(f"odc{i}", "F", "od_w_in", D + i * 256, 1)
        section(f"odu{i}", "F", "od_w_in", 2 * D + i * 256, 1)
        section(f"odb{i}", "F", "od_w_in", i * 256, 1)
    section("odo", "F", "od_w_out", 0, 4)
    ffn(1)
    return units, spans


def build(nc, x, norm_gain, w_in, b_forget, lambda_q1, lambda_k1, lambda_q2, lambda_k2, subln_gain, sinks,
          w_up_a, w_up_b, w_up_c, w_o, final_gain, c_2, ctx_2, c_ctx_2, ada_w_2, ada_b_2,
          norm_mix_w_2, norm_ffn_w_2, ev_w_in_2, ev_w_out_2, na_rpb_2, hg_lb_logits_2, hg_norm_w_2,
          od_w_in_2, od_conv_w_2, od_conv_b_2, od_w_out_2, ffn_w_up_2, ffn_conv_w_2, ffn_conv_b_2,
          ffn_w_down_2, final_norm_w_2, out, stop_at=None, probe=None):
    UNITS, SPAN = plan_units()
    NU = len(UNITS)
    SRC = {"w_in": w_in[0], "w_up_a": w_up_a[0], "w_up_b": w_up_b[0], "w_up_c": w_up_c[0], "w_o": w_o[0],
           "ev_w_in": ev_w_in_2[0], "ev_w_out": ev_w_out_2[0],
           "od_w_in": od_w_in_2[0], "od_w_out": od_w_out_2[0],
           "ffn_up0": ffn_w_up_2[0], "ffn_up1": ffn_w_up_2[1],
           "ffn_down0": ffn_w_down_2[0], "ffn_down1": ffn_w_down_2[1]}

    halves = {"C": 1, "U": 1, "V": 1}
    NH = [halves.get(k[0], 2) for k in UNITS]
    H0 = [sum(NH[:u]) for u in range(NU)]
    loads = {"B": 2, "V": 2}
    LD = [loads.get(k[0], 1) for k in UNITS]
    LANDED = [16 * sum(LD[v] for v in range(u % RAW, u + 1, RAW)) for u in range(NU)]
    banked = [int(k[0] != "D") for k in UNITS]
    B0 = [sum(banked[:u]) for u in range(NU)]
    split_order = [u for u in range(NU) if NH[u]]
    after = {u: u + 1 for u in split_order[:-1] if NH[u + 1]}

    with ExitStack() as ctx:
        def sb(name, shape, dt=F32):
            return ctx.enter_context(nc.sbuf_tensor(name, shape, dt))

        def sem(name):
            return ctx.enter_context(nc.semaphore(name))

        raw = sb("raw", [P, RAW, 2 * HALF])
        whi = sb("whi", [P, WRING, HALF], F32R)
        wlo = sb("wlo", [P, WRING, HALF], F32R)
        xT = sb("xT", [P, KT, S])
        Hhi = sb("Hhi", [P, KT, S], F32R)
        Hlo = sb("Hlo", [P, KT, S], F32R)
        tok = sb("tok", [P, NT, D])
        rn = sb("rn", [P, 2, S])
        ident = sb("ident", [P, P])
        ones = sb("ones", [P, S])
        pcol = sb("pcol", [P, 4 * P])
        eps = sb("eps", [P, 2])
        mod = sb("mod", [P, 2, 48, 2])
        cm = sb("cm", [P, 5, KT])
        cs = sb("cs", [P, KT, 2])
        cse = sb("cse", [P, 2 * KT])
        stat = sb("stat", [P, 6, 4])
        vt = sb("vt", [P, 2, S])
        prow = vt[:, :, :].rearrange("p a (b c) -> p (a b) c", c=P)
        sctx = sb("sctx", [P, 2, 4, P])

        with ExitStack() as a1:
            def s1(name, shape, dt=F32):
                return a1.enter_context(nc.sbuf_tensor(name, shape, dt))
            dist = s1("dist", [P, 384])
            distw = s1("distw", [P, 384])
            cmask = s1("cmask", [P, 384])
            distI = s1("distI", [P, 384], I32)
            sel = s1("sel", [8, 8, P])
            sinkb = s1("sinkb", [P, 4, 2, 2])
            smallr = s1("smallr", [P, 16])
            lam4 = s1("lam4", [HD, 4])
            lamp = s1("lamp", [P, 8])
            negc = s1("negc", [8, S])
            bfc = s1("bfc", [8, 1])
            sg = s1("sg", [P, 12, S])
            e2 = s1("e2", [P, 2, S])
            adaw0 = s1("adaw0", [P, AW, D])
            acc0 = s1("acc0", [P, 2, D])
            adat0 = s1("adat0", [P, D])
            with ExitStack() as a1a:
                def s2(name, shape, dt=F32):
                    return a1a.enter_context(nc.sbuf_tensor(name, shape, dt))
                qaT, kaT = s2("qaT", [P, 4, S]), s2("kaT", [P, 4, S])
                qbT, kbT = s2("qbT", [P, 4, S]), s2("kbT", [P, S])
                qcT, kcT = s2("qcT", [P, 4, S]), s2("kcT", [P, 4, S])
                va, vb, vc = s2("va", [P, NT, 512]), s2("vb", [P, NT, P]), s2("vc", [P, NT, 512])
                pr = s2("pr", [P, 2, 2, 384])
                pT = s2("pT", [P, 2, 2, 384])
                yA = s2("yA", [P, 4, S])
                fcw = yA[0:8, :, :]
            with ExitStack() as a1b:
                def s2b(name, shape, dt=F32):
                    return a1b.enter_context(nc.sbuf_tensor(name, shape, dt))
                Mhi = s2b("Mhi", [P, 12, S], F32R)
                Mlo = s2b("Mlo", [P, 12, S], F32R)
                gate = s2b("gate", [P, 2, 2, S])
                merged = s2b("merged", [P, 2, S])
                mt = s2b("mt", [P, 2, S])
                Whi, Wlo = s2b("Whi", [P, KT, S], F32R), s2b("Wlo", [P, KT, S], F32R)
        with ExitStack() as a2:
            def s3(name, shape, dt=F32):
                return a2.enter_context(nc.sbuf_tensor(name, shape, dt))
            naq, nak, cnk = s3("naq", [P, 4, S]), s3("nak", [P, 4, S]), s3("cnk", [P, 4, S])
            nav, cnv = s3("nav", [P, NT, 512]), s3("cnv", [P, NT, 512])
            Yhi, Ylo = s3("Yhi", [P, KT, S], F32R), s3("Ylo", [P, KT, S], F32R)
            nbB = s3("nbB", [P, 3, 6, HD])
            lbc = s3("lbc", [P, 3, 8])
            with ExitStack() as a2a:
                def s4(name, shape, dt=F32):
                    return a2a.enter_context(nc.sbuf_tensor(name, shape, dt))
                hq, hv = s4("hq", [P, 4, S]), s4("hv", [P, NT, 512])
                kk = s4("kk", [P, 2, 4, S])
                lg = s4("lg", [P, 2, 4, S])
                qe, ke, kd = s4("qe", [P, 4, S]), s4("ke", [P, 4, S]), s4("kd", [P, 4, S])
                kdt = s4("kdt", [P, 2, P])
                attm = s4("attm", [P, 2, P])
                vbd = s4("vbd", [P, NT, 4, P])
                sq = s4("sq", [P, NCH, P])
                oT = s4("oT", [P, 4, S])
                smask = s4("smask", [P, 2, P])
                reset = s4("reset", [P, S])
                hgt = s4("hgt", [P, 2, S])
                sgh = s4("sgh", [P, 4, S])
                dec = s4("dec", [P, 4 * NCH])
            with ExitStack() as a2b:
                def s5(name, shape, dt=F32):
                    return a2b.enter_context(nc.sbuf_tensor(name, shape, dt))
                pn = s5("pn", [P, 2, NT, 512])
                pnT = s5("pnT", [P, 4, 512])
                adaw1 = s5("adaw1", [P, AW, D])
                acc1 = s5("acc1", [P, 2, D])
                adat1 = s5("adat1", [P, D])
        with ExitStack() as a3:
            def s6(name, shape, dt=F32):
                return a3.enter_context(nc.sbuf_tensor(name, shape, dt))
            Ghi, Glo = s6("Ghi", [P, FT, S], F32R), s6("Glo", [P, FT, S], F32R)
            fa = s6("fa", [P, 2, 2, S])
            fz = s6("fz", [P, 2, 2, S])
        cxT = sg[:, 0:KT, :]
        sqv = tok[:, :, :].rearrange("p t (k s) -> p (t k) s", s=S)
        headr = tok[:, 1, :].rearrange("p (a b) -> p a b", a=2)
        headr2 = qe[:, :, :].rearrange("p (a h) s -> p a (h s)", a=2)
        nbA = tok[:, :, :].rearrange("p t n -> p (t n)")[:, 0:5 * 6 * HD].rearrange(
            "p (h j c) -> p h j c", h=5, j=6)
        rpad, rrev = hgt[0:120, 0, 0:P], hgt[0:120, 1, 0:P]
        rscr = nc.dram_tensor("rpb_rows", (120, P), F32, kind="Internal").ap()

        psG = ctx.enter_context(nc.psum_tensor("psG", [P, 2, 512], F32))
        psS = ctx.enter_context(nc.psum_tensor("psS", [P, 4, 512], F32))
        psX = ctx.enter_context(nc.psum_tensor("psX", [P, 512], F32))
        psY = ctx.enter_context(nc.psum_tensor("psY", [P, 512], F32))

        raw_landed = [sem(f"raw_landed{i}") for i in range(RAW)]
        hi_split, lo_split = sem("hi_split"), sem("lo_split")
        half_used, ada_kept = sem("half_used"), sem("ada_kept")
        adaw_landed = [sem(f"adaw_landed{i}") for i in range(AW)]
        acc_ready, acc_summed = sem("acc_ready"), sem("acc_summed")
        v_set, vhi_set = sem("v_set"), sem("vhi_set")
        M_high, core_done, down_part = sem("M_high"), sem("core_done"), sem("down_part")
        gate_used, ident_set = sem("gate_used"), sem("ident_set")
        bank_free = [sem("bank_free0"), sem("bank_free1")]
        acts, dves, pools = sem("act_step"), sem("dve_step"), sem("pool_step")
        tok_in, par_in, misc_in, scr_out, nb_in, out_done = [sem(n) for n in (
            "tok_in", "par_in", "misc_in", "scr_out", "nb_in", "out_done")]
        consts, ones_set = sem("consts"), sem("ones_set")
        turned, turned_kept = sem("turned"), sem("turned_kept")
        squares, sums, rms_inv, H_ready, norm_done = [sem(n) for n in (
            "squares", "sums", "rms_inv", "H_ready", "norm_done")]
        kept = sem("kept")
        silu_e = sem("silu_e")
        c_silu, c_exp = sem("c_silu"), sem("c_exp")
        small_mm, small_ev, small_ex = sem("small_mm"), sem("small_ev"), sem("small_ex")
        forget, forget_a = sem("forget"), sem("forget_a")
        scored, biased, exped, probs, turnedP, pT_kept, yed, y_kept = [sem(n) for n in (
            "scored", "biased", "exped", "probs", "turnedP", "pT_kept", "yed", "y_kept")]
        yA_kept = sem("yA_kept")
        sub_sq, sub_sum, sub_inv = sem("sub_sq"), sem("sub_sum"), sem("sub_inv")
        M_ready = sem("M_ready")
        gate_e = sem("gate_e")
        merge_ready = sem("merge_ready")
        x_ready = sem("x_ready")
        lb_e, lb_set = sem("lb_e"), sem("lb_set")
        f_e, f_set, f_ln, f_cum, f_exp, f_mul = [sem(n) for n in (
            "f_e", "f_set", "f_ln", "f_cum", "f_exp", "f_mul")]
        vbd_set, kd_turned, kd_kept, kv_done, att_done, att_set, st_set, o_done, o_kept = [sem(n) for n in (
            "vbd_set", "kd_turned", "kd_kept", "kv_done", "att_done", "att_set", "st_set", "o_done", "o_kept")]
        ctx_state, ctx_kept = sem("ctx_state"), sem("ctx_kept")
        nb_set, rpad_set = sem("nb_set"), sem("rpad_set")
        conv_a, gelu_in, gelu_out, G_ready, down_done = [sem(n) for n in (
            "conv_a", "gelu_in", "gelu_out", "G_ready", "down_done")]
        cu_set, c_kept = sem("cu_set"), sem("c_kept")
        out_turned, out_kept = sem("out_turned"), sem("out_kept")

        block = ctx.enter_context(nc.Block())

        def bank(u):
            return psG[:, B0[u] % 2, :]

        def y_bank(g):
            return psG[:, 1, 0:S] if g % 2 else psY[:, 0:S]

        def na_y_bank(j):
            return psG[:, 0, 0:S] if j % 2 else psY[:, 0:S]

        def na_x_bank(n):
            return psG[:, 1, :] if n % 2 else psX[:, :]

        def token_bank(n):
            return psX[:, :] if n % 2 else psY[:, :]

        ACCS = [(0, 0, 0), (0, 0, 1), (0, 1, 0), (0, 1, 1)] + [(0, s, 0) for s in range(2, 6)] + [
            (1, s, 0) for s in range(6)]

        def ada_bank(n):
            return psG[:, 0, 0:KT] if n in range(2, 7) else psX[:, 0:KT]

        def nb_head(h):
            return nbA[:, h, :, :] if h < 5 else nbB[:, h - 5, :, :]

        attP = psG[:, 1, 0:S]

        def half(ring, h):
            return ring[:, h % WRING, :]

        def raw_half(u, i):
            kind = UNITS[u][0]
            r = raw[:, u % RAW, :]
            if kind in "FM":
                return r.rearrange("p (k n) -> p k n", k=KT)[:, :, i * P:(i + 1) * P], KT
            if kind == "B":
                return r.rearrange("p (k i j r) -> p k i j r", k=KT, i=2, j=2)[:, :, :, i, :], KT
            if kind == "C":
                return r[:, 0:HALF], 1
            if kind in "UV":
                return r[:, 0:HALF], 1
            return r[:, i * HALF:(i + 1) * HALF], 1

        def ring_half(ring, u, i):
            kind = UNITS[u][0]
            a = half(ring, H0[u] + i)
            if kind in "FM":
                return a.rearrange("p (k n) -> p k n", k=KT)
            if kind == "B":
                return a.rearrange("p (k i r) -> p k i r", k=KT, i=2)
            return a

        GROUPS = [("A", h) for h in range(4)] + [("B", j) for j in range(4)] + [("C", j) for j in range(4)]
        NG = len(GROUPS)
        TSETS = [1 if b == "A" else 2 for b, _ in GROUPS]
        T0 = [sum(TSETS[:g]) for g in range(NG)]
        NT0 = T0[-1] + TSETS[-1]
        COLS = [(0, P), (P, 384)]
        KEPT = {"kc": 13, "vc": 15}
        col = lambda ap: ap.rearrange("a (k p) -> (a k) p", p=P)
        PAR_ROWS = [(col(norm_gain), C_NG, 8), (final_gain.rearrange("(k p) -> k p", p=P), C_FG, 8),
                    (col(norm_mix_w_2), C_MIX, 16), (col(norm_ffn_w_2), C_FFN, 16), (col(hg_norm_w_2), C_HGN, 4),
                    (hg_lb_logits_2.rearrange("n d (k p) -> (n d k) p", p=P), C_LB, 16), (col(c_2), C_C, 8),
                    (c_ctx_2.rearrange("(k p) -> k p", p=P), C_CC, 8),
                    (od_conv_w_2.rearrange("a t (k p) -> (a t k) p", p=P), C_ODW, 24), (col(od_conv_b_2), C_ODB, 8),
                    (final_norm_w_2.rearrange("(k p) -> k p", p=P), C_FN, 8), (subln_gain, C_SUB, 1),
                    (col(ada_b_2), C_ADAB, 96)]
        for l in range(2):
            PAR_ROWS += [(ffn_conv_w_2[l].rearrange("t (k p) -> (t k) p", p=P), C_FCW + P * l, 66),
                         (ffn_conv_b_2[l:l + 1, :].rearrange("t (k p) -> (t k) p", p=P), C_FCB + P * l, 22)]
        PARS, MISC = len(PAR_ROWS), 6
        F = {n: i for i, n in enumerate(["h1", "ctx", "fin1", "mix0", "ffn0", "mix1", "ffn1", "last"])}
        H_COUNT = {"h1": 1, "ctx": 2, "mix0": 3, "ffn0": 4, "mix1": 5, "ffn1": 6}

        @block.sync
        def _(sp):
            for u, (kind, src, k0, col0, width) in enumerate(UNITS):
                if stop_at is not None and u >= stop_at:
                    break
                slot = u % RAW
                if u == 1:
                    for rows, at, n in PAR_ROWS:
                        sp.dma_start(prow[at % P:at % P + n, at // P, :], rows).then_inc(par_in, 16)
                    for q, v in enumerate((lambda_q1, lambda_k1, lambda_q2, lambda_k2)):
                        sp.dma_start(lam4[:, q:q + 1], v.rearrange("a d -> d a")).then_inc(misc_in, 16)
                    sp.dma_start(smallr[0:1, 0:8], sinks).then_inc(misc_in, 16)
                    sp.dma_start(bfc[:, :], b_forget.rearrange("a h -> h a")).then_inc(misc_in, 16)
                if u >= RAW:
                    sp.wait_ge(lo_split, H0[u - RAW] + NH[u - RAW])
                w = SRC[src]
                r = raw[:, slot, :]
                if kind == "B":
                    rv = r.rearrange("p (k i n) -> p k i n", k=KT, i=2)
                    for i in range(2):
                        c = col0 + i * 256
                        sp.dma_start(rv[:, :, i, :], w[:, c:c + P].rearrange("(k p) n -> p k n", p=P)
                                     ).then_inc(raw_landed[slot], 16)
                elif kind == "V":
                    for i in range(2):
                        sp.dma_start(r[i * HD:(i + 1) * HD, 0:HALF].rearrange("p (k n) -> p k n", k=4),
                                     w[i * 256:(i + 1) * 256, col0:col0 + width].rearrange("(k p) n -> p k n", p=HD)
                                     ).then_inc(raw_landed[slot], 16)
                elif kind == "D":
                    sp.dma_start(r.rearrange("p (k n) -> p k n", k=2),
                                 w[k0 * P:(k0 + 2) * P, :].rearrange("(k p) n -> p k n", p=P)
                                 ).then_inc(raw_landed[slot], 16)
                else:
                    kt = 4 if kind == "U" else KT
                    sp.dma_start(r[:, 0:kt * width].rearrange("p (k n) -> p k n", k=kt),
                                 w[:, col0:col0 + width].rearrange("(k p) n -> p k n", p=P)
                                 ).then_inc(raw_landed[slot], 16)
            ov = out.rearrange("b (t p) d -> p (b t) d", p=P)
            for t in range(NT):
                sp.wait_ge(out_kept, 2 * (t + 1))
                sp.dma_start(ov[:, t, :], tok[:, t, :]).then_inc(out_done, 16)
            sp.wait_ge(out_done, 16 * NT)

        @block.tensor
        def _(pe):
            mm = nc.tensor.matmul

            def product(o, a_hi, a_lo, b_hi, b_lo, first, last, shared=False):
                mm(o, a_hi, b_lo, start=first, stop=False, skip_group_check=shared)
                mm(o, a_lo, b_hi, start=False, stop=False, skip_group_check=shared)
                return mm(o, a_hi, b_hi, start=False, stop=last, skip_group_check=shared)

            def open_bank(u):
                n = B0[u] // 2
                if n:
                    pe.wait_ge(bank_free[B0[u] % 2], n)

            def project(u, ahi, alo, ready=None, base=0, scale_ready=1):
                kind = UNITS[u][0]
                open_bank(u)
                o = bank(u)
                h = H0[u]

                def pair(k):
                    if ready is not None and k % 2 == 0:
                        pe.wait_ge(ready[0], ready[1] + k // 2 + 1)
                if kind in "FBC":
                    for n in range(NH[u]):
                        pe.wait_ge(lo_split, h + n + 1)
                        wh = half(whi, h + n).rearrange("p (k n) -> p k n", k=KT)
                        wl = half(wlo, h + n).rearrange("p (k n) -> p k n", k=KT)
                        for k in range(KT):
                            if n == 0:
                                pair(k)
                            last = product(o[:, n * S:(n + 1) * S], wh[:, k, :], wl[:, k, :],
                                           ahi[:, base + k, :], alo[:, base + k, :], k == 0, k == KT - 1)
                        last.then_inc(half_used, 1)
                elif kind == "T":
                    for t in range(NT):
                        for k in range(KT):
                            if t == 0:
                                pair(k)
                            if t == 0 and k % 4 == 0:
                                pe.wait_ge(lo_split, h + k // 4 + 1)
                            q, n = k // 4, k % 4
                            last = product(o[:, t * 256:(t + 1) * 256],
                                           ahi[:, base + k, t * P:(t + 1) * P], alo[:, base + k, t * P:(t + 1) * P],
                                           half(whi, h + q)[:, n * 256:(n + 1) * 256],
                                           half(wlo, h + q)[:, n * 256:(n + 1) * 256], k == 0, k == KT - 1)
                            if t == NT - 1 and k % 4 == 3:
                                last.then_inc(half_used, 1)
                elif kind == "M":
                    for n in range(2):
                        pe.wait_ge(lo_split, h + n + 1)
                        wh = half(whi, h + n).rearrange("p (k n) -> p k n", k=KT)
                        wl = half(wlo, h + n).rearrange("p (k n) -> p k n", k=KT)
                        for t in range(1 if n == 0 else NT):
                            for k in range(KT):
                                if n == 0:
                                    last = product(o[:, 0:S], wh[:, k, :], wl[:, k, :], ahi[:, k, :], alo[:, k, :],
                                                   k == 0, k == KT - 1)
                                else:
                                    last = product(o[:, S + t * P:S + (t + 1) * P],
                                                   ahi[:, k, t * P:(t + 1) * P], alo[:, k, t * P:(t + 1) * P],
                                                   wh[:, k, :], wl[:, k, :], k == 0, k == KT - 1)
                        last.then_inc(half_used, 1)
                else:
                    pe.wait_ge(lo_split, h + 1)
                    wh = half(whi, h).rearrange("p (k n) -> p k n", k=4)
                    wl = half(wlo, h).rearrange("p (k n) -> p k n", k=4)
                    for n in range(2):
                        for k in range(4):
                            last = product(o[:, n * S:(n + 1) * S], wh[:, k, n * P:(n + 1) * P],
                                           wl[:, k, n * P:(n + 1) * P], ahi[:, base + k, :], alo[:, base + k, :],
                                           k == 0, k == 3)
                    last.then_inc(half_used, 1)

            def sum_ada(n):
                pe.wait_ge(acc_ready, n + 1)
                if n:
                    pe.wait_ge(ada_kept, n)
                acc = acc0 if n < 8 else acc1
                for k in range(KT):
                    last = mm(ada_bank(n)[:, k:k + 1], acc[:, n % 2, k * P:(k + 1) * P], ones[:, 0:1],
                              start=True, stop=True)
                last.then_inc(acc_summed, 1)

            def sum_squares(i):
                for k in range(KT):
                    if k % 2 == 0:
                        pe.wait_ge(squares, 4 * i + k // 2 + 1)
                    last = mm(psY[:, 0:S], ones[:, 0:P], sqv[:, k, :], start=(k == 0), stop=(k == KT - 1))
                last.then_inc(sums, 1)


            def turn_tokens(i):
                pe.wait_ge(tok_in, 16 * NT * (i + 1))
                for k4 in range(4):
                    if k4 >= 2:
                        pe.wait_ge(turned_kept, 4 * i + k4 - 1)
                    for kk_ in range(2):
                        k = 2 * k4 + kk_
                        for t in range(NT):
                            last = nc.tensor.transpose(token_bank(k4)[:, kk_ * S + t * P:kk_ * S + (t + 1) * P],
                                                       tok[:, t, k * P:(k + 1) * P], ident[:, :])
                    last.then_inc(turned, 1)

            pe.wait_ge(ident_set, 1)
            pe.wait_ge(ones_set, 1)
            turn_tokens(0)
            pe.wait_ge(par_in, 16 * PARS)
            pe.wait_ge(turned_kept, 4)
            for i, rows in enumerate((125, 96, 88, 88)):
                last = nc.tensor.transpose(psX[:, i * P:i * P + rows], prow[0:rows, i, :], ident[0:rows, 0:rows])
            last.then_inc(small_mm, 1)
            sum_squares(F["h1"])

            for name in ("qa", "ka", "va", "qb", "kvb", "qc", "kc", "vc", "fc", "ga", "gb", "gc"):
                for u in SPAN[name]:
                    project(u, Hhi, Hlo, ready=(H_ready, 0) if u == 0 else None)
                if name == "ka":
                    pe.wait_ge(misc_in, 16 * MISC)
                    pe.wait_ge(small_ev, 2)
                    mm(psX[:, 0:2], ones[0:HD, 0:P], lamp[0:HD, 0:2], start=True, stop=True)
                    mm(psX[:, 8:16], ones[0:1, 0:P], smallr[0:1, 0:8], start=True, stop=True).then_inc(small_mm, 1)
                if name == "gb":
                    pe.wait_ge(small_ex, 1)
                    for n in range(2):
                        sum_ada(n)

            def scores(g):
                br, j = GROUPS[g]
                if g == 0:
                    pe.wait_ge(kept, KEPT["kc"])
                if g >= 2:
                    pe.wait_ge(exped, g - 1)
                if br == "C" and j == 0:
                    pe.wait_ge(forget, 1)
                for i in range(2):
                    q = (qaT, qbT, qcT)["ABC".index(br)][i * HD:(i + 1) * HD, j, :]
                    k = kaT[i * HD:(i + 1) * HD, j, :] if br == "A" else (
                        kbT[i * HD:(i + 1) * HD, :] if br == "B" else kcT[i * HD:(i + 1) * HD, j, :])
                    for t in range(NT):
                        o = psS[:, 2 * (g % 2) + i, COLS[t][0]:COLS[t][1]]
                        last = mm(o, q[:, t * P:(t + 1) * P], k[:, 0:(t + 1) * P], start=True, stop=(br != "C"))
                        if br == "C":
                            last = mm(o, sel[0:8, 2 * j + i, :], negc[0:8, 0:(t + 1) * P], start=False, stop=True)
                last.then_inc(scored, 1)

            def turn_probs(g, i):
                n = T0[g] + i
                pe.wait_ge(probs, g + 1)
                if n >= 1:
                    pe.wait_ge(pT_kept, n)
                for b in range(3):
                    last = nc.tensor.transpose(psX[:, b * P:(b + 1) * P], pr[:, g % 2, i, b * P:(b + 1) * P],
                                               ident[:, :])
                last.then_inc(turnedP, 1)

            def weigh(g):
                br, j = GROUPS[g]
                pe.wait_ge(pT_kept, T0[g] + TSETS[g])
                if g == 0:
                    pe.wait_ge(kept, KEPT["vc"])
                if 2 <= g < 6:
                    pe.wait_ge(yA_kept, g - 1)
                elif g >= 6:
                    pe.wait_ge(y_kept, g - 5)
                for i in range(TSETS[g]):
                    if br == "A":
                        rows, v = slice(0, P), va[:, :, j * P:(j + 1) * P]
                    elif br == "B":
                        rows, v = slice(i * HD, (i + 1) * HD), vb[:, :, i * HD:(i + 1) * HD]
                    else:
                        rows, v = slice(i * HD, (i + 1) * HD), vc[:, :, (2 * j + i) * HD:(2 * j + i + 1) * HD]
                    y = y_bank(g)
                    mm(y[rows, :], v[:, 0, :], pT[:, g % 2, i, 0:S], start=True, stop=False)
                    last = mm(y[rows, P:S], v[:, 1, :], pT[:, g % 2, i, S:384], start=False, stop=True)
                last.then_inc(yed, 1)

            for b in range(2):
                pe.wait_ge(bank_free[b], (B0[SPAN["gc"][1]] + 2 - b) // 2)
            pe.wait_ge(ada_kept, 2)
            for g in range(NG + 2):
                if g < NG:
                    scores(g)
                if 1 <= g <= NG:
                    turn_probs(g - 1, 0)
                for n in {2: (2, 3), 4: (4,), 7: (5,), 10: (6,)}.get(g, ()):
                    sum_ada(n)
                if 1 <= g <= NG and TSETS[g - 1] == 2:
                    turn_probs(g - 1, 1)
                if g >= 2:
                    weigh(g - 2)
            pe.wait_ge(sub_sq, 1)
            for i in range(2):
                last = mm(psS[:, i, :], ones[:, 0:P], sqv[:, 2 * i:2 * i + 2, :], start=True, stop=True)
            last.then_inc(sub_sum, 1)

            pe.wait_ge(ada_kept, 7)
            pe.wait_ge(y_kept, 8)
            for i in range(4):
                for b, br in enumerate("bca"):
                    project(SPAN[f"gm_{br}{i}"][0], Hhi, Hlo)
                    if i == 0:
                        pe.wait_ge(M_ready, b + 1)
                    project(SPAN[f"up_{br}{i}"][0], Mhi, Mlo, base=4 * "abc".index(br))
                if i == 1:
                    turn_tokens(1)
                elif i == 2:
                    pe.wait_ge(turned_kept, 8)
                    sum_ada(7)
                    sum_squares(F["ctx"])
            for u in SPAN["wo"]:
                project(u, Whi, Wlo, ready=(merge_ready, 0) if u == SPAN["wo"][0] else None)

            for name in ("cnk", "cnv", "chi", "chf", "chb"):
                for u in SPAN[name]:
                    project(u, Hhi, Hlo, ready=(H_ready, 4) if u == SPAN["cnk"][0] else None)
                    if u == SPAN["cnk"][0]:
                        sum_squares(F["fin1"])
                    if u == SPAN["chi"][0]:
                        sum_squares(F["mix0"])

            def turn_kd(n, j):
                if n >= 1:
                    pe.wait_ge(kd_kept, n)
                for t in range(NT):
                    last = nc.tensor.transpose(psX[:, t * P:(t + 1) * P],
                                               kd[:, j, t * P:(t + 1) * P], ident[:, :])
                last.then_inc(kd_turned, 1)

            def ctx_states(d):
                for j in range(4):
                    n = 4 * d + j
                    pe.wait_ge(f_mul, d + 1)
                    turn_kd(n, j)
                    pe.wait_ge(kd_kept, n + 1)
                    if n >= 1:
                        pe.wait_ge(ctx_kept, n)
                    for t in range(NT):
                        last = mm(psS[:, 0, 0:P], kdt[:, t, :], hv[:, t, j * P:(j + 1) * P],
                                  start=(t == 0), stop=(t == NT - 1))
                    last.then_inc(ctx_state, 1)

            for name in ("nq", "nk", "nv", "hq", "hi", "hf", "hb", "hg"):
                for u in SPAN[name]:
                    project(u, Hhi, Hlo, ready=(H_ready, 8) if u == SPAN["nq"][0] else None)
                if name in ("nk", "nv"):
                    ctx_states(int(name == "nv"))

            for b in range(2):
                pe.wait_ge(bank_free[b], (B0[SPAN["hg"][1]] + 2 - b) // 2)
            for d in range(2):
                for j in range(4):
                    n = 4 * d + j
                    pe.wait_ge(f_mul, 3 + d)
                    turn_kd(8 + n, j)
                    if n:
                        pe.wait_ge(att_set, n)
                    for t in range(NT):
                        last = mm(attP[:, t * P:(t + 1) * P],
                                  ke[:, j, t * P:(t + 1) * P], qe[:, j, t * P:(t + 1) * P], start=True, stop=True)
                    last.then_inc(att_done, 1)
                    pe.wait_ge(kd_kept, 8 + n + 1)
                    pe.wait_ge(vbd_set, n + 1)
                    if n >= 1:
                        pe.wait_ge(st_set, n)
                    for t in range(NT):
                        last = mm(psS[:, t, :], kdt[:, t, :], vbd[:, t, :, :], start=True, stop=True)
                    last.then_inc(kv_done, 1)
                    pe.wait_ge(att_set, n + 1)
                    if n >= 1:
                        pe.wait_ge(o_kept, n)
                    pe.wait_ge(st_set, n + 1)
                    for t in range(NT):
                        mm(psY[:, t * P:(t + 1) * P], hv[:, t, j * P:(j + 1) * P], attm[:, t, :],
                           start=True, stop=False)
                        for c in range(4):
                            cc = 4 * t + c
                            last = mm(psY[:, cc * CH:(cc + 1) * CH], sq[:, cc, :], qe[:, j, cc * CH:(cc + 1) * CH],
                                      start=False, stop=(c == 3))
                    last.then_inc(o_done, 1)
            pe.wait_ge(sub_sq, 2)
            for i in range(2):
                last = mm(psS[:, 2 + i, :], ones[:, 0:P], kd[:, 2 * i:2 * i + 2, :], start=True, stop=True)
            last.then_inc(sub_sum, 1)

            def na_scores(h):
                j, i = h // 2, h % 2
                if h >= 2:
                    pe.wait_ge(exped, NG + h - 1)
                elif h == 1:
                    pe.wait_ge(sub_inv, 2)
                for t in range(NT):
                    q = naq[i * HD:(i + 1) * HD, j, t * P:(t + 1) * P]
                    o = psS[:, 2 * (h % 2) + t, :]
                    mm(o[:, 0:S], q, nak[i * HD:(i + 1) * HD, j, :], start=True, stop=True)
                    last = mm(o[:, S:512], q, cnk[i * HD:(i + 1) * HD, j, :], start=True, stop=True)
                last.then_inc(scored, 1)



            def na_turn(h, t):
                n = 2 * h + t
                pe.wait_ge(probs, NG + h + 1)
                if n >= 2:
                    pe.wait_ge(pT_kept, NT0 + n - 1)
                for b in range(4):
                    last = nc.tensor.transpose(na_x_bank(n)[:, b * P:(b + 1) * P], pn[:, h % 2, t, b * P:(b + 1) * P],
                                               ident[:, :])
                last.then_inc(turnedP, 1)

            def na_weigh(h):
                j, i = h // 2, h % 2
                pe.wait_ge(pT_kept, NT0 + 2 * h + 2)
                if h % 2 == 0 and j >= 2:
                    pe.wait_ge(y_kept, 8 + j - 1)
                for t in range(NT):
                    for b in range(4):
                        v = (nav if b < 2 else cnv)[:, b % 2, h * HD:(h + 1) * HD]
                        last = mm(na_y_bank(j)[i * HD:(i + 1) * HD, t * P:(t + 1) * P], v, pnT[:, (2 * h + t) % 4, b * P:(b + 1) * P],
                                  start=(b == 0), stop=(b == 3))
                last.then_inc(yed, 1)

            for h in range(8 + 2):
                if h < 8:
                    na_scores(h)
                if 1 <= h <= 8:
                    na_turn(h - 1, 0)
                    na_turn(h - 1, 1)
                if h >= 2:
                    na_weigh(h - 2)
            pe.wait_ge(M_ready, 8)
            for u in SPAN["evo"]:
                project(u, Yhi, Ylo)

            def feed_forward(layer):
                sum_squares(F[f"ffn{layer}"])
                for i in range(FT // 2):
                    for part in ("fa", "fv"):
                        u = SPAN[f"{part}{layer}.{i}"][0]
                        project(u, Hhi, Hlo, ready=(H_ready, 12 + 8 * layer) if part == "fa" and i == 0 else None)
                    if layer == 0 and i in (5, 10):
                        sum_ada({5: 8, 10: 9}[i])
                for i in range(FT // 2):
                    u = SPAN[f"fd{layer}.{i}"][0]
                    pe.wait_ge(G_ready, (FT // 2 + 4) * layer + i + 1)
                    h = H0[u]
                    if i < FT // 2 - 1:
                        for q in range(2):
                            k = 2 * i + q
                            pe.wait_ge(lo_split, h + q + 1)
                            for n in range(KT):
                                last = product(psS[:, n // 2, (n % 2) * S:(n % 2 + 1) * S],
                                               half(whi, h + q)[:, n * P:(n + 1) * P],
                                               half(wlo, h + q)[:, n * P:(n + 1) * P],
                                               Ghi[:, k, :], Glo[:, k, :], k == 0 and n % 2 == 0, False, shared=True)
                            last.then_inc(half_used, 1)
                    else:
                        pe.wait_ge(lo_split, h + 2)
                        for n in range(KT):
                            for q in range(2):
                                k = 2 * i + q
                                last = product(psS[:, n // 2, (n % 2) * S:(n % 2 + 1) * S],
                                               half(whi, h + q)[:, n * P:(n + 1) * P],
                                               half(wlo, h + q)[:, n * P:(n + 1) * P],
                                               Ghi[:, k, :], Glo[:, k, :], False, q == 1, shared=True)
                            if n in (1, 3, 5):
                                last.then_inc(down_part, 1)
                        last.then_inc(half_used, 2)
                    if layer == 0 and i == 6:
                        sum_ada(10)

            feed_forward(0)
            sum_squares(F["mix1"])
            for i in range(4):
                for part in "cub":
                    u = SPAN[f"od{part}{i}"][0]
                    project(u, Hhi, Hlo, ready=(H_ready, 16) if part == "c" and i == 0 else None)
                if i >= 1:
                    sum_ada(10 + i)
            pe.wait_ge(G_ready, FT // 2 + 4)
            for u in SPAN["odo"]:
                project(u, Ghi, Glo)
            feed_forward(1)
            sum_squares(F["last"])

            pe.wait_ge(norm_done, 2)
            for t in range(NT):
                for k4 in range(2):
                    n = 2 * t + k4
                    if n >= 2:
                        pe.wait_ge(out_kept, n - 1)
                    for q in range(4):
                        k = 4 * k4 + q
                        last = nc.tensor.transpose(token_bank(n)[:, q * P:(q + 1) * P], xT[:, k, t * P:(t + 1) * P], ident[:, :])
                    last.then_inc(out_turned, 1)

        @block.scalar
        def _(act):
            steps = [0]
            half_at = [0]

            def step(ins):
                steps[0] += 1
                ins.then_inc(acts, 1)
                act.wait_ge(acts, steps[0])

            def split_through(u):
                while half_at[0] < H0[u] + NH[u]:
                    h = half_at[0]
                    v = next(w for w in split_order if H0[w] <= h < H0[w] + NH[w])
                    i = h - H0[v]
                    if i == 0:
                        act.wait_ge(raw_landed[v % RAW], LANDED[v])
                    if h >= WRING:
                        act.wait_ge(half_used, h - WRING + 1)
                    src, _ = raw_half(v, i)
                    nc.scalar.copy(ring_half(whi, v, i), src).then_inc(hi_split, 1)
                    half_at[0] += 1

            def ahead(u):
                if u in after:
                    split_through(after[u])

            def keep(u, dst, scale=None, free=True):
                act.wait_ge(half_used, H0[u] + NH[u])
                src = bank(u)
                nc.scalar.activation(dst, src.rearrange("p (a b) -> p a b", a=2), ACT.Copy,
                                     scale=1.0 if scale is None else scale).then_inc(bank_free[B0[u] % 2], 1)
                act.wait_ge(bank_free[B0[u] % 2], B0[u] // 2 + 1)
                act.sem_inc(kept, 1)

            nc.scalar.preload_act_table_set(TABLES)
            ctxv = ctx_2.rearrange("b (t p) d -> p (b t) d", p=P)
            xv = x.rearrange("b (t p) d -> p (b t) d", p=P)
            for t in range(NT):
                act.dma_start(tok[:, t, :], xv[:, t, :]).then_inc(tok_in, 16)
            def turn_keep(i, g, dst):
                act.wait_ge(turned, 4 * i + g + 1)
                nc.scalar.copy(dst, token_bank(g).rearrange("p (a b) -> p a b", a=2)).then_inc(turned_kept, 1)
                act.wait_ge(turned_kept, 4 * i + g + 1)

            def norm(i, src, e):
                norm_squares(src)
                inverse(i)

            def norm_squares(src):
                for g in range(4):
                    nc.scalar.activation(sqv[:, 2 * g:2 * g + 2, :], src[:, 2 * g:2 * g + 2, :], ACT.Square
                                         ).then_inc(squares, 1)

            def highs(i, shift=None):
                n0 = KT * (H_COUNT[i] - 1)
                for k in range(KT):
                    act.wait_ge(v_set, n0 + k + 1)
                    if shift is None:
                        ins = nc.scalar.copy(Hhi[:, k, :], vt[:, k % 2, :])
                    else:
                        ins = nc.scalar.activation(Hhi[:, k, :], vt[:, k % 2, :], ACT.Identity,
                                                   bias=shift[:, k:k + 1])
                    ins.then_inc(vhi_set, 1)

            def inverse(i):
                act.wait_ge(sums, i + 1)
                step(nc.scalar.activation(rn[:, 0, :], psY[:, 0:S], ACT.Ln, bias=eps[:, 0:1], scale=1.0 / D))
                nc.scalar.activation(rn[:, 1, :], rn[:, 0, :], ACT.Exp, scale=-0.5).then_inc(rms_inv, 1)
                act.wait_ge(rms_inv, i + 1)

            act.wait_ge(ones_set, 1)
            split_through(0)
            for g in range(4):
                turn_keep(0, g, xT[:, 2 * g:2 * g + 2, :])
            norm(F["h1"], xT, None)
            act.wait_ge(c_exp, 1)
            nc.scalar.activation(cse[:, :], pcol[:, C_C:C_C + 16], ACT.Exp, scale=-1.0).then_inc(c_exp, 1)
            highs("h1")

            for name, dst, sc in (("qa", qaT, SCALE), ("ka", kaT, None)):
                for n, u in enumerate(SPAN[name]):
                    ahead(u)
                    keep(u, dst[:, 2 * n:2 * n + 2, :], sc)
            act.wait_ge(small_mm, 2)
            step(nc.scalar.activation(lamp[:, 2:4], psX[:, 0:2], ACT.Exp))
            nc.scalar.copy(smallr[:, 8:16], psX[:, 8:16]).then_inc(small_ex, 1)

            def keep_values(name, dst):
                for n, u in enumerate(SPAN[name]):
                    ahead(u)
                    keep(u, dst[:, :, n * 256:(n + 1) * 256])

            keep_values("va", va)
            for n, u in enumerate(SPAN["qb"]):
                ahead(u)
                keep(u, qbT[:, 2 * n:2 * n + 2, :], SCALE)
            u = SPAN["kvb"][0]
            ahead(u)
            act.wait_ge(half_used, H0[u] + NH[u])
            step(nc.scalar.copy(kbT[:, :], bank(u)[:, 0:S]))
            nc.scalar.copy(vb[:, :, :], bank(u)[:, S:512].rearrange("p (a b) -> p a b", a=2)
                           ).then_inc(bank_free[B0[u] % 2], 1)
            act.wait_ge(bank_free[B0[u] % 2], B0[u] // 2 + 1)
            act.sem_inc(kept, 1)
            for name, dst, sc in (("qc", qcT, SCALE), ("kc", kcT, None)):
                for n, u in enumerate(SPAN[name]):
                    ahead(u)
                    keep(u, dst[:, 2 * n:2 * n + 2, :], sc)
            keep_values("vc", vc)
            u = SPAN["fc"][0]
            ahead(u)
            act.wait_ge(forget_a, 1)
            step(nc.scalar.activation(fcw[:, 2, :], fcw[:, 1, :], ACT.Exp, scale=-1.0))
            nc.scalar.activation(fcw[:, 3, :], fcw[:, 2, :], ACT.Ln, bias=ones[0:8, 0:1]).then_inc(forget_a, 1)

            def silu_exp(u, n):
                ahead(u)
                act.wait_ge(half_used, H0[u] + NH[u])
                if n >= 1:
                    act.wait_ge(bank_free[(B0[u] - 1) % 2], (B0[u] - 1) // 2 + 1)
                nc.scalar.activation(e2[:, :, :], bank(u).rearrange("p (a b) -> p a b", a=2), ACT.Exp, scale=-1.0
                                     ).then_inc(silu_e, 1)

            n = 0
            for name in ("ga", "gb", "gc"):
                for u in SPAN[name]:
                    silu_exp(u, n)
                    n += 1

            def exps(g, tiles, rows):
                act.wait_ge(biased, g + 1)
                for n, (dst, src) in enumerate(tiles):
                    ins = nc.scalar.activation(dst, src, ACT.Exp, bias=stat[:, 0 + 3 * (g % 2), n:n + 1],
                                               accum_out=stat[:, 1 + 3 * (g % 2), n:n + 1])
                    if n < len(tiles) - 1 or rows:
                        step(ins)
                if rows:
                    ins = nc.scalar.activation(stat[:, 2 + 3 * (g % 2), 0:4], stat[:, 2 + 3 * (g % 2), 0:4], ACT.Exp)
                ins.then_inc(exped, 1)
                act.wait_ge(exped, g + 1)

            for g in range(NG + 2):
                if g < NG:
                    if g >= 2:
                        act.wait_ge(turnedP, T0[g - 2] + TSETS[g - 2])
                    exps(g, [(pr[:, g % 2, i, COLS[t][0]:COLS[t][1]],
                              psS[:, 2 * (g % 2) + i, COLS[t][0]:COLS[t][1]]) for i in range(2) for t in range(2)],
                         GROUPS[g][0] == "B")
                if 1 <= g <= NG:
                    for i in range(TSETS[g - 1]):
                        n = T0[g - 1] + i
                        act.wait_ge(turnedP, n + 1)
                        if g >= 3 and i == 0:
                            act.wait_ge(yed, g - 2)
                        nc.scalar.copy(pT[:, (g - 1) % 2, i, :], psX[:, 0:384]).then_inc(pT_kept, 1)
                        act.wait_ge(pT_kept, n + 1)
                if g == NG + 1:
                    act.wait_ge(yed, NG)
                if 2 <= g < 6:
                    act.wait_ge(yed, g - 1)
                    nc.scalar.copy(yA[:, g - 2, :], y_bank(g - 2)).then_inc(yA_kept, 1)
                    act.wait_ge(yA_kept, g - 1)
            nc.scalar.activation(sqv[:, 0:4, :], yA[:, :, :], ACT.Square).then_inc(sub_sq, 1)
            act.wait_ge(y_kept, 8)
            for b in (1, 2):
                nc.scalar.copy(Mhi[:, 4 * b:4 * b + 4, :], sg[:, 4 * b:4 * b + 4, :]).then_inc(M_high, 1)
            act.wait_ge(sub_sum, 1)
            step(nc.scalar.activation(headr[:, :, :], psS[:, 0:2, :], ACT.Ln, bias=eps[:, 1:2], scale=1.0 / P))
            nc.scalar.activation(headr[:, :, :], headr[:, :, :], ACT.Exp, scale=-0.5).then_inc(sub_inv, 1)
            act.wait_ge(sub_inv, 1)

            split_through(SPAN["gm_b0"][0])
            n = 0
            for i in range(4):
                for br in "bca":
                    u = SPAN[f"gm_{br}{i}"][0]
                    ahead(u)
                    ahead(SPAN[f"up_{br}{i}"][0])
                    act.wait_ge(half_used, H0[u] + NH[u])
                    if n >= 2:
                        act.wait_ge(gate_used, n - 1)
                    nc.scalar.activation(gate[:, n % 2, :, :], bank(u).rearrange("p (a b) -> p a b", a=2), ACT.Exp,
                                         scale=-1.0).then_inc(bank_free[B0[u] % 2], 1)
                    act.wait_ge(bank_free[B0[u] % 2], B0[u] // 2 + 1)
                    act.sem_inc(gate_e, 1)
                    n += 1
                if i == 0:
                    act.wait_ge(M_ready, 3)
                    for t in range(NT):
                        act.dma_start(tok[:, t, :], ctxv[:, t, :]).then_inc(tok_in, 16)
                elif i == 1:
                    for g in range(4):
                        turn_keep(1, g, cxT[:, 2 * g:2 * g + 2, :])
                elif i == 2:
                    norm(F["ctx"], cxT, None)
            for n, u in enumerate(SPAN["wo"]):
                ahead(u)
                if n == 0:
                    highs("ctx", mod[:, 0, 0:8, 1])
            for g in range(4):
                act.wait_ge(x_ready, g + 1)
                nc.scalar.activation(sqv[:, 2 * g:2 * g + 2, :], xT[:, 2 * g:2 * g + 2, :], ACT.Square
                                     ).then_inc(squares, 1)
            for n, u in enumerate(SPAN["cnk"]):
                ahead(u)
                keep(u, cnk[:, 2 * n:2 * n + 2, :])
                if n == 0:
                    act.wait_ge(H_ready, 8)
                    inverse(F["fin1"])
            keep_values("cnv", cnv)
            act.wait_ge(norm_done, 1)
            norm_squares(xT)
            keep_values("chi", hv)
            inverse(F["mix0"])

            act.wait_ge(lb_e, 1)
            nc.scalar.activation(lbc[:, 0, :], lbc[:, 0, :], ACT.Exp).then_inc(lb_e, 1)

            def gates_exp(name, n0):
                for n, u in enumerate(SPAN[name]):
                    ahead(u)
                    act.wait_ge(half_used, H0[u] + NH[u])
                    if n0 + n >= 1:
                        act.wait_ge(f_set, n0 + n)
                    nc.scalar.activation(hgt[:, :, :], bank(u).rearrange("p (a b) -> p a b", a=2), ACT.Exp,
                                         scale=-1.0).then_inc(bank_free[B0[u] % 2], 1)
                    act.wait_ge(bank_free[B0[u] % 2], B0[u] // 2 + 1)
                    act.sem_inc(f_e, 1)

            gates_exp("chf", 0)
            gates_exp("chb", 2)
            act.wait_ge(f_set, 4)
            step(nc.scalar.activation(lg[:, :, :, :], lg[:, :, :, :], ACT.Ln))
            act.sem_inc(f_ln, 1)
            highs("mix0", mod[:, 0, 0:8, 0])

            def ctx_states(d):
                act.wait_ge(f_cum, d + 1)
                for j in range(4):
                    tot = lg[:, d, j, S - 1:S] if d == 0 else lg[:, d, j, 0:1]
                    ins = nc.scalar.activation(kd[:, j, :], lg[:, d, j, :], ACT.Exp, bias=tot, scale=-1.0)
                step(ins)
                act.sem_inc(f_exp, 1)
                for j in range(4):
                    n = 4 * d + j
                    act.wait_ge(kd_turned, n + 1)
                    if n >= 1:
                        act.wait_ge(ctx_state, n)
                    nc.scalar.copy(kdt[:, :, :], psX[:, 0:S].rearrange("p (a b) -> p a b", a=2)).then_inc(kd_kept, 1)
                    act.wait_ge(kd_kept, n + 1)
                    act.wait_ge(ctx_state, n + 1)
                    nc.scalar.copy(sctx[:, d, j, :], psS[:, 0, 0:P]).then_inc(ctx_kept, 1)
                    act.wait_ge(ctx_kept, n + 1)

            for name, dst, sc in (("nq", naq, SCALE), ("nk", nak, None)):
                for n, u in enumerate(SPAN[name]):
                    ahead(u)
                    keep(u, dst[:, 2 * n:2 * n + 2, :], sc)
            ctx_states(0)
            keep_values("nv", nav)
            ctx_states(1)
            for n, u in enumerate(SPAN["hq"]):
                ahead(u)
                act.wait_ge(half_used, H0[u] + NH[u])
                if n >= 1:
                    act.wait_ge(bank_free[(B0[u] - 1) % 2], (B0[u] - 1) // 2 + 1)
                nc.scalar.activation(hgt[:, :, :], bank(u).rearrange("p (a b) -> p a b", a=2), ACT.Exp, scale=-1.0
                                     ).then_inc(silu_e, 1)
            keep_values("hi", hv)
            act.wait_ge(bank_free[(B0[SPAN["hq"][1]]) % 2], (B0[SPAN["hq"][1]]) // 2 + 1)
            gates_exp("hf", 4)
            gates_exp("hb", 6)
            act.wait_ge(f_set, 8)
            step(nc.scalar.activation(lg[:, :, :, :], lg[:, :, :, :], ACT.Ln))
            act.sem_inc(f_ln, 1)
            for n, u in enumerate(SPAN["hg"]):
                ahead(u)
                act.wait_ge(half_used, H0[u] + NH[u])
                if n >= 1:
                    act.wait_ge(bank_free[(B0[u] - 1) % 2], (B0[u] - 1) // 2 + 1)
                nc.scalar.activation(hgt[:, :, :], bank(u).rearrange("p (a b) -> p a b", a=2), ACT.Exp, scale=-1.0
                                     ).then_inc(silu_e, 1)
            for d in range(2):
                act.wait_ge(f_cum, 3 + d)
                nc.scalar.activation(qe[:, :, :], lg[:, d, :, :], ACT.Exp)
                nc.scalar.activation(ke[:, :, :], lg[:, d, :, :], ACT.Exp, scale=-1.0)
                step(nc.scalar.activation(kd[:, :, :], kd[:, :, :], ACT.Exp))
                act.sem_inc(f_exp, 1)
                for j in range(4):
                    n = 4 * d + j
                    act.wait_ge(kd_turned, 8 + n + 1)
                    if n >= 1:
                        act.wait_ge(kv_done, n)
                    nc.scalar.copy(kdt[:, :, :], psX[:, 0:S].rearrange("p (a b) -> p a b", a=2)).then_inc(kd_kept, 1)
                    act.wait_ge(kd_kept, 8 + n + 1)
            act.wait_ge(o_kept, 8)
            nc.scalar.activation(kd[:, :, :], oT[:, :, :], ACT.Square).then_inc(sub_sq, 1)
            act.wait_ge(sub_sum, 2)
            step(nc.scalar.activation(headr2, psS[:, 2:4, :], ACT.Ln, bias=eps[:, 0:1], scale=1.0 / P))
            nc.scalar.activation(headr2, headr2, ACT.Exp, scale=-0.5).then_inc(sub_inv, 1)
            act.wait_ge(sub_inv, 2)

            for h in range(8 + 2):
                if h < 8:
                    if h >= 2:
                        act.wait_ge(turnedP, NT0 + 2 * (h - 2) + 2)
                    else:
                        act.wait_ge(nb_set, 1)
                    exps(NG + h, [(pn[:, h % 2, t, :], psS[:, 2 * (h % 2) + t, :]) for t in range(NT)], False)
                if 1 <= h <= 8:
                    for t in range(2):
                        n = 2 * (h - 1) + t
                        act.wait_ge(turnedP, NT0 + n + 1)
                        if h >= 3 and t == 0:
                            act.wait_ge(yed, NG + h - 2)
                        nc.scalar.copy(pnT[:, n % 4, :], na_x_bank(n)).then_inc(pT_kept, 1)
                        act.wait_ge(pT_kept, NT0 + n + 1)

            split_through(SPAN["evo"][0])
            for u in SPAN["evo"]:
                ahead(u)

            def squares_of_x(i):
                for g in range(4):
                    act.wait_ge(x_ready, XR[i] + g + 1)
                    nc.scalar.activation(sqv[:, 2 * g:2 * g + 2, :], xT[:, 2 * g:2 * g + 2, :], ACT.Square
                                         ).then_inc(squares, 1)
                inverse(F[i])

            XR = {"ffn0": 4, "mix1": 8, "ffn1": 12, "last": 16}

            def conv_centre(src, n, w, b, z):
                for q in range(2):
                    ins = nc.scalar.activation(z[:, q, :], src[:, q, :], ACT.Identity, scale=pcol[:, w + q:w + q + 1],
                                               bias=pcol[:, b + q:b + q + 1])
                    if q == 0:
                        step(ins)
                ins.then_inc(conv_a, 1)
                act.wait_ge(conv_a, n + 1)

            def feed_forward(layer):
                squares_of_x(f"ffn{layer}")
                highs(f"ffn{layer}", mod[:, layer, 24:32, 0])
                n0 = (FT // 2 + 4) * layer
                for i in range(FT // 2):
                    ua, uv = SPAN[f"fa{layer}.{i}"][0], SPAN[f"fv{layer}.{i}"][0]
                    ahead(ua)
                    act.wait_ge(half_used, H0[ua] + NH[ua])
                    if i >= 2:
                        act.wait_ge(G_ready, n0 + i - 1)
                    src = bank(ua).rearrange("p (a b) -> p a b", a=2)
                    nc.scalar.copy(fa[:, i % 2, :, :], src).then_inc(bank_free[B0[ua] % 2], 1)
                    act.wait_ge(bank_free[B0[ua] % 2], B0[ua] // 2 + 1)
                    conv_centre(fa[:, i % 2, :, :], n0 + i, C_FCW + P * layer + FT + 2 * i,
                                C_FCB + P * layer + 2 * i, fz[:, i % 2, :, :])
                    ahead(uv)
                    act.wait_ge(gelu_in, FT // 2 * layer + i + 1)
                    nc.scalar.activation(fz[:, i % 2, :, :], fz[:, i % 2, :, :], ACT.Gelu).then_inc(gelu_out, 1)
                    act.wait_ge(gelu_out, FT // 2 * layer + i + 1)
                for i in range(FT // 2):
                    ahead(SPAN[f"fd{layer}.{i}"][0])

            feed_forward(0)
            nc.scalar.preload_act_table_set(TABLES)
            squares_of_x("mix1")
            highs("mix1", mod[:, 1, 0:8, 0])
            for i in range(4):
                uc, uu, ub = [SPAN[f"od{q}{i}"][0] for q in "cub"]
                n = FT // 2 + i
                ahead(uc)
                act.wait_ge(half_used, H0[uc] + NH[uc])
                if i >= 2:
                    act.wait_ge(G_ready, n - 1)
                nc.scalar.copy(fa[:, i % 2, :, :], bank(uc).rearrange("p (a b) -> p a b", a=2)
                               ).then_inc(bank_free[B0[uc] % 2], 1)
                act.wait_ge(bank_free[B0[uc] % 2], B0[uc] // 2 + 1)
                act.sem_inc(c_kept, 1)
                ahead(uu)
                act.wait_ge(cu_set, i + 1)
                conv_centre(fa[:, i % 2, :, :], n, C_ODW + 8 + 2 * i, C_ODB + 2 * i, fz[:, i % 2, :, :])
                ahead(ub)
            for u in SPAN["odo"]:
                ahead(u)
            feed_forward(1)
            nc.scalar.preload_act_table_set(TABLES)
            squares_of_x("last")

            for t in range(NT):
                for k4 in range(2):
                    n = 2 * t + k4
                    act.wait_ge(out_turned, n + 1)
                    nc.scalar.copy(tok[:, t, k4 * 512:(k4 + 1) * 512], token_bank(n)).then_inc(out_kept, 1)
                    act.wait_ge(out_kept, n + 1)

        @block.vector
        def _(dve):
            steps = [0]
            half_at = [0]
            V = nc.vector

            def step(ins):
                steps[0] += 1
                ins.then_inc(dves, 1)
                dve.wait_ge(dves, steps[0])

            def then(ins, s, n):
                ins.then_inc(s, 1)
                dve.wait_ge(s, n)

            def split_through(u):
                while half_at[0] < H0[u] + NH[u]:
                    h = half_at[0]
                    v = next(w for w in split_order if H0[w] <= h < H0[w] + NH[w])
                    dve.wait_ge(hi_split, h + 1)
                    src, _ = raw_half(v, h - H0[v])
                    V.tensor_tensor(ring_half(wlo, v, h - H0[v]), src, ring_half(whi, v, h - H0[v]).bitcast(F32),
                                    ALU.subtract).then_inc(lo_split, 1)
                    half_at[0] += 1

            def ahead(u):
                if u in after:
                    split_through(after[u])

            def split_value(v, hi, lo, s, n):
                step(V.tensor_copy(hi, v))
                then(V.tensor_tensor(lo, v, hi.bitcast(F32), ALU.subtract), s, n)

            V.memset(eps[:, 0:1], EPS)
            V.memset(eps[:, 1:2], SUBLN_EPS)
            then(V.memset(ones[:, :], 1.0), ones_set, 1)
            split_through(0)
            dve.wait_ge(small_mm, 1)
            for i, rows in enumerate((125, 96, 88, 88)):
                step(V.tensor_copy(pcol[:, i * P:i * P + rows], psX[:, i * P:i * P + rows]))
            dve.sem_inc(small_ev, 1)
            dve.sem_inc(c_exp, 1)

            ada_at = [0]

            def keep_ada(limit):
                while ada_at[0] < limit:
                    n = ada_at[0]
                    layer, s, who = ACCS[n]
                    c = C_ADAB + 48 * layer + 8 * s
                    dve.wait_ge(acc_summed, n + 1)
                    then(V.tensor_tensor(mod[:, layer, 8 * s:8 * s + 8, who], ada_bank(n), pcol[:, c:c + 8], ALU.add),
                         ada_kept, n + 1)
                    ada_at[0] += 1

            def normed(i, src, g0, shift=None):
                dve.wait_ge(rms_inv, F[i] + 1)
                n0 = KT * (H_COUNT[i] - 1)
                for k in range(KT + 1):
                    if k < KT:
                        V.scalar_tensor_tensor(vt[:, k % 2, :], src[:, k, :], g0[:, k:k + 1], rn[:, 1, :],
                                               ALU.mult, ALU.mult).then_inc(v_set, 1)
                    if k:
                        m = k - 1
                        dve.wait_ge(vhi_set, n0 + m + 1)
                        if shift is None:
                            ins = V.tensor_tensor(Hlo[:, m, :], vt[:, m % 2, :], Hhi[:, m, :].bitcast(F32),
                                                  ALU.subtract)
                        else:
                            ins = V.scalar_tensor_tensor(Hlo[:, m, :], vt[:, m % 2, :], shift[:, m:m + 1],
                                                         Hhi[:, m, :].bitcast(F32), ALU.add, ALU.subtract)
                        if m % 2:
                            then(ins, H_ready, 4 * (H_COUNT[i] - 1) + m // 2 + 1)
                        else:
                            step(ins)

            dve.wait_ge(c_exp, 2)
            step(V.tensor_scalar(cse[:, :], cse[:, :], 1.0, None, ALU.add))
            step(V.reciprocal(cse[:, :], cse[:, :]))
            for i in range(2):
                step(V.tensor_tensor(cs[:, :, i], cse[:, 8 * i:8 * i + 8], pcol[:, C_C + 8 * i:C_C + 8 * i + 8],
                                     ALU.mult))
            dve.sem_inc(c_silu, 1)

            normed("h1", xT, pcol[:, C_NG:C_NG + 8])
            for name in ("qa", "ka", "va", "qb", "kvb", "qc", "kc", "vc"):
                for u in SPAN[name]:
                    ahead(u)
                    if u == 0:
                        dve.wait_ge(consts, 1)
                        step(V.tensor_copy(dist[:, :], distI[:, :]))
                        step(V.tensor_copy(distw[:, :], distI[:, :]))
                        step(V.memset(cmask[:, :], 0.0))
                        dve.sem_inc(consts, 1)
                        dve.wait_ge(misc_in, 16 * MISC)
                        then(V.tensor_tensor(lamp[0:HD, 0:2], lam4[:, 0:4:2], lam4[:, 1:4:2], ALU.mult), small_ev, 2)
                if name == "ka":
                    dve.wait_ge(small_ex, 1)
                    step(V.tensor_tensor(lamp[:, 4:5], lamp[:, 3:4], lamp[:, 2:3], ALU.subtract))
                    step(V.tensor_scalar(lamp[:, 5:6], lamp[:, 4:5], -LAM_INIT, None, ALU.add))
                    step(V.tensor_scalar(lamp[:, 6:7], pcol[:, C_SUB:C_SUB + 1], 1.0 - LAM_INIT, None, ALU.mult))
                    for t in range(2):
                        step(V.tensor_copy(sinkb[:, :, :, t], smallr[:, 8:16].rearrange("p (i j) -> p j i", i=2)))
            u = SPAN["fc"][0]
            ahead(u)
            dve.wait_ge(half_used, H0[u] + NH[u])
            then(V.tensor_scalar(fcw[:, 0, :], bank(u)[0:8, 0:S], bfc[:, 0:1], None, ALU.add),
                 bank_free[B0[u] % 2], B0[u] // 2 + 1)
            then(V.scalar_tensor_tensor(fcw[:, 1, :], fcw[:, 0, :], -1.0, fcw[:, 0, :], ALU.mult, ALU.max),
                 forget_a, 1)
            step(V.tensor_scalar(fcw[:, 0, :], fcw[:, 0, :], 0.0, None, ALU.min))
            dve.wait_ge(forget_a, 2)
            step(V.tensor_tensor(fcw[:, 3, :], fcw[:, 3, :], fcw[:, 0, :], ALU.subtract))
            then(V.tensor_tensor_scan(negc[:, :], ones[0:8, 0:S], fcw[:, 3, :], 0.0, ALU.mult, ALU.add), forget, 1)
            

            def silu(u, n, dst, tmp):
                ahead(u)
                dve.wait_ge(silu_e, n + 1)
                step(V.tensor_scalar(tmp, tmp, 1.0, None, ALU.add))
                step(V.reciprocal(tmp, tmp))
                then(V.tensor_tensor(dst, tmp, bank(u).rearrange("p (a b) -> p a b", a=2), ALU.mult),
                     bank_free[B0[u] % 2], B0[u] // 2 + 1)

            n = 0
            for name in ("ga", "gb", "gc"):
                for u in SPAN[name]:
                    silu(u, n, sg[:, 2 * n:2 * n + 2, :], e2[:, :, :])
                    n += 1
                if name == "gb":
                    keep_ada(2)

            SLOPE_A = [2.0 ** (-8.0 * (h + 1) / 4) for h in range(4)]
            SLOPE_B = [2.0 ** (-8.0 * (h + 1) / 8) for h in range(8)]
            def bias_max(g):
                br, j = GROUPS[g]
                st = 3 * (g % 2)
                dve.wait_ge(scored, g + 1)
                if g == 4:
                    dve.wait_ge(consts, 3)
                if g == 0:
                    dve.wait_ge(consts, 3)
                for i in range(2):
                    o = psS[:, 2 * (g % 2) + i, 0:384]
                    if br == "A":
                        step(V.scalar_tensor_tensor(o, dist[:, :], -SLOPE_A[j], o, ALU.mult, ALU.add))
                    elif br == "B":
                        step(V.scalar_tensor_tensor(o, distw[:, :], -SLOPE_B[j + 4 * i], o, ALU.mult, ALU.add))
                    else:
                        step(V.tensor_tensor(o, o, cmask[:, :], ALU.add))
                for t in range(2):
                    ins = V.tensor_reduce(stat[:, st, t:4:2], psS[:, 2 * (g % 2):2 * (g % 2) + 2, COLS[t][0]:COLS[t][1]],
                                          AX.X, ALU.max, negate=(br != "B"))
                    if t == 0 or br == "B":
                        step(ins)
                if br == "B":
                    sk = sinkb[:, j, :, :].rearrange("p i t -> p (i t)")
                    step(V.tensor_tensor(stat[:, st, :], stat[:, st, :], sk, ALU.max))
                    step(V.tensor_scalar(stat[:, st, :], stat[:, st, :], -1.0, None, ALU.mult))
                    ins = V.tensor_tensor(stat[:, st + 2, :], sk, stat[:, st, :], ALU.add)
                then(ins, biased, g + 1)

            def normalise(g):
                br, j = GROUPS[g]
                st = 3 * (g % 2)
                dve.wait_ge(exped, g + 1)
                if br == "B":
                    step(V.tensor_tensor(stat[:, st + 1, :], stat[:, st + 1, :], stat[:, st + 2, :], ALU.add))
                step(V.reciprocal(stat[:, st + 1, :], stat[:, st + 1, :]))
                if br == "A":
                    step(V.tensor_scalar(stat[:, st + 1, 2:4], stat[:, st + 1, 2:4], lamp[:, 5:6], None, ALU.mult))
                for t in range(2):
                    a, b = COLS[t]
                    for i in range(2):
                        v = pr[:, g % 2, i, a:b]
                        if br == "A" and i == 1:
                            ins = V.scalar_tensor_tensor(pr[:, g % 2, 0, a:b], v, stat[:, st + 1, 2 + t:3 + t],
                                                         pr[:, g % 2, 0, a:b], ALU.mult, ALU.add)
                        else:
                            ins = V.tensor_scalar(v, v, stat[:, st + 1, 2 * i + t:2 * i + t + 1], None, ALU.mult)
                        if (t, i) != (1, 1):
                            step(ins)
                then(ins, probs, g + 1)

            def gate_y(g):
                dve.wait_ge(yed, g + 1)
                then(V.tensor_tensor(sg[:, g, :], y_bank(g), sg[:, g, :], ALU.mult), y_kept, g - 4 + 1)

            for g in range(NG + 3):
                if g < NG:
                    bias_max(g)
                if g >= 7:
                    gate_y(g - 3)
                if 1 <= g <= NG:
                    normalise(g - 1)
                keep_ada(2 + 2 * (g >= 2) + (g >= 4) + (g >= 7) + (g >= 10))
            for b in (1, 2):
                dve.wait_ge(M_high, b)
                then(V.tensor_tensor(Mlo[:, 4 * b:4 * b + 4, :], sg[:, 4 * b:4 * b + 4, :],
                                     Mhi[:, 4 * b:4 * b + 4, :].bitcast(F32), ALU.subtract), M_ready, b)
            split_through(SPAN["gm_b0"][0])
            dve.wait_ge(sub_inv, 1)
            for i in range(2):
                v = yA[:, 2 * i:2 * i + 2, :]
                step(V.scalar_tensor_tensor(v, v, lamp[:, 6:7], headr[:, i, :].rearrange("p (a b) -> p a b", a=2),
                                            ALU.mult, ALU.mult))
                step(V.tensor_tensor(v, v, sg[:, 2 * i:2 * i + 2, :], ALU.mult))
            step(V.tensor_copy(Mhi[:, 0:4, :], yA[:, :, :]))
            then(V.tensor_tensor(Mlo[:, 0:4, :], yA[:, :, :], Mhi[:, 0:4, :].bitcast(F32), ALU.subtract), M_ready, 3)

            n = 0
            for i in range(4):
                for b, br in enumerate("bca"):
                    ug, u = SPAN[f"gm_{br}{i}"][0], SPAN[f"up_{br}{i}"][0]
                    ahead(ug)
                    ahead(u)
                    dve.wait_ge(gate_e, n + 1)
                    v = gate[:, n % 2, :, :]
                    step(V.tensor_scalar(v, v, 1.0, None, ALU.add))
                    step(V.reciprocal(v, v))
                    dve.wait_ge(half_used, H0[u] + NH[u])
                    dst = merged if b == 0 else mt
                    then(V.tensor_tensor(dst[:, :, :], v, bank(u).rearrange("p (a b) -> p a b", a=2), ALU.mult),
                         bank_free[B0[u] % 2], B0[u] // 2 + 1)
                    dve.sem_inc(gate_used, 1)
                    if b:
                        step(V.tensor_tensor(merged[:, :, :], merged[:, :, :], mt[:, :, :], ALU.add))
                    n += 1
                split_value(merged[:, :, :], Whi[:, 2 * i:2 * i + 2, :], Wlo[:, 2 * i:2 * i + 2, :],
                            merge_ready, i + 1)
                if i == 2:
                    keep_ada(8)
                    for m, (layer, s, who, w) in enumerate(((0, 1, 1, C_MIX), (0, 1, 0, C_MIX), (0, 4, 0, C_FFN))):
                        step(V.scalar_tensor_tensor(cm[:, m, :], mod[:, layer, 8 * s:8 * s + 8, who], 1.0,
                                                    pcol[:, w:w + 8], ALU.add, ALU.mult))
            for n, u in enumerate(SPAN["wo"]):
                ahead(u)
                if n == 0:
                    u = SPAN["gm_a3"][0]
                    dve.wait_ge(half_used, H0[u] + NH[u])
                    normed("ctx", cxT, cm[:, 0, :], mod[:, 0, 0:8, 1])
                    u = SPAN["wo"][0]
                dve.wait_ge(half_used, H0[u] + NH[u])
                v = xT[:, 2 * n:2 * n + 2, :]
                then(V.tensor_tensor(v, v, bank(u).rearrange("p (a b) -> p a b", a=2), ALU.add),
                     bank_free[B0[u] % 2], B0[u] // 2 + 1)
                dve.sem_inc(x_ready, 1)

            def renorm(i, gain, n):
                dve.wait_ge(rms_inv, F[i] + 1)
                for k in range(KT):
                    step(V.scalar_tensor_tensor(xT[:, k, :], xT[:, k, :], pcol[:, gain + k:gain + k + 1], rn[:, 1, :],
                                                ALU.mult, ALU.mult))
                dve.sem_inc(norm_done, 1)

            for name in ("cnk", "cnv", "chi"):
                for n, u in enumerate(SPAN[name]):
                    ahead(u)
                    if (name, n) == ("cnk", 1):
                        renorm("fin1", C_FG, 1)
                        step(V.tensor_tensor(lbc[:, 0, :], pcol[:, C_LB + 8:C_LB + 16], pcol[:, C_LB:C_LB + 8],
                                             ALU.subtract))
                        dve.sem_inc(lb_e, 1)
            dve.wait_ge(lb_e, 2)
            step(V.tensor_scalar(lbc[:, 0, :], lbc[:, 0, :], 1.0, None, ALU.add))
            step(V.reciprocal(lbc[:, 1, :], lbc[:, 0, :]))
            step(V.tensor_scalar(lbc[:, 2, :], lbc[:, 1, :], -1.0, 1.0, ALU.mult, ALU.add))

            def forget_gates(name, d, n0):
                for n, u in enumerate(SPAN[name]):
                    ahead(u)
                    dve.wait_ge(f_e, n0 + n + 1)
                    v = hgt[:, :, :]
                    step(V.tensor_scalar(v, v, 1.0, None, ALU.add))
                    step(V.reciprocal(v, v))
                    for q in range(2):
                        c = 4 * d + 2 * n + q
                        step(V.tensor_scalar(lg[:, d, 2 * n + q, :], hgt[:, q, :], lbc[:, 2, c:c + 1], lbc[:, 1, c:c + 1],
                                             ALU.mult, ALU.add))
                    then(V.tensor_scalar(kk[:, d, 2 * n:2 * n + 2, :], lg[:, d, 2 * n:2 * n + 2, :], -1.0, 1.0,
                                         ALU.mult, ALU.add), f_set, n0 + n + 1)

            forget_gates("chf", 0, 0)
            forget_gates("chb", 1, 2)
            dve.wait_ge(f_ln, 1)
            u = SPAN["chb"][1]
            dve.wait_ge(half_used, H0[u] + NH[u])
            normed("mix0", xT, cm[:, 1, :], mod[:, 0, 0:8, 0])

            def ctx_states(d):
                dve.wait_ge(f_ln, 1)
                if d:
                    dve.wait_ge(ctx_kept, 4)
                for j in range(4):
                    r = slice(None, None, -1) if d else slice(None)
                    ins = V.tensor_tensor_scan(lg[:, d, j, r], ones[:, 0:S], lg[:, d, j, r], 0.0, ALU.mult, ALU.add)
                then(ins, f_cum, d + 1)
                dve.wait_ge(f_exp, d + 1)
                then(V.tensor_tensor(kd[:, :, :], kd[:, :, :], kk[:, d, :, :], ALU.mult), f_mul, d + 1)

            for name in ("nq", "nk", "nv"):
                for u in SPAN[name]:
                    ahead(u)
                if name != "nq":
                    ctx_states(int(name == "nv"))
            for n, u in enumerate(SPAN["hq"]):
                silu(u, 6 + n, hq[:, 2 * n:2 * n + 2, :], hgt[:, :, :])
            for u in SPAN["hi"]:
                ahead(u)
            forget_gates("hf", 0, 4)
            forget_gates("hb", 1, 6)
            for n, u in enumerate(SPAN["hg"]):
                silu(u, 8 + n, sgh[:, 2 * n:2 * n + 2, :], hgt[:, :, :])
            dve.sem_inc(rpad_set, 1)
            dve.wait_ge(f_ln, 2)
            step(V.memset(reset[:, :], 1.0))
            step(V.memset(reset[:, :].rearrange("p (c t) -> p c t", t=CH)[:, :, 0:1], 0.0))
            for t in range(NT):
                step(V.memset(attm[:, t, :], 0.0))
            step(V.memset(vbd[:, :, :, :], 0.0))
            dve.wait_ge(consts, 4)
            for d in range(2):
                r = slice(None, None, -1) if d else slice(None)
                if d:
                    dve.wait_ge(o_done, 4)
                    for t in range(NT):
                        step(V.memset(attm[:, t, :], 0.0))
                for j in range(4):
                    ins = V.tensor_tensor_scan(lg[:, d, j, r], reset[:, :], lg[:, d, j, r], 0.0, ALU.mult, ALU.add)
                step(ins)
                b3 = lg[:, d, :, :].rearrange("p h (c t) -> p (h c) t", t=CH)
                tot = (b3[:, :, 0:1] if d else b3[:, :, CH - 1:CH]).to_broadcast([P, 4 * NCH, CH])
                then(V.tensor_tensor(kd[:, :, :].rearrange("p h (c t) -> p (h c) t", t=CH), tot, b3, ALU.subtract),
                     f_cum, 3 + d)
                dve.wait_ge(f_exp, 3 + d)
                q3 = qe[:, :, :].rearrange("p h (c t) -> p (h c) t", t=CH)
                step(V.tensor_copy(dec[:, :].rearrange("p (c o) -> p c o", o=1), q3[:, :, 0:1] if d else q3[:, :, CH - 1:CH]))
                step(V.tensor_tensor(qe[:, :, :], qe[:, :, :], hq[:, :, :], ALU.mult))
                step(V.tensor_tensor(ke[:, :, :], ke[:, :, :], kk[:, d, :, :], ALU.mult))
                then(V.tensor_tensor(kd[:, :, :], kd[:, :, :], kk[:, d, :, :], ALU.mult), f_mul, 3 + d)
                for j in range(4):
                    n = 4 * d + j
                    if n >= 1:
                        dve.wait_ge(kv_done, n)
                    for c in range(4):
                        a = slice(c * CH, (c + 1) * CH)
                        ins = V.tensor_copy(vbd[a, :, c, :], hv[a, :, j * P:(j + 1) * P])
                    then(ins, vbd_set, n + 1)
                    dve.wait_ge(att_done, n + 1)
                    if n >= 1:
                        dve.wait_ge(o_done, n)
                    for t in range(NT):
                        src = attP[:, t * P:(t + 1) * P]
                        ins = V.copy_predicated(attm[:, t, :], smask[:, d, :].bitcast(U32), src)
                        if t == 0:
                            step(ins)
                    then(ins, att_set, n + 1)
                    first = NCH - 1 if d else 0
                    step(V.tensor_copy(sq[:, first, :], sctx[:, d, j, :]))
                    dve.wait_ge(kv_done, n + 1)
                    order = list(range(NCH - 1, -1, -1)) if d else list(range(NCH))
                    for a, b in zip(order[:-1], order[1:]):
                        step(V.scalar_tensor_tensor(sq[:, b, :], sq[:, a, :], dec[:, NCH * j + a:NCH * j + a + 1],
                                                    psS[:, a // 4, (a % 4) * P:(a % 4 + 1) * P], ALU.mult, ALU.add))
                    dve.sem_inc(st_set, 1)
                    dve.wait_ge(o_done, n + 1)
                    if d == 0:
                        ins = V.tensor_copy(oT[:, j, :], psY[:, 0:S])
                    else:
                        ins = V.tensor_tensor(oT[:, j, :], oT[:, j, :], psY[:, 0:S], ALU.add)
                    then(ins, o_kept, n + 1)
            dve.wait_ge(sub_inv, 2)
            for j in range(4):
                step(V.scalar_tensor_tensor(oT[:, j, :], oT[:, j, :], pcol[:, C_HGN + j:C_HGN + j + 1],
                                            headr2[:, j // 2, (j % 2) * S:(j % 2 + 1) * S], ALU.mult, ALU.mult))
            step(V.tensor_tensor(oT[:, :, :], oT[:, :, :], sgh[:, :, :], ALU.mult))
            step(V.tensor_copy(Yhi[:, 4:8, :], oT[:, :, :]))
            then(V.tensor_tensor(Ylo[:, 4:8, :], oT[:, :, :], Yhi[:, 4:8, :].bitcast(F32), ALU.subtract),
                 M_ready, 4)
            dve.sem_inc(core_done, 1)
            dve.wait_ge(nb_set, 1)
            for h in range(8 + 3):
                if h < 8:
                    st = 3 * (h % 2)
                    dve.wait_ge(scored, NG + h + 1)
                    for t in range(NT):
                        o = psS[:, 2 * (h % 2) + t, 0:S].rearrange("p (a b) -> p a b", a=4)
                        step(V.tensor_tensor(o, o, nb_head(h)[:, 2 - 2 * t:6 - 2 * t, ::-1], ALU.add))
                    then(V.tensor_reduce(stat[:, st, 0:2], psS[:, 2 * (h % 2):2 * (h % 2) + 2, :], AX.X, ALU.max,
                                         negate=True), biased, NG + h + 1)
                if h >= 3 and h % 2 == 0:
                    j = (h - 4) // 2
                    dve.wait_ge(yed, NG + 2 * j + 2)
                    src = na_y_bank(j)
                    then(V.tensor_copy(vt[:, 1, :], src), y_kept, 8 + j + 1)
                    split_value(vt[:, 1, :], Yhi[:, j, :], Ylo[:, j, :], M_ready, 4 + j + 1)
                if h < 8:
                    dve.wait_ge(exped, NG + h + 1)
                    step(V.reciprocal(stat[:, st + 1, 0:2], stat[:, st + 1, 0:2]))
                    for t in range(NT):
                        v = pn[:, h % 2, t, :]
                        ins = V.tensor_scalar(v, v, stat[:, st + 1, t:t + 1], None, ALU.mult)
                        if t == 0:
                            step(ins)
                    then(ins, probs, NG + h + 1)
            def add_gated(u, n, layer, s):
                dve.wait_ge(half_used, H0[u] + NH[u])
                for q in range(2):
                    k = 2 * n + q
                    ins = V.scalar_tensor_tensor(xT[:, k, :], bank(u)[:, q * S:(q + 1) * S],
                                                 mod[:, layer, 8 * s + k, 0:1], xT[:, k, :], ALU.mult, ALU.add)
                    if q == 0:
                        step(ins)
                then(ins, bank_free[B0[u] % 2], B0[u] // 2 + 1)
                dve.sem_inc(x_ready, 1)

            split_through(SPAN["evo"][0])
            for n, u in enumerate(SPAN["evo"]):
                ahead(u)
                add_gated(u, n, 0, 2)

            def conv_sides(z, src, w, n):
                dve.wait_ge(conv_a, n + 1)
                for q in range(2):
                    step(V.scalar_tensor_tensor(z[:, q, 1:S], src[:, q, 0:S - 1], pcol[:, w[0] + q:w[0] + q + 1],
                                                z[:, q, 1:S], ALU.mult, ALU.add))
                    ins = V.scalar_tensor_tensor(z[:, q, 0:S - 1], src[:, q, 1:S], pcol[:, w[1] + q:w[1] + q + 1],
                                                 z[:, q, 0:S - 1], ALU.mult, ALU.add)
                    if q == 0:
                        step(ins)
                return ins

            def gains(m, s, w):
                step(V.scalar_tensor_tensor(cm[:, m, :], mod[:, 1, 8 * s:8 * s + 8, 0], 1.0, pcol[:, w:w + 8],
                                            ALU.add, ALU.mult))

            def feed_forward(layer):
                normed(f"ffn{layer}", xT, cm[:, 2 + 2 * layer, :], mod[:, layer, 24:32, 0])
                n0 = (FT // 2 + 4) * layer
                for i in range(FT // 2):
                    ua, uv = SPAN[f"fa{layer}.{i}"][0], SPAN[f"fv{layer}.{i}"][0]
                    ahead(ua)
                    z, src = fz[:, i % 2, :, :], fa[:, i % 2, :, :]
                    c = C_FCW + P * layer + 2 * i
                    then(conv_sides(z, src, (c, c + 2 * FT), n0 + i), gelu_in, FT // 2 * layer + i + 1)
                    ahead(uv)
                    dve.wait_ge(gelu_out, FT // 2 * layer + i + 1)
                    dve.wait_ge(half_used, H0[uv] + NH[uv])
                    then(V.tensor_tensor(z, z, bank(uv).rearrange("p (a b) -> p a b", a=2), ALU.mult),
                         bank_free[B0[uv] % 2], B0[uv] // 2 + 1)
                    split_value(z, Ghi[:, 2 * i:2 * i + 2, :], Glo[:, 2 * i:2 * i + 2, :], G_ready, n0 + i + 1)
                    if layer == 0 and i in (6, 10):
                        keep_ada({6: 9, 10: 10}[i])
                for i in range(FT // 2):
                    ahead(SPAN[f"fd{layer}.{i}"][0])
                    if layer == 0 and i == 6:
                        keep_ada(11)
                        gains(3, 1, C_MIX + 8)
                u = SPAN[f"fd{layer}.{FT // 2 - 1}"][0]
                for k in range(KT):
                    if k == 6:
                        dve.wait_ge(half_used, H0[u] + NH[u])
                    elif k % 2 == 0:
                        dve.wait_ge(down_part, 3 * layer + k // 2 + 1)
                    step(V.scalar_tensor_tensor(xT[:, k, :], psS[:, k // 2, (k % 2) * S:(k % 2 + 1) * S],
                                                mod[:, layer, 40 + k, 0:1], xT[:, k, :], ALU.mult, ALU.add))
                    if k % 2:
                        dve.sem_inc(x_ready, 1)

            feed_forward(0)
            normed("mix1", xT, cm[:, 3, :], mod[:, 1, 0:8, 0])
            for i in range(4):
                uc, uu, ub = [SPAN[f"od{q}{i}"][0] for q in "cub"]
                n = FT // 2 + i
                z, src = fz[:, i % 2, :, :], fa[:, i % 2, :, :]
                ahead(uc)
                ahead(uu)
                dve.wait_ge(c_kept, i + 1)
                dve.wait_ge(half_used, H0[uu] + NH[uu])
                then(V.tensor_tensor(src, src, bank(uu).rearrange("p (a b) -> p a b", a=2), ALU.mult),
                     bank_free[B0[uu] % 2], B0[uu] // 2 + 1)
                dve.sem_inc(cu_set, 1)
                ahead(ub)
                step(conv_sides(z, src, (C_ODW + 2 * i, C_ODW + 16 + 2 * i), n))
                dve.wait_ge(half_used, H0[ub] + NH[ub])
                then(V.tensor_tensor(z, z, bank(ub).rearrange("p (a b) -> p a b", a=2), ALU.mult),
                     bank_free[B0[ub] % 2], B0[ub] // 2 + 1)
                split_value(z, Ghi[:, 2 * i:2 * i + 2, :], Glo[:, 2 * i:2 * i + 2, :], G_ready, n + 1)
                if i >= 1:
                    keep_ada(11 + i)
            gains(4, 4, C_FFN + 8)
            for n, u in enumerate(SPAN["odo"]):
                ahead(u)
                add_gated(u, n, 1, 2)
            feed_forward(1)
            renorm("last", C_FN, 2)

        @block.gpsimd
        def _(pool):
            G = nc.gpsimd
            steps = [0]

            def step(ins):
                steps[0] += 1
                ins.then_inc(pools, 1)
                pool.wait_ge(pools, steps[0])

            step(G.memset(ident[:, :], 0.0))
            step(G.affine_select(out=ident[:, :], in_=ident[:, :], compare_op=ALU.not_equal, fill=1.0, base=0,
                                 pattern=[[-1, P]], channel_multiplier=1))
            pool.sem_inc(ident_set, 1)
            step(G.memset(sel[:, :, :], 0.0))
            step(G.affine_select(out=sel[:, :, :], in_=sel[:, :, :], compare_op=ALU.not_equal, fill=1.0, base=0,
                                 pattern=[[-1, 8], [0, P]], channel_multiplier=1))
            step(G.iota(distI[:, 0:P], pattern=[[-1, P]], base=0, channel_multiplier=1))
            step(G.iota(distI[:, P:384], pattern=[[-1, S]], base=P, channel_multiplier=1))
            pool.sem_inc(consts, 1)
            pool.wait_ge(consts, 2)
            for tile_, fill in ((dist, FAR), (distw, FAR), (cmask, -FAR)):
                for a, b, base in ((0, P, 0), (P, 384, P)):
                    step(G.affine_select(out=tile_[:, a:b], in_=tile_[:, a:b], compare_op=ALU.is_ge, fill=fill,
                                         base=base, pattern=[[-1, b - a]], channel_multiplier=1))
            step(G.affine_select(out=distw[:, P:384], in_=distw[:, P:384], compare_op=ALU.is_ge, fill=FAR,
                                 base=-1, pattern=[[1, S]], channel_multiplier=-1))
            pool.sem_inc(consts, 1)

            def ada(n0, buf, acc, tmp):
                secs = [(0, s) for s in range(6)] if n0 == 0 else [(1, s) for s in range(6)]
                chunks = [(l, s, k) for l, s in secs for k in range(KT)]
                c0 = 0 if n0 == 0 else 6 * KT

                def load(c):
                    l, s, k = chunks[c]
                    pool.dma_start(buf[:, (c0 + c) % AW, :], ada_w_2[l, k * P:(k + 1) * P, s * D:(s + 1) * D]
                                   ).then_inc(adaw_landed[(c0 + c) % AW], 16)
                for c in range(AW):
                    load(c)
                n = n0
                for c, (l, s, k) in enumerate(chunks):
                    pool.wait_ge(adaw_landed[(c0 + c) % AW], 16 * ((c0 + c) // AW + 1))
                    w = buf[:, (c0 + c) % AW, :]
                    whos = [who for a, b, who in ACCS if (a, b) == (l, s)]
                    for who in whos:
                        a = acc[:, (n + who) % 2, :]
                        sc = cs[:, k, who:who + 1]
                        if k == 0:
                            if n + who - n0 >= 2:
                                pool.wait_ge(acc_summed, n + who - 1)
                            step(G.tensor_scalar(a, w, sc, 1.0, ALU.mult, ALU.mult))
                        else:
                            step(G.tensor_scalar(tmp[:, :], w, sc, 1.0, ALU.mult, ALU.mult))
                            step(G.tensor_tensor(a, a, tmp[:, :], ALU.add))
                    if k == KT - 1:
                        pool.sem_inc(acc_ready, len(whos))
                        n += len(whos)
                    if c + AW < len(chunks):
                        load(c + AW)

            pool.wait_ge(c_silu, 1)
            ada(0, adaw0, acc0, adat0)
            pool.wait_ge(norm_done, 1)
            step(G.memset(smask[:, :, :], 1.0))
            step(G.affine_select(out=smask[:, 0, :], in_=smask[:, 0, :], compare_op=ALU.is_ge, fill=0.0, base=0,
                                 pattern=[[1, P]], channel_multiplier=-1))
            step(G.affine_select(out=smask[:, 0, :], in_=smask[:, 0, :], compare_op=ALU.is_ge, fill=0.0, base=0,
                                 pattern=[[-CH, 4], [0, CH]], channel_multiplier=1))
            step(G.affine_select(out=smask[:, 1, :], in_=smask[:, 1, :], compare_op=ALU.is_ge, fill=0.0, base=0,
                                 pattern=[[-1, P]], channel_multiplier=1))
            step(G.affine_select(out=smask[:, 1, :], in_=smask[:, 1, :], compare_op=ALU.is_ge, fill=0.0, base=CH - 1,
                                 pattern=[[CH, 4], [0, CH]], channel_multiplier=-1))
            pool.sem_inc(consts, 1)
            pool.wait_ge(rpad_set, 1)
            step(G.memset(rpad, 0.0))
            pool.dma_start(rpad[:, 48:79], na_rpb_2.rearrange("a h r c -> (a h r) c")).then_inc(scr_out, 16)
            pool.wait_ge(scr_out, 16)
            step(G.memset(rrev, 0.0))
            step(G.tensor_copy(rrev[:, 0:127], rpad[:, 126::-1]))
            pool.dma_start(rscr, rrev).then_inc(scr_out, 16)
            pool.wait_ge(scr_out, 32)
            for half_ in range(2):
                for h in range(8):
                    src = bass.AP(rscr.tensor, (h * 15 + 5 - half_) * P, [[1, HD], [P, 6], [1, HD]])
                    pool.dma_start(nb_head(h)[half_ * HD:(half_ + 1) * HD, :, :], src).then_inc(nb_in, 16)
            pool.wait_ge(nb_in, 16 * 16)
            for half_ in range(2):
                a = slice(half_ * HD, (half_ + 1) * HD)
                for nb in (nbA, nbB):
                    v = nb[a, :, :, :].rearrange("p h j c -> p (h j) c")
                    m = v.shape[1]
                    step(G.affine_select(out=v[:, :, 0:48], in_=v[:, :, 0:48], compare_op=ALU.is_ge, fill=-FAR,
                                         base=7 - 63, pattern=[[0, m], [1, 48]], channel_multiplier=1))
                    step(G.affine_select(out=v[:, :, 16:64], in_=v[:, :, 16:64], compare_op=ALU.is_ge, fill=-FAR,
                                         base=63 + 8 - 16, pattern=[[0, m], [-1, 48]], channel_multiplier=-1))
            pool.sem_inc(nb_set, 1)
            pool.wait_ge(core_done, 1)
            ada(8, adaw1, acc1, adat1)


_INS = ['x', 'norm_gain', 'w_in', 'b_forget', 'lambda_q1', 'lambda_k1', 'lambda_q2', 'lambda_k2', 'subln_gain',
        'sinks', 'w_up_a', 'w_up_b', 'w_up_c', 'w_o', 'final_gain', 'c_2', 'ctx_2', 'c_ctx_2', 'ada_w_2', 'ada_b_2',
        'norm_mix_w_2', 'norm_ffn_w_2', 'ev_w_in_2', 'ev_w_out_2', 'na_rpb_2', 'hg_lb_logits_2', 'hg_norm_w_2',
        'od_w_in_2', 'od_conv_w_2', 'od_conv_b_2', 'od_w_out_2', 'ffn_w_up_2', 'ffn_conv_w_2', 'ffn_conv_b_2',
        'ffn_w_down_2', 'final_norm_w_2']
_OUTS = [((1, 256, 1024), 'float32')]


def kernel(**inputs):
    import numpy as _np
    import concourse.bacc as _bacc
    from concourse import mybir as _mybir
    from concourse.bass_utils import run_bass_kernel_spmd as _run

    nc = _bacc.Bacc("TRN2", target_bir_lowering=False, num_devices=1)
    arrays, args = {}, []
    for name in _INS:
        a = _np.ascontiguousarray(inputs[name])
        arrays[f"in_{name}_dram"] = a
        args.append(nc.dram_tensor(f"in_{name}_dram", a.shape, _mybir.dt.from_np(a.dtype), kind="ExternalInput").ap())
    for i, (shape, dtype) in enumerate(_OUTS):
        dt = _mybir.dt.from_np(_np.dtype(dtype))
        args.append(nc.dram_tensor(f"out_{i}_dram", shape, dt, kind="ExternalOutput").ap())
    build(nc, *args)
    r = _run(nc, [arrays], core_ids=[0])
    return r.results[0]["out_0_dram"]
```

```python
from contextlib import ExitStack
import math

import concourse.bass as bass
from concourse import mybir

F32 = mybir.dt.float32
F32R = mybir.dt.float32r
I32 = mybir.dt.int32
U32 = mybir.dt.uint32
ALU = mybir.AluOpType
ACT = mybir.ActivationFunctionType
AX = mybir.AxisListType

P = 128
D = 1024
KT = D // P
S = 256
NT = S // P
HD = 64
SCALE = HD ** -0.5
EPS = 1e-6
SUBLN_EPS = 1e-5
LAM_INIT = 0.8 - 0.6 * math.exp(-0.3 * 0)
FAR = 1e30
AW = 3
RAW = 4
WRING = 4
HALF = 1024
CH = 32
NCH = S // CH
FF = 2816
FT = FF // P
TABLES = "natural_log_exp_and_others"

O_QA, O_KA, O_VA, O_GA = 0, 512, 1024, 1536
O_QB, O_KB, O_GB = 2048, 2560, 2816
O_QC, O_KC, O_VC, O_FC, O_GC, O_GM = 3328, 3840, 4352, 4864, 4872, 5384
E_NQ, E_NK, E_NV, E_HQ, E_HF, E_HB, E_HI, E_HG = [512 * i for i in range(8)]

C_NG, C_FG, C_MIX, C_FFN, C_HGN, C_LB, C_C, C_CC, C_ODW, C_ODB, C_FN, C_SUB = (
    0, 8, 16, 32, 48, 52, 68, 76, 84, 108, 116, 124)
C_ADAB, C_FCW, C_FCB = 128, 256, 256 + 66


BEFORE = [("qa", 0), ("qa", 1), ("ka", 0), ("ka", 1), ("va", 0), ("qb", 0)]
BESIDE = [[("va", 1)], [("qb", 1)], [("kvb", 0)], [("qc", 0)], [("qc", 1)], [("kc", 0)], [("kc", 1), ("fc", 0)],
          [("vc", 0)], [("vc", 1)], [("gb", 0)], [("gb", 1)], [("gc", 0)], [("gc", 1)], [("ga", 0), ("ga", 1)]]


def plan_units():
    units, spans = [], {}

    def section(name, kind, src, col0, n, width=256, step=None, k0=0):
        spans[name] = list(range(len(units), len(units) + n))
        for i in range(n):
            units.append((kind, src, k0, col0 + i * (width if step is None else step), width))

    first = {"qa": ("F", O_QA), "ka": ("F", O_KA), "va": ("T", O_VA), "qb": ("B", O_QB), "kvb": ("M", O_KB),
             "qc": ("F", O_QC), "kc": ("F", O_KC), "vc": ("T", O_VC), "fc": ("C", O_FC), "ga": ("F", O_GA),
             "gb": ("B", O_GB), "gc": ("F", O_GC)}
    for name, i in BEFORE + [unit for slot in BESIDE for unit in slot]:
        kind, off = first[name]
        spans.setdefault(name, []).append(len(units))
        units.append((kind, "w_in", 0, off + i * (128 if kind == "B" else 256), 128 if kind == "C" else 256))
    for i in range(4):
        for br in "bca":
            section(f"gm_{br}{i}", "F", "w_in", O_GM + D * "abc".index(br) + 256 * i, 1)
            section(f"up_{br}{i}", "U" if br != "b" else "V", f"w_up_{br}", i * 256, 1)
    section("wo", "F", "w_o", 0, 4)
    for name, kind, off in (("chf", "F", E_HF), ("chb", "F", E_HB), ("cnk", "F", E_NK), ("cnv", "T", E_NV),
                            ("chi", "T", E_HI), ("nq", "F", E_NQ), ("nk", "F", E_NK), ("hf", "F", E_HF),
                            ("hb", "F", E_HB), ("hq", "F", E_HQ), ("nv", "T", E_NV), ("hi", "T", E_HI),
                            ("hg", "F", E_HG)):
        section(name, kind, "ev_w_in", off, 2)
    for part in "AB":
        section(f"evo{part}", "U", f"ev_w_out{part}", 0, 4)

    def ffn(layer):
        for i in range(FT // 2):
            section(f"fa{layer}.{i}", "F", f"ffn_up{layer}", i * 256, 1)
            section(f"fv{layer}.{i}", "F", f"ffn_up{layer}", FF + i * 256, 1)
        for i in range(FT // 2):
            section(f"fd{layer}.{i}", "D", f"ffn_down{layer}", 0, 1, width=D, k0=2 * i)

    ffn(0)
    for i in range(4):
        section(f"odc{i}", "F", "od_w_in", D + i * 256, 1)
        section(f"odu{i}", "F", "od_w_in", 2 * D + i * 256, 1)
        section(f"odb{i}", "F", "od_w_in", i * 256, 1)
    section("odo", "F", "od_w_out", 0, 4)
    ffn(1)
    return units, spans


def build(nc, x, norm_gain, w_in, b_forget, lambda_q1, lambda_k1, lambda_q2, lambda_k2, subln_gain, sinks,
          w_up_a, w_up_b, w_up_c, w_o, final_gain, c_2, ctx_2, c_ctx_2, ada_w_2, ada_b_2,
          norm_mix_w_2, norm_ffn_w_2, ev_w_in_2, ev_w_out_2, na_rpb_2, hg_lb_logits_2, hg_norm_w_2,
          od_w_in_2, od_conv_w_2, od_conv_b_2, od_w_out_2, ffn_w_up_2, ffn_conv_w_2, ffn_conv_b_2,
          ffn_w_down_2, final_norm_w_2, out):
    UNITS, SPAN = plan_units()
    NU = len(UNITS)
    SRC = {"w_in": w_in[0], "w_up_a": w_up_a[0], "w_up_b": w_up_b[0], "w_up_c": w_up_c[0], "w_o": w_o[0],
           "ev_w_in": ev_w_in_2[0], "ev_w_outA": ev_w_out_2[0, 0:512], "ev_w_outB": ev_w_out_2[0, 512:1024],
           "od_w_in": od_w_in_2[0], "od_w_out": od_w_out_2[0],
           "ffn_up0": ffn_w_up_2[0], "ffn_up1": ffn_w_up_2[1],
           "ffn_down0": ffn_w_down_2[0], "ffn_down1": ffn_w_down_2[1]}

    halves = {"C": 1, "U": 1, "V": 1}
    NH = [halves.get(k[0], 2) for k in UNITS]
    H0 = [sum(NH[:u]) for u in range(NU)]
    loads = {"B": 2, "V": 2}
    LD = [loads.get(k[0], 1) for k in UNITS]
    LANDED = [16 * sum(LD[v] for v in range(u % RAW, u + 1, RAW)) for u in range(NU)]
    banked = [int(k[0] != "D") for k in UNITS]
    B0 = [sum(banked[:u]) for u in range(NU)]
    split_order = [u for u in range(NU) if NH[u]]
    after = {u: u + 1 for u in split_order[:-1] if NH[u + 1]}

    with ExitStack() as ctx:
        def sb(name, shape, dt=F32):
            return ctx.enter_context(nc.sbuf_tensor(name, shape, dt))

        def sem(name):
            return ctx.enter_context(nc.semaphore(name))

        raw = sb("raw", [P, RAW, 2 * HALF])
        whi = sb("whi", [P, WRING, HALF], F32R)
        wlo = sb("wlo", [P, WRING, HALF], F32R)
        xT = sb("xT", [P, KT, S])
        tok = sb("tok", [P, NT, D])
        rn = sb("rn", [P, 2, S])
        ident = sb("ident", [P, P])
        ones = sb("ones", [P, S])
        pcol = sb("pcol", [P, 4 * P])
        eps = sb("eps", [P, 2])
        mod = sb("mod", [P, 2, 48, 2])
        cm = sb("cm", [P, 5, KT])
        cs = sb("cs", [P, KT, 2])
        cse = sb("cse", [P, 2 * KT])
        stat = sb("stat", [P, 6, 4])
        vt = sb("vt", [P, 2, S])
        prow = vt[:, :, :].rearrange("p a (b c) -> p (a b) c", c=P)
        sctx = sb("sctx", [P, 2, 4, P])

        Hhi, Hlo = sb("Hhi", [P, KT, S], F32R), sb("Hlo", [P, KT, S], F32R)

        with ExitStack() as a1:
            def s1(name, shape, dt=F32):
                return a1.enter_context(nc.sbuf_tensor(name, shape, dt))
            dist = s1("dist", [P, 384])
            distw = s1("distw", [P, 384])
            cmask = s1("cmask", [P, 384])
            sel = s1("sel", [8, 8, P])
            sinkb = s1("sinkb", [P, 4, 2, 2])
            smallr = s1("smallr", [P, 16])
            lam4 = s1("lam4", [HD, 4])
            lamp = s1("lamp", [P, 8])
            negc = s1("negc", [8, S])
            bfc = s1("bfc", [8, 1])
            sg = s1("sg", [P, 12, S])
            sig = s1("sig", [P, 4, S])
            adaw0 = s1("adaw0", [P, AW, D])
            acc0 = s1("acc0", [P, 2, D])
            adat0 = s1("adat0", [P, D])
            with ExitStack() as a1a:
                def s2(name, shape, dt=F32):
                    return a1a.enter_context(nc.sbuf_tensor(name, shape, dt))
                qaT, kaT = s2("qaT", [P, 4, S]), s2("kaT", [P, 4, S])
                qbT, kbT = s2("qbT", [P, 4, S]), s2("kbT", [P, S])
                qcT, kcT = s2("qcT", [P, 4, S]), s2("kcT", [P, 4, S])
                va, vb, vc = s2("va", [P, NT, 512]), s2("vb", [P, NT, P]), s2("vc", [P, NT, 512])
                pr = s2("pr", [P, 2, 2, 384])
                pT = s2("pT", [P, 2, 2, 384])
                yA = s2("yA", [P, 4, S])
                distI = s2("distI", [P, 384], I32)
            fcw = sig[0:8, 0:2, :]
            with ExitStack() as a1b:
                def s2b(name, shape, dt=F32):
                    return a1b.enter_context(nc.sbuf_tensor(name, shape, dt))
                Mhi = s2b("Mhi", [P, 12, S], F32R)
                Mlo = s2b("Mlo", [P, 12, S], F32R)
                gate = s2b("gate", [P, 2, 2, S])
                merged = s2b("merged", [P, 2, S])
                mt = s2b("mt", [P, 2, S])
                Whi, Wlo = s2b("Whi", [P, KT, S], F32R), s2b("Wlo", [P, KT, S], F32R)
        with ExitStack() as a2:
            def s3(name, shape, dt=F32):
                return a2.enter_context(nc.sbuf_tensor(name, shape, dt))
            naq, nak, cnk = s3("naq", [P, 4, S]), s3("nak", [P, 4, S]), s3("cnk", [P, 4, S])
            nav, cnv = s3("nav", [P, NT, 512]), s3("cnv", [P, NT, 512])
            with ExitStack() as aX:
                Xhi = aX.enter_context(nc.sbuf_tensor("Xhi", [P, KT, S], F32R))
                Xlo = aX.enter_context(nc.sbuf_tensor("Xlo", [P, KT, S], F32R))
            hov = s3("hov", [P, 4, 4, S])
            nbB = s3("nbB", [P, 3, 6, HD])
            lbc = s3("lbc", [P, 3, 8])
            with ExitStack() as a2a:
                def s4(name, shape, dt=F32):
                    return a2a.enter_context(nc.sbuf_tensor(name, shape, dt))
                qe, ke, kd = s4("qe", [P, 4, S]), s4("ke", [P, 4, S]), s4("kd", [P, 4, S])
                sq = s4("sq", [P, NCH, P])
                hq, hv = s4("hq", [P, 4, S]), s4("hv", [P, NT, 512])
                kk = s4("kk", [P, 2, 4, S])
                lg = s4("lg", [P, 2, 4, S])
                kdt = s4("kdt", [P, 2, P])
                attm = s4("attm", [P, 2, P])
                vbd = s4("vbd", [P, NT, 4, P])
                oT = s4("oT", [P, 4, S])
                smask = s4("smask", [P, 2, P])
                reset = s4("reset", [P, S])
                hgt = s4("hgt", [P, 2, S])
                sgh = s4("sgh", [P, 4, S])
                dec = s4("dec", [P, 2, 4 * NCH])
            with ExitStack() as a2b:
                def s5(name, shape, dt=F32):
                    return a2b.enter_context(nc.sbuf_tensor(name, shape, dt))
                pn = s5("pn", [P, 2, NT, 512])
                pnT = s5("pnT", [P, 4, 512])
                adaw1 = s5("adaw1", [P, AW, D])
                acc1 = s5("acc1", [P, 2, D])
                adat1 = s5("adat1", [P, D])
        with ExitStack() as a3:
            def s6(name, shape, dt=F32):
                return a3.enter_context(nc.sbuf_tensor(name, shape, dt))
            Ghi, Glo = s6("Ghi", [P, FT, S], F32R), s6("Glo", [P, FT, S], F32R)
            fa = s6("fa", [P, 2, 2, S])
            fz = s6("fz", [P, 2, 2, S])
        SIG = (None, tok[:, 0, :].rearrange("p (h s) -> p h s", s=S), sig, tok[:, 0, :].rearrange(
            "p (h s) -> p h s", s=S))
        xn = sg[:, 0:KT, :].rearrange("p (t k) s -> p t (k s)", t=NT)
        FIRST = [sg[:, KT + i, :] for i in range(4)]
        cxT = sg[:, 0:KT, :]
        sqv = tok[:, :, :].rearrange("p t (k s) -> p (t k) s", s=S)
        headr = tok[:, 1, :].rearrange("p (a b) -> p a b", a=2)
        headr2 = qe[:, :, :].rearrange("p (a h) s -> p a (h s)", a=2)
        nbA = tok[:, :, :].rearrange("p t n -> p (t n)")[:, 0:5 * 6 * HD].rearrange(
            "p (h j c) -> p h j c", h=5, j=6)
        rpad, rrev = attm[0:120, 0, :], attm[0:120, 1, :]
        QE, KE, KD = (qe, hov[:, 0]), (ke, hov[:, 1]), (kd, hov[:, 2])
        SQ = (sq, tok[:, 0, :].rearrange("p (c v) -> p c v", c=NCH))
        nbf = nbB[:, :, :, :].rearrange("p h j c -> p (h j c)")
        ATTM = [attm[:, :, :]] + [nbf[:, i * S:(i + 1) * S].rearrange("p (t n) -> p t n", t=NT) for i in range(3)]
        kdc = hq[:, :, :].rearrange("p h (t n) -> p h t n", t=NT)
        rscr = nc.dram_tensor("rpb_rows", (120, P), F32, kind="Internal").ap()

        psG = ctx.enter_context(nc.psum_tensor("psG", [P, 2, 512], F32))
        psS = ctx.enter_context(nc.psum_tensor("psS", [P, 4, 512], F32))
        psX = ctx.enter_context(nc.psum_tensor("psX", [P, 512], F32))
        psY = ctx.enter_context(nc.psum_tensor("psY", [P, 512], F32))

        raw_landed = [sem(f"raw_landed{i}") for i in range(RAW)]
        hi_split, lo_split = sem("hi_split"), sem("lo_split")
        half_used, ada_kept = sem("half_used"), sem("ada_kept")
        adaw_landed = [sem(f"adaw_landed{i}") for i in range(AW)]
        acc_ready, acc_summed = sem("acc_ready"), sem("acc_summed")
        v_set, vhi_set = sem("v_set"), sem("vhi_set")
        M_high, core_done, down_part = sem("M_high"), sem("core_done"), sem("down_part")
        rest_in = sem("rest_in")
        h1_inv, xn_set, xn_turned = sem("h1_inv"), sem("xn_set"), sem("xn_turned")
        sig_set, gated, sub_taken = sem("sig_set"), sem("gated"), sem("sub_taken")
        gate_used, ident_set = sem("gate_used"), sem("ident_set")
        bank_free = [sem("bank_free0"), sem("bank_free1")]
        acts, dves, pools = sem("act_step"), sem("dve_step"), sem("pool_step")
        tok_in, par_in, misc_in, scr_out, nb_in, out_done = [sem(n) for n in (
            "tok_in", "par_in", "misc_in", "scr_out", "nb_in", "out_done")]
        consts, ones_set = sem("consts"), sem("ones_set")
        turned, turned_kept = sem("turned"), sem("turned_kept")
        squares, sums, rms_inv, H_ready, norm_done = [sem(n) for n in (
            "squares", "sums", "rms_inv", "H_ready", "norm_done")]
        kept = sem("kept")
        silu_e = sem("silu_e")
        c_silu, c_exp = sem("c_silu"), sem("c_exp")
        small_mm, small_ev, small_ex = sem("small_mm"), sem("small_ev"), sem("small_ex")
        forget, forget_a = sem("forget"), sem("forget_a")
        scored, biased, exped, probs, turnedP, pT_kept, yed, y_kept = [sem(n) for n in (
            "scored", "biased", "exped", "probs", "turnedP", "pT_kept", "yed", "y_kept")]
        sub_sq, sub_sum, sub_inv = sem("sub_sq"), sem("sub_sum"), sem("sub_inv")
        M_ready = sem("M_ready")
        gate_e = sem("gate_e")
        merge_ready = sem("merge_ready")
        x_ready = sem("x_ready")
        lb_e = sem("lb_e")
        f_e, f_set, f_ln, f_cum, f_exp, f_mul = [sem(n) for n in (
            "f_e", "f_set", "f_ln", "f_cum", "f_exp", "f_mul")]
        vbd_set, kd_turned, kd_kept, kv_done, att_done, att_set, st_set, o_done, o_kept = [sem(n) for n in (
            "vbd_set", "kd_turned", "kd_kept", "kv_done", "att_done", "att_set", "st_set", "o_done", "o_kept")]
        ctx_state, ctx_kept = sem("ctx_state"), sem("ctx_kept")
        nb_set, nb_used, masks_set = sem("nb_set"), sem("nb_used"), sem("masks_set")
        conv_a, gelu_in, gelu_out, G_ready = [sem(n) for n in (
            "conv_a", "gelu_in", "gelu_out", "G_ready")]
        cu_set, c_kept = sem("cu_set"), sem("c_kept")
        out_turned, out_kept = sem("out_turned"), sem("out_kept")

        block = ctx.enter_context(nc.Block())

        def bank(u):
            return psG[:, B0[u] % 2, :]

        def token_bank(n):
            return psX[:, :] if n % 2 else psY[:, :]

        ACCS = [(0, 0, 0), (0, 0, 1), (0, 1, 0), (0, 1, 1)] + [(0, s, 0) for s in range(2, 6)] + [
            (1, s, 0) for s in range(6)]

        def ada_bank(n):
            return psX[:, 0:KT]

        def nb_head(h):
            return nbA[:, h, :, :] if h < 5 else nbB[:, h - 5, :, :]


        def half(ring, h):
            return ring[:, h % WRING, :]

        def raw_half(u, i):
            kind = UNITS[u][0]
            r = raw[:, u % RAW, :]
            if kind in "FM":
                return r.rearrange("p (k n) -> p k n", k=KT)[:, :, i * P:(i + 1) * P], KT
            if kind == "B":
                return r.rearrange("p (k i j r) -> p k i j r", k=KT, i=2, j=2)[:, :, :, i, :], KT
            if kind == "C":
                return r[:, 0:HALF], 1
            if kind in "UV":
                return r[:, 0:HALF], 1
            return r[:, i * HALF:(i + 1) * HALF], 1

        def ring_half(ring, u, i):
            kind = UNITS[u][0]
            a = half(ring, H0[u] + i)
            if kind in "FM":
                return a.rearrange("p (k n) -> p k n", k=KT)
            if kind == "B":
                return a.rearrange("p (k i r) -> p k i r", k=KT, i=2)
            return a

        GROUPS = [("A", h) for h in range(4)] + [("B", j) for j in range(4)] + [("C", j) for j in range(4)]
        NG = len(GROUPS)
        TSETS = [1 if b == "A" else 2 for b, _ in GROUPS]
        T0 = [sum(TSETS[:g]) for g in range(NG)]
        NT0 = T0[-1] + TSETS[-1]
        COLS = [(0, P), (P, 384)]
        SLOT = [[SPAN[name][i] for name, i in units] for units in BESIDE]
        KEEPS = [u for u in range(SLOT[-1][-1] + 1) if UNITS[u][0] != "C" and u not in
                 SPAN["ga"] + SPAN["gb"] + SPAN["gc"]]
        K1 = len(KEEPS)
        SLOT2 = SPAN["nv"] + SPAN["hi"] + SPAN["hg"] + 4 * [None]
        KEPT = {name: KEEPS.index(SPAN[name][-1]) + 1 for name in ("ka", "va", "kvb", "kc", "vc")}
        GATES = SPAN["gb"] + SPAN["gc"] + SPAN["ga"]
        SUM_AT = {5: 0, 6: 1, 12: 2, 13: 3}
        col = lambda ap: ap.rearrange("a (k p) -> (a k) p", p=P)
        PAR_ROWS = [(col(norm_gain), C_NG, 8), (final_gain.rearrange("(k p) -> k p", p=P), C_FG, 8),
                    (col(norm_mix_w_2), C_MIX, 16), (col(norm_ffn_w_2), C_FFN, 16), (col(hg_norm_w_2), C_HGN, 4),
                    (hg_lb_logits_2.rearrange("n d (k p) -> (n d k) p", p=P), C_LB, 16), (col(c_2), C_C, 8),
                    (c_ctx_2.rearrange("(k p) -> k p", p=P), C_CC, 8),
                    (od_conv_w_2.rearrange("a t (k p) -> (a t k) p", p=P), C_ODW, 24), (col(od_conv_b_2), C_ODB, 8),
                    (final_norm_w_2.rearrange("(k p) -> k p", p=P), C_FN, 8), (subln_gain, C_SUB, 1),
                    (col(ada_b_2), C_ADAB, 96)]
        for l in range(2):
            PAR_ROWS += [(ffn_conv_w_2[l].rearrange("t (k p) -> (t k) p", p=P), C_FCW + P * l, 66),
                         (ffn_conv_b_2[l:l + 1, :].rearrange("t (k p) -> (t k) p", p=P), C_FCB + P * l, 22)]
        PAR_FIRST, PAR_REST = [r for r in PAR_ROWS if r[1] < P], [r for r in PAR_ROWS if r[1] >= P]
        MISC = 6
        F = {n: i for i, n in enumerate(["ctx", "fin1", "mix0", "ffn0", "mix1", "ffn1", "last"])}
        VALUE = (vt[:, 0, :], vt[:, 1, :], rn[:, 0, :])
        XR = {"ffn0": 4, "mix1": 8, "ffn1": 12, "last": 16}
        H_COUNT = {"h1": 1, "ctx": 2, "mix0": 3, "ffn0": 4, "mix1": 5, "ffn1": 6}

        @block.sync
        def _(sp):
            xv = x.rearrange("b (t p) d -> p (b t) d", p=P)
            for t in range(NT):
                sp.dma_start(tok[:, t, :], xv[:, t, :]).then_inc(tok_in, 16)
            for rows, at, n in PAR_FIRST[0::2]:
                sp.dma_start(prow[at % P:at % P + n, at // P, :], rows).then_inc(par_in, 16)
            for u, (kind, src, k0, col0, width) in enumerate(UNITS):
                slot = u % RAW
                if u == 2:
                    for rows, at, n in PAR_REST:
                        sp.dma_start(prow[at % P:at % P + n, at // P, :], rows).then_inc(rest_in, 16)
                    for q, v in enumerate((lambda_q1, lambda_k1, lambda_q2, lambda_k2)):
                        sp.dma_start(lam4[:, q:q + 1], v.rearrange("a d -> d a")).then_inc(misc_in, 16)
                    sp.dma_start(smallr[0:1, 0:8], sinks).then_inc(misc_in, 16)
                    sp.dma_start(bfc[:, :], b_forget.rearrange("a h -> h a")).then_inc(misc_in, 16)
                if u >= RAW:
                    sp.wait_ge(lo_split, H0[u - RAW] + NH[u - RAW])
                w = SRC[src]
                r = raw[:, slot, :]
                if kind == "B":
                    rv = r.rearrange("p (k i n) -> p k i n", k=KT, i=2)
                    for i in range(2):
                        c = col0 + i * 256
                        sp.dma_start(rv[:, :, i, :], w[:, c:c + P].rearrange("(k p) n -> p k n", p=P)
                                     ).then_inc(raw_landed[slot], 16)
                elif kind == "V":
                    for i in range(2):
                        sp.dma_start(r[i * HD:(i + 1) * HD, 0:HALF].rearrange("p (k n) -> p k n", k=4),
                                     w[i * 256:(i + 1) * 256, col0:col0 + width].rearrange("(k p) n -> p k n", p=HD)
                                     ).then_inc(raw_landed[slot], 16)
                elif kind == "D":
                    sp.dma_start(r.rearrange("p (k n) -> p k n", k=2),
                                 w[k0 * P:(k0 + 2) * P, :].rearrange("(k p) n -> p k n", p=P)
                                 ).then_inc(raw_landed[slot], 16)
                else:
                    kt = 4 if kind == "U" else KT
                    sp.dma_start(r[:, 0:kt * width].rearrange("p (k n) -> p k n", k=kt),
                                 w[:, col0:col0 + width].rearrange("(k p) n -> p k n", p=P)
                                 ).then_inc(raw_landed[slot], 16)
            ov = out.rearrange("b (t p) d -> p (b t) d", p=P)
            for k4 in range(2):
                for t in range(NT):
                    sp.wait_ge(out_kept, 2 * k4 + t + 1)
                    a = slice(k4 * 512, (k4 + 1) * 512)
                    sp.dma_start(ov[:, t, a], tok[:, t, a]).then_inc(out_done, 16)
            sp.wait_ge(out_done, 16 * 2 * NT)

        @block.tensor
        def _(pe):
            mm = nc.tensor.matmul

            def product(o, a_hi, a_lo, b_hi, b_lo, first, last, shared=False):
                mm(o, a_hi, b_lo, start=first, stop=False, skip_group_check=shared)
                mm(o, a_lo, b_hi, start=False, stop=False, skip_group_check=shared)
                return mm(o, a_hi, b_hi, start=False, stop=last, skip_group_check=shared)

            def open_bank(u):
                n = B0[u] // 2
                if n:
                    pe.wait_ge(bank_free[B0[u] % 2], n)

            def project(u, ahi, alo, ready=None, base=0, between=lambda: None):
                kind = UNITS[u][0]
                open_bank(u)
                o = bank(u)
                h = H0[u]

                def pair(k):
                    if ready is not None:
                        if ready[0] is H_ready:
                            pe.wait_ge(H_ready, ready[1] + k + 1)
                        elif k % 2 == 0:
                            pe.wait_ge(ready[0], ready[1] + k // 2 + 1)
                if kind == "F" and ready is not None and ready[0] is H_ready:
                    pe.wait_ge(lo_split, h + 2)
                    wh = [half(whi, h + n).rearrange("p (k n) -> p k n", k=KT) for n in range(2)]
                    wl = [half(wlo, h + n).rearrange("p (k n) -> p k n", k=KT) for n in range(2)]
                    for k in range(KT):
                        pair(k)
                        for n in range(2):
                            last = product(o[:, n * S:(n + 1) * S], wh[n][:, k, :], wl[n][:, k, :],
                                           ahi[:, base + k, :], alo[:, base + k, :], k == 0 and n == 0, k == KT - 1,
                                           shared=True)
                    last.then_inc(half_used, 2)
                elif kind in "FBC":
                    for n in range(NH[u]):
                        pe.wait_ge(lo_split, h + n + 1)
                        wh = half(whi, h + n).rearrange("p (k n) -> p k n", k=KT)
                        wl = half(wlo, h + n).rearrange("p (k n) -> p k n", k=KT)
                        for k in range(KT):
                            if n == 0:
                                pair(k)
                            last = product(o[:, n * S:(n + 1) * S], wh[:, k, :], wl[:, k, :],
                                           ahi[:, base + k, :], alo[:, base + k, :], k == 0, k == KT - 1)
                        last.then_inc(half_used, 1)
                        if n == 0:
                            between()
                elif kind == "T":
                    for t in range(NT):
                        for k in range(KT):
                            if t == 0:
                                pair(k)
                            if t == 0 and k % 4 == 0:
                                pe.wait_ge(lo_split, h + k // 4 + 1)
                            q, n = k // 4, k % 4
                            last = product(o[:, t * 256:(t + 1) * 256],
                                           ahi[:, base + k, t * P:(t + 1) * P], alo[:, base + k, t * P:(t + 1) * P],
                                           half(whi, h + q)[:, n * 256:(n + 1) * 256],
                                           half(wlo, h + q)[:, n * 256:(n + 1) * 256], k == 0, k == KT - 1)
                            if t == NT - 1 and k % 4 == 3:
                                last.then_inc(half_used, 1)
                        if t == 0:
                            between()
                elif kind == "M":
                    for n in range(2):
                        pe.wait_ge(lo_split, h + n + 1)
                        wh = half(whi, h + n).rearrange("p (k n) -> p k n", k=KT)
                        wl = half(wlo, h + n).rearrange("p (k n) -> p k n", k=KT)
                        for t in range(1 if n == 0 else NT):
                            for k in range(KT):
                                if n == 0:
                                    last = product(o[:, 0:S], wh[:, k, :], wl[:, k, :], ahi[:, k, :], alo[:, k, :],
                                                   k == 0, k == KT - 1)
                                else:
                                    last = product(o[:, S + t * P:S + (t + 1) * P],
                                                   ahi[:, k, t * P:(t + 1) * P], alo[:, k, t * P:(t + 1) * P],
                                                   wh[:, k, :], wl[:, k, :], k == 0, k == KT - 1)
                        last.then_inc(half_used, 1)
                        if n == 0:
                            between()
                else:
                    pe.wait_ge(lo_split, h + 1)
                    wh = half(whi, h).rearrange("p (k n) -> p k n", k=4)
                    wl = half(wlo, h).rearrange("p (k n) -> p k n", k=4)
                    for n in range(2):
                        for k in range(4):
                            last = product(o[:, n * S:(n + 1) * S], wh[:, k, n * P:(n + 1) * P],
                                           wl[:, k, n * P:(n + 1) * P], ahi[:, base + k, :], alo[:, base + k, :],
                                           k == 0, k == 3)
                    last.then_inc(half_used, 1)

            def sum_ada(n):
                pe.wait_ge(acc_ready, n + 1)
                if n:
                    pe.wait_ge(ada_kept, n)
                acc = acc0 if n < 8 else acc1
                for k in range(KT):
                    last = mm(ada_bank(n)[:, k:k + 1], acc[:, n % 2, k * P:(k + 1) * P], ones[:, 0:1],
                              start=True, stop=True)
                last.then_inc(acc_summed, 1)

            def sum_squares(i):
                for k in range(KT):
                    if k % 2 == 0:
                        pe.wait_ge(squares, 4 * i + k // 2 + 1)
                    last = mm(psY[:, 0:S], ones[:, 0:P], sqv[:, k, :], start=(k == 0), stop=(k == KT - 1))
                last.then_inc(sums, 1)


            def turn_tokens(i):
                pe.wait_ge(tok_in, 16 * NT * (i + 1))
                for k4 in range(4):
                    if k4 >= 2:
                        pe.wait_ge(turned_kept, 4 * i + k4 - 1)
                    for kk_ in range(2):
                        k = 2 * k4 + kk_
                        for t in range(NT):
                            last = nc.tensor.transpose(token_bank(k4)[:, kk_ * S + t * P:kk_ * S + (t + 1) * P],
                                                       tok[:, t, k * P:(k + 1) * P], ident[:, :])
                    last.then_inc(turned, 1)

            pe.wait_ge(ident_set, 1)
            pe.wait_ge(ones_set, 1)
            pe.wait_ge(par_in, 16 * len(PAR_FIRST))
            nc.tensor.transpose(psX[:, 0:125], prow[0:125, 0, :], ident[0:125, 0:125]).then_inc(small_mm, 1)
            pe.wait_ge(xn_set, NT)
            for k4 in range(2):
                for t in range(NT):
                    for q in range(4):
                        k = 4 * k4 + q
                        last = nc.tensor.transpose(psS[:, 2 * k4 + t, q * P:(q + 1) * P],
                                                   xn[:, t, k * P:(k + 1) * P], ident[:, :])
                last.then_inc(xn_turned, 1)

            for name, i in BEFORE:
                u = SPAN[name][i]
                project(u, Hhi, Hlo, ready=(H_ready, 0) if u == 0 else None)
                if u == 0:
                    pe.wait_ge(rest_in, 16 * len(PAR_REST))
                    pe.wait_ge(small_ev, 1)
                    for t, rows in ((1, 96), (2, 88), (3, 88)):
                        last = nc.tensor.transpose(psX[:, t * P:t * P + rows], prow[0:rows, t, :],
                                                   ident[0:rows, 0:rows])
                    last.then_inc(small_mm, 1)
                if u == SPAN["ka"][1]:
                    pe.wait_ge(misc_in, 16 * MISC)
                    pe.wait_ge(small_ev, 3)
                    mm(psX[:, 0:2], ones[0:HD, 0:P], lamp[0:HD, 0:2], start=True, stop=True)
                    mm(psX[:, 8:16], ones[0:1, 0:P], smallr[0:1, 0:8], start=True, stop=True).then_inc(small_mm, 1)
                elif name == "va":
                    pe.wait_ge(small_ex, 1)
                    turn_tokens(0)

            def scores(g):
                br, j = GROUPS[g]
                if j == 0:
                    pe.wait_ge(kept, KEPT[{"A": "ka", "B": "kvb", "C": "kc"}[br]])
                if g >= 2:
                    pe.wait_ge(exped, g - 1)
                if br == "C" and j == 0:
                    pe.wait_ge(forget, 1)
                for i in range(2):
                    q = (qaT, qbT, qcT)["ABC".index(br)][i * HD:(i + 1) * HD, j, :]
                    k = kaT[i * HD:(i + 1) * HD, j, :] if br == "A" else (
                        kbT[i * HD:(i + 1) * HD, :] if br == "B" else kcT[i * HD:(i + 1) * HD, j, :])
                    for t in range(NT):
                        o = psS[:, 2 * (g % 2) + i, COLS[t][0]:COLS[t][1]]
                        last = mm(o, q[:, t * P:(t + 1) * P], k[:, 0:(t + 1) * P], start=True, stop=(br != "C"))
                        if br == "C":
                            last = mm(o, sel[0:8, 2 * j + i, :], negc[0:8, 0:(t + 1) * P], start=False, stop=True)
                last.then_inc(scored, 1)

            def turn_probs(g, i):
                n = T0[g] + i
                pe.wait_ge(probs, g + 1)
                if n >= 1:
                    pe.wait_ge(pT_kept, n)
                else:
                    pe.wait_ge(turned_kept, 4)
                if i == 0 and g + 1 in SUM_AT:
                    pe.wait_ge(ada_kept, SUM_AT[g + 1] + 1)
                if i == 0 and g in (6, 7):
                    pe.wait_ge(sub_taken, g - 5)
                for b in range(3):
                    last = nc.tensor.transpose(psX[:, b * P:(b + 1) * P], pr[:, g % 2, i, b * P:(b + 1) * P],
                                               ident[:, :])
                last.then_inc(turnedP, 1)

            def weigh(g):
                br, j = GROUPS[g]
                pe.wait_ge(pT_kept, T0[g] + TSETS[g])
                if j == 0:
                    pe.wait_ge(kept, KEPT[{"A": "va", "B": "kvb", "C": "vc"}[br]])
                if g:
                    pe.wait_ge(y_kept, g)
                for i in range(TSETS[g]):
                    if br == "A":
                        rows, v = slice(0, P), va[:, :, j * P:(j + 1) * P]
                    elif br == "B":
                        rows, v = slice(i * HD, (i + 1) * HD), vb[:, :, i * HD:(i + 1) * HD]
                    else:
                        rows, v = slice(i * HD, (i + 1) * HD), vc[:, :, (2 * j + i) * HD:(2 * j + i + 1) * HD]
                    y = psY[:, 0:S]
                    mm(y[rows, :], v[:, 0, :], pT[:, g % 2, i, 0:S], start=True, stop=False)
                    last = mm(y[rows, P:S], v[:, 1, :], pT[:, g % 2, i, S:384], start=False, stop=True)
                last.then_inc(yed, 1)

            for s, fill in enumerate(SLOT):
                if s < NG:
                    scores(s)
                if s >= 2:
                    turn_probs(s - 2, 0)
                two = s >= 2 and TSETS[s - 2] == 2
                project(fill[0], Hhi, Hlo, between=(lambda: turn_probs(s - 2, 1)) if two else (lambda: None))
                if s >= 2:
                    weigh(s - 2)
                for u in fill[1:]:
                    project(u, Hhi, Hlo)
                if s in SUM_AT:
                    sum_ada(SUM_AT[s])
                if s in (7, 8):
                    pe.wait_ge(sub_sq, 1)
                    mm(psX[:, :], ones[:, 0:P], sqv[:, 2 * (s - 7):2 * (s - 7) + 2, :], start=True, stop=True
                       ).then_inc(sub_sum, 1)
            for i in range(4):
                for b, br in enumerate("bca"):
                    project(SPAN[f"gm_{br}{i}"][0], Hhi, Hlo)
                    if i == 0:
                        pe.wait_ge(M_ready, b + 1)
                    project(SPAN[f"up_{br}{i}"][0], Mhi, Mlo, base=4 * "abc".index(br))
                if i == 0:
                    sum_ada(4)
                elif i == 1:
                    pe.wait_ge(ada_kept, 5)
                    turn_tokens(1)
                elif i == 2:
                    pe.wait_ge(turned_kept, 8)
                    sum_ada(5)
                    sum_squares(F["ctx"])
                else:
                    sum_ada(6)
            for u in SPAN["wo"]:
                project(u, Whi, Wlo, ready=(merge_ready, 0) if u == SPAN["wo"][0] else None)
                if u == SPAN["wo"][2]:
                    sum_ada(7)

            for name in ("chf", "chb", "cnk", "cnv", "chi"):
                for u in SPAN[name]:
                    project(u, Hhi, Hlo, ready=(H_ready, KT) if u == SPAN["chf"][0] else None)
                    if u == SPAN["chf"][0]:
                        sum_squares(F["fin1"])
                    if u == SPAN["cnk"][0]:
                        sum_squares(F["mix0"])

            def turn_ctx_keys(d):
                pe.wait_ge(f_mul, d + 1)
                if d:
                    pe.wait_ge(ctx_kept, 1)
                else:
                    pe.wait_ge(rms_inv, F["mix0"] + 1)
                for j in range(4):
                    for t in range(NT):
                        n = (j % 2) * NT + t
                        last = nc.tensor.transpose((psX, psY)[j // 2][:, n * P:(n + 1) * P],
                                                   kd[:, j, t * P:(t + 1) * P], ident[:, :])
                last.then_inc(kd_turned, 1)

            def ctx_states(d):
                pe.wait_ge(kd_kept, d + 1)
                for j in range(4):
                    for t in range(NT):
                        last = mm(psY[:, j * P:(j + 1) * P], kdc[:, j, t, :], hv[:, t, j * P:(j + 1) * P],
                                  start=(t == 0), stop=(t == NT - 1))
                last.then_inc(ctx_state, 1)

            for name, i in (("nq", 0), ("nq", 1), ("nk", 0), ("nk", 1)):
                u = SPAN[name][i]
                if (name, i) == ("nk", 0):
                    turn_ctx_keys(0)
                elif (name, i) == ("nk", 1):
                    ctx_states(0)
                project(u, Xhi, Xlo, ready=(H_ready, 2 * KT) if u == SPAN["nq"][0] else None)
            turn_ctx_keys(1)
            for u in SPAN["hf"] + SPAN["hb"] + SPAN["hq"]:
                project(u, Xhi, Xlo)
                if u == SPAN["hf"][0]:
                    ctx_states(1)

            def na_scores(h):
                j, i = h // 2, h % 2
                if h == 0:
                    pe.wait_ge(kept, K1 + 10)
                elif h >= 2:
                    pe.wait_ge(exped, NG + h - 1)
                for t in range(NT):
                    q = naq[i * HD:(i + 1) * HD, j, t * P:(t + 1) * P]
                    o = psS[:, 2 * (h % 2) + t, :]
                    mm(o[:, 0:S], q, nak[i * HD:(i + 1) * HD, j, :], start=True, stop=True)
                    last = mm(o[:, S:512], q, cnk[i * HD:(i + 1) * HD, j, :], start=True, stop=True)
                last.then_inc(scored, 1)

            def na_turn(h, t):
                n = 2 * h + t
                pe.wait_ge(probs, NG + h + 1)
                if n >= 1:
                    pe.wait_ge(pT_kept, NT0 + n)
                for b in range(4):
                    last = nc.tensor.transpose(psX[:, b * P:(b + 1) * P], pn[:, h % 2, t, b * P:(b + 1) * P],
                                               ident[:, :])
                last.then_inc(turnedP, 1)

            def na_weigh(h):
                j, i = h // 2, h % 2
                pe.wait_ge(pT_kept, NT0 + 2 * h + 2)
                if h == 0:
                    pe.wait_ge(kept, K1 + 12)
                    pe.wait_ge(ctx_kept, 2)
                elif i == 0:
                    pe.wait_ge(y_kept, NG + j)
                for t in range(NT):
                    for b in range(4):
                        v = (nav if b < 2 else cnv)[:, b % 2, h * HD:(h + 1) * HD]
                        last = mm(psY[i * HD:(i + 1) * HD, t * P:(t + 1) * P], v,
                                  pnT[:, (2 * h + t) % 4, b * P:(b + 1) * P], start=(b == 0), stop=(b == 3))
                last.then_inc(yed, 1)

            for s, u in enumerate(SLOT2):
                if s < 8:
                    na_scores(s)
                if s >= 2:
                    na_turn(s - 2, 0)
                if u is None:
                    na_turn(s - 2, 1)
                else:
                    project(u, Xhi, Xlo, between=(lambda: na_turn(s - 2, 1)) if s >= 2 else (lambda: None))
                if s >= 2:
                    na_weigh(s - 2)

            def turn_kd(n):
                d, j = 1 - n // 4, n % 4
                pe.wait_ge(f_mul, 3 + n // 4)
                if n:
                    pe.wait_ge(kd_kept, 2 + n)
                for t in range(NT):
                    last = nc.tensor.transpose(psX[:, t * P:(t + 1) * P], KD[d][:, j, t * P:(t + 1) * P], ident[:, :])
                last.then_inc(kd_turned, 1)

            def within(n):
                d, j = 1 - n // 4, n % 4
                if n < 2:
                    u = SPAN["hg"][0]
                    u += (B0[u] + n) % 2
                    pe.wait_ge(bank_free[n % 2], B0[u] // 2 + 1)
                else:
                    pe.wait_ge(att_set, n - 1)
                for t in range(NT):
                    a = slice(t * P, (t + 1) * P)
                    last = mm(psG[:, n % 2, a], KE[d][:, j, a], QE[d][:, j, a], start=True, stop=True)
                last.then_inc(att_done, 1)

            def adds(n):
                pe.wait_ge(kd_kept, 2 + n + 1)
                pe.wait_ge(vbd_set, n + 1)
                if n >= 2:
                    pe.wait_ge(st_set, n - 1)
                else:
                    pe.wait_ge(exped, NG + 8)
                for t in range(NT):
                    last = mm(psS[:, 2 * (n % 2) + t, :], kdt[:, t, :], vbd[:, t, :, :], start=True, stop=True)
                last.then_inc(kv_done, 1)

            def outputs(n):
                d, j = 1 - n // 4, n % 4
                pe.wait_ge(att_set, n + 1)
                pe.wait_ge(st_set, n + 1)
                if n:
                    pe.wait_ge(o_kept, n)
                for t in range(NT):
                    mm(psY[:, t * P:(t + 1) * P], hv[:, t, j * P:(j + 1) * P], ATTM[2 * (n // 4) + n % 2][:, t, :],
                       start=True, stop=False)
                    for c in range(4):
                        cc = 4 * t + c
                        last = mm(psY[:, cc * CH:(cc + 1) * CH], SQ[n % 2][:, cc, :],
                                  QE[d][:, j, cc * CH:(cc + 1) * CH], start=False, stop=(c == 3))
                last.then_inc(o_done, 1)

            for n in range(8 + 1):
                if n < 8:
                    turn_kd(n)
                    within(n)
                    adds(n)
                if n:
                    outputs(n - 1)
            pe.wait_ge(sub_sq, 2)
            for i in range(2):
                last = mm(psS[:, 2 + i, :], ones[:, 0:P], kd[:, 2 * i:2 * i + 2, :], start=True, stop=True)
            last.then_inc(sub_sum, 1)
            pe.wait_ge(M_ready, 7)
            for u in SPAN["evoA"]:
                project(u, Hhi, Hlo)
            pe.wait_ge(M_ready, 8)
            for u in SPAN["evoB"]:
                project(u, Hhi, Hlo, base=4)

            def feed_forward(layer):
                sum_squares(F[f"ffn{layer}"])
                for i in range(FT // 2):
                    for part in ("fa", "fv"):
                        u = SPAN[f"{part}{layer}.{i}"][0]
                        project(u, Hhi, Hlo, ready=(H_ready, KT * (3 + 2 * layer)) if part == "fa" and i == 0 else None)
                    if layer == 0 and i in (5, 10):
                        sum_ada({5: 8, 10: 9}[i])
                for i in range(FT // 2):
                    u = SPAN[f"fd{layer}.{i}"][0]
                    pe.wait_ge(G_ready, (FT // 2 + 4) * layer + i + 1)
                    h = H0[u]
                    if i < FT // 2 - 1:
                        for q in range(2):
                            k = 2 * i + q
                            pe.wait_ge(lo_split, h + q + 1)
                            for n in range(KT):
                                last = product(psS[:, n // 2, (n % 2) * S:(n % 2 + 1) * S],
                                               half(whi, h + q)[:, n * P:(n + 1) * P],
                                               half(wlo, h + q)[:, n * P:(n + 1) * P],
                                               Ghi[:, k, :], Glo[:, k, :], k == 0 and n % 2 == 0, False, shared=True)
                            last.then_inc(half_used, 1)
                    else:
                        pe.wait_ge(lo_split, h + 2)
                        for n in range(KT):
                            for q in range(2):
                                k = 2 * i + q
                                last = product(psS[:, n // 2, (n % 2) * S:(n % 2 + 1) * S],
                                               half(whi, h + q)[:, n * P:(n + 1) * P],
                                               half(wlo, h + q)[:, n * P:(n + 1) * P],
                                               Ghi[:, k, :], Glo[:, k, :], False, q == 1, shared=True)
                            if n in (1, 3, 5):
                                last.then_inc(down_part, 1)
                        last.then_inc(half_used, 2)
                    if layer == 0 and i == 6:
                        sum_ada(10)

            feed_forward(0)
            sum_squares(F["mix1"])
            for i in range(4):
                for part in "cub":
                    u = SPAN[f"od{part}{i}"][0]
                    project(u, Hhi, Hlo, ready=(H_ready, 4 * KT) if part == "c" and i == 0 else None)
                if i >= 1:
                    sum_ada(10 + i)
            pe.wait_ge(G_ready, FT // 2 + 4)
            for u in SPAN["odo"]:
                project(u, Ghi, Glo)
            feed_forward(1)
            sum_squares(F["last"])

            for k4 in range(2):
                pe.wait_ge(norm_done, 2 + k4)
                for t in range(NT):
                    n = 2 * k4 + t
                    if n >= 2:
                        pe.wait_ge(out_kept, n - 1)
                    for q in range(4):
                        k = 4 * k4 + q
                        last = nc.tensor.transpose(token_bank(n)[:, q * P:(q + 1) * P], xT[:, k, t * P:(t + 1) * P],
                                                   ident[:, :])
                    last.then_inc(out_turned, 1)

        @block.scalar
        def _(act):
            steps = [0]
            half_at = [0]

            def step(ins):
                steps[0] += 1
                ins.then_inc(acts, 1)
                act.wait_ge(acts, steps[0])

            def split_through(u):
                while half_at[0] < H0[u] + NH[u]:
                    h = half_at[0]
                    v = next(w for w in split_order if H0[w] <= h < H0[w] + NH[w])
                    i = h - H0[v]
                    if i == 0:
                        act.wait_ge(raw_landed[v % RAW], LANDED[v])
                    if h >= WRING:
                        act.wait_ge(half_used, h - WRING + 1)
                    src, _ = raw_half(v, i)
                    nc.scalar.copy(ring_half(whi, v, i), src).then_inc(hi_split, 1)
                    half_at[0] += 1

            def ahead(u):
                if u in after:
                    split_through(after[u])

            def keep(u, dst, scale=None, free=True):
                act.wait_ge(half_used, H0[u] + NH[u])
                src = bank(u)
                nc.scalar.activation(dst, src.rearrange("p (a b) -> p a b", a=2), ACT.Copy,
                                     scale=1.0 if scale is None else scale).then_inc(bank_free[B0[u] % 2], 1)
                act.wait_ge(bank_free[B0[u] % 2], B0[u] // 2 + 1)
                act.sem_inc(kept, 1)

            for rows, at, n in PAR_FIRST[1::2]:
                act.dma_start(prow[at % P:at % P + n, at // P, :], rows).then_inc(par_in, 16)
            nc.scalar.preload_act_table_set(TABLES)
            ctxv = ctx_2.rearrange("b (t p) d -> p (b t) d", p=P)
            def turn_keep(i, g, dst):
                act.wait_ge(turned, 4 * i + g + 1)
                nc.scalar.copy(dst, token_bank(g).rearrange("p (a b) -> p a b", a=2)).then_inc(turned_kept, 1)
                act.wait_ge(turned_kept, 4 * i + g + 1)

            def norm(i, src, e):
                norm_squares(src)
                inverse(i)

            def norm_squares(src):
                for g in range(4):
                    nc.scalar.activation(sqv[:, 2 * g:2 * g + 2, :], src[:, 2 * g:2 * g + 2, :], ACT.Square
                                         ).then_inc(squares, 1)

            def highs(i, shift=None, out_=Hhi, tiles=range(KT)):
                n0 = KT * (H_COUNT[i] - 1)
                for k in tiles:
                    act.wait_ge(v_set, n0 + k + 1)
                    if shift is None:
                        ins = nc.scalar.copy(out_[:, k, :], VALUE[k % 3])
                    else:
                        ins = nc.scalar.activation(out_[:, k, :], VALUE[k % 3], ACT.Identity,
                                                   bias=shift[:, k:k + 1])
                    ins.then_inc(vhi_set, 1)

            def inverse(i):
                act.wait_ge(sums, i + 1)
                step(nc.scalar.activation(rn[:, 0, :], psY[:, 0:S], ACT.Ln, bias=eps[:, 0:1], scale=1.0 / D))
                nc.scalar.activation(rn[:, 1, :], rn[:, 0, :], ACT.Exp, scale=-0.5).then_inc(rms_inv, 1)
                act.wait_ge(rms_inv, i + 1)

            act.wait_ge(ones_set, 1)
            act.wait_ge(tok_in, 16 * NT)
            for t in range(NT):
                step(nc.scalar.activation(adat0[:, :], tok[:, t, :], ACT.Square, accum_out=stat[:, 0, t:t + 1]))
                step(nc.scalar.activation(stat[:, 1, t:t + 1], stat[:, 0, t:t + 1], ACT.Ln, bias=eps[:, 0:1],
                                          scale=1.0 / D))
                nc.scalar.activation(stat[:, 2, t:t + 1], stat[:, 1, t:t + 1], ACT.Exp, scale=-0.5).then_inc(h1_inv, 1)
            split_through(0)
            act.wait_ge(c_exp, 1)
            for k in range(KT):
                if k % 4 == 0:
                    act.wait_ge(xn_turned, k // 4 + 1)
                if k >= 4:
                    act.wait_ge(H_ready, k - 3)
                nc.scalar.activation(FIRST[k % 4].rearrange("p (t n) -> p t n", t=NT),
                                     psS[:, 2 * (k // 4):2 * (k // 4) + 2, (k % 4) * P:(k % 4 + 1) * P], ACT.Identity,
                                     scale=pcol[:, C_NG + k:C_NG + k + 1]).then_inc(v_set, 1)
            nc.scalar.activation(cse[:, :], pcol[:, C_C:C_C + 16], ACT.Exp, scale=-1.0).then_inc(c_exp, 1)

            def keep_first(u):
                name = next(n for n in ("qa", "ka", "va", "qb", "kvb", "qc", "kc", "vc") if u in SPAN[n])
                n = SPAN[name].index(u)
                if name == "kvb":
                    act.wait_ge(half_used, H0[u] + NH[u])
                    nc.scalar.copy(kbT[:, :], bank(u)[:, 0:S])
                    nc.scalar.copy(vb[:, :, :], bank(u)[:, S:512].rearrange("p (a b) -> p a b", a=2)
                                   ).then_inc(bank_free[B0[u] % 2], 1)
                    act.wait_ge(bank_free[B0[u] % 2], B0[u] // 2 + 1)
                    act.sem_inc(kept, 1)
                elif name in ("va", "vc"):
                    keep(u, {"va": va, "vc": vc}[name][:, :, n * 256:(n + 1) * 256])
                else:
                    dst = {"qa": qaT, "ka": kaT, "qb": qbT, "qc": qcT, "kc": kcT}[name]
                    keep(u, dst[:, 2 * n:2 * n + 2, :], SCALE if name[0] == "q" else None)

            def keep_values(name, dst):
                for n, u in enumerate(SPAN[name]):
                    ahead(u)
                    keep(u, dst[:, :, n * 256:(n + 1) * 256])

            for name, i in BEFORE:
                ahead(SPAN[name][i])
                keep_first(SPAN[name][i])
                if (name, i) == ("ka", 1):
                    act.wait_ge(small_mm, 3)
                    step(nc.scalar.activation(lamp[:, 2:4], psX[:, 0:2], ACT.Exp))
                    nc.scalar.copy(smallr[:, 8:16], psX[:, 8:16]).then_inc(small_ex, 1)
                elif name == "va":
                    for g in range(4):
                        turn_keep(0, g, xT[:, 2 * g:2 * g + 2, :])

            def keep_gate(u):
                m = 4 * "abc".index("bca"[GATES.index(u) // 2]) + 2 * (GATES.index(u) % 2)
                act.wait_ge(half_used, H0[u] + NH[u])
                nc.scalar.copy(sg[:, m:m + 2, :], bank(u).rearrange("p (a b) -> p a b", a=2)
                               ).then_inc(bank_free[B0[u] % 2], 1)
                act.wait_ge(bank_free[B0[u] % 2], B0[u] // 2 + 1)

            def sigmoids(n):
                b = n % 3
                if n == 3:
                    act.wait_ge(gated, 1)
                elif n == 2:
                    act.wait_ge(forget, 1)
                nc.scalar.activation(SIG[n][:, :, :], sg[:, 4 * b:4 * b + 4, :], ACT.Sigmoid).then_inc(sig_set, 1)

            def exps(g, tiles, rows):
                act.wait_ge(biased, g + 1)
                for n, (dst, src) in enumerate(tiles):
                    ins = nc.scalar.activation(dst, src, ACT.Exp, bias=stat[:, 0 + 3 * (g % 2), n:n + 1],
                                               accum_out=stat[:, 1 + 3 * (g % 2), n:n + 1])
                if rows:
                    ins = nc.scalar.activation(stat[:, 2 + 3 * (g % 2), 0:4], stat[:, 2 + 3 * (g % 2), 0:4], ACT.Exp)
                ins.then_inc(exped, 1)
                act.wait_ge(exped, g + 1)

            def keep_y(g):
                act.wait_ge(yed, g + 1)
                nc.scalar.copy(yA[:, g, :] if g < 4 else YBC[g // 4][:, g % 4, :], psY[:, 0:S]).then_inc(y_kept, 1)
                act.wait_ge(y_kept, g + 1)

            YBC = (None, kaT, qaT)

            def high_of(b):
                act.wait_ge(gated, b)
                nc.scalar.copy(Mhi[:, 4 * b:4 * b + 4, :], sg[:, 4 * b:4 * b + 4, :]).then_inc(M_high, 1)

            for s, fill in enumerate(SLOT):
                ahead(fill[0])
                if s >= 3:
                    keep_y(s - 3)
                if s == 7:
                    nc.scalar.activation(sqv[:, 0:4, :], yA[:, :, :], ACT.Square).then_inc(sub_sq, 1)
                if s in (8, 9):
                    act.wait_ge(sub_sum, s - 7)
                    nc.scalar.activation(headr[:, s - 8, :], psX[:, :], ACT.Ln, bias=eps[:, 1:2], scale=1.0 / P
                                         ).then_inc(sub_taken, 1)
                    act.wait_ge(sub_taken, s - 7)
                if s == 9:
                    nc.scalar.activation(headr[:, :, :], headr[:, :, :], ACT.Exp, scale=-0.5).then_inc(sub_inv, 1)
                if s >= 2:
                    g = s - 2
                    for i in range(TSETS[g]):
                        n = T0[g] + i
                        act.wait_ge(turnedP, n + 1)
                        if g >= 2 and i == 0:
                            act.wait_ge(yed, g - 1)
                        nc.scalar.copy(pT[:, g % 2, i, :], psX[:, 0:384]).then_inc(pT_kept, 1)
                        act.wait_ge(pT_kept, n + 1)
                if s < NG:
                    exps(s, [(pr[:, s % 2, i, COLS[t][0]:COLS[t][1]],
                              psS[:, 2 * (s % 2) + i, COLS[t][0]:COLS[t][1]]) for i in range(2) for t in range(2)],
                         GROUPS[s][0] == "B")
                if s == 7:
                    act.wait_ge(forget_a, 1)
                    step(nc.scalar.activation(fcw[:, 1, :], fcw[:, 1, :], ACT.Exp, scale=-1.0))
                    nc.scalar.activation(fcw[:, 1, :], fcw[:, 1, :], ACT.Ln, bias=ones[0:8, 0:1]
                                         ).then_inc(forget_a, 1)
                if s == 12:
                    sigmoids(1)
                elif s == 13:
                    sigmoids(2)
                    high_of(1)
                for i, u in enumerate(fill):
                    if i:
                        ahead(u)
                    if u in GATES:
                        keep_gate(u)
                    elif UNITS[u][0] != "C":
                        keep_first(u)
            ahead(SPAN["gm_b0"][0])
            sigmoids(3)
            keep_y(NG - 1)
            high_of(2)

            split_through(SPAN["gm_b0"][0])
            n = 0
            for i in range(4):
                for br in "bca":
                    u = SPAN[f"gm_{br}{i}"][0]
                    ahead(u)
                    ahead(SPAN[f"up_{br}{i}"][0])
                    act.wait_ge(half_used, H0[u] + NH[u])
                    if n >= 2:
                        act.wait_ge(gate_used, n - 1)
                    nc.scalar.activation(gate[:, n % 2, :, :], bank(u).rearrange("p (a b) -> p a b", a=2),
                                         ACT.Sigmoid).then_inc(bank_free[B0[u] % 2], 1)
                    act.wait_ge(bank_free[B0[u] % 2], B0[u] // 2 + 1)
                    act.sem_inc(gate_e, 1)
                    n += 1
                if i == 0:
                    act.wait_ge(M_ready, 3)
                    for t in range(NT):
                        act.dma_start(tok[:, t, :], ctxv[:, t, :]).then_inc(tok_in, 16)
                elif i == 1:
                    for g in range(4):
                        turn_keep(1, g, cxT[:, 2 * g:2 * g + 2, :])
                elif i == 2:
                    nc.scalar.preload_act_table_set(TABLES)
                    norm(F["ctx"], cxT, None)
            nc.scalar.preload_act_table_set(TABLES)
            for n, u in enumerate(SPAN["wo"]):
                ahead(u)
                if n == 0:
                    highs("ctx", mod[:, 0, 0:8, 1])
            for g in range(4):
                act.wait_ge(x_ready, g + 1)
                nc.scalar.activation(sqv[:, 2 * g:2 * g + 2, :], xT[:, 2 * g:2 * g + 2, :], ACT.Square
                                     ).then_inc(squares, 1)
            act.wait_ge(lb_e, 1)
            nc.scalar.activation(lbc[:, 0, :], lbc[:, 0, :], ACT.Exp).then_inc(lb_e, 1)

            def gate_sigmoid(u, n):
                act.wait_ge(half_used, H0[u] + NH[u])
                if n:
                    act.wait_ge(f_set, n)
                nc.scalar.activation(hgt[:, :, :], bank(u).rearrange("p (a b) -> p a b", a=2), ACT.Sigmoid
                                     ).then_inc(bank_free[B0[u] % 2], 1)
                act.wait_ge(bank_free[B0[u] % 2], B0[u] // 2 + 1)
                act.sem_inc(f_e, 1)

            for n, u in enumerate(SPAN["chf"] + SPAN["chb"]):
                ahead(u)
                if n == 0:
                    act.wait_ge(H_ready, 2 * KT)
                    inverse(F["fin1"])
                gate_sigmoid(u, n)
            nc.scalar.preload_act_table_set(TABLES)
            act.wait_ge(norm_done, 1)
            norm_squares(xT)
            for n, u in enumerate(SPAN["cnk"]):
                ahead(u)
                keep(u, cnk[:, 2 * n:2 * n + 2, :])
                if n == 0:
                    act.wait_ge(f_set, 4)
                    nc.scalar.activation(lg[:, :, :, :], lg[:, :, :, :], ACT.Ln).then_inc(f_ln, 1)
                    inverse(F["mix0"])
            for n, u in enumerate(SPAN["cnv"] + SPAN["chi"]):
                ahead(u)
                if n < 2:
                    highs("mix0", mod[:, 0, 0:8, 0], Xhi, range(4 * n, 4 * n + 4))
                keep(u, (cnv if n < 2 else hv)[:, :, n % 2 * 256:(n % 2 + 1) * 256])

            def ctx_decay(d):
                act.wait_ge(f_cum, d + 1)
                if d:
                    act.wait_ge(kd_turned, 1)
                for j in range(4):
                    tot = lg[:, d, j, S - 1:S] if d == 0 else lg[:, d, j, 0:1]
                    ins = nc.scalar.activation(kd[:, j, :], lg[:, d, j, :], ACT.Exp, bias=tot, scale=-1.0)
                ins.then_inc(f_exp, 1)

            def keep_ctx_keys(d):
                act.wait_ge(kd_turned, d + 1)
                if d:
                    act.wait_ge(ctx_state, 1)
                for i, b in enumerate((psX, psY)):
                    ins = nc.scalar.copy(kdc[:, 2 * i:2 * i + 2, :, :],
                                         b[:, :].rearrange("p (h t n) -> p h t n", h=2, t=NT))
                ins.then_inc(kd_kept, 1)

            def keep_states(d):
                act.wait_ge(ctx_state, d + 1)
                nc.scalar.copy(sctx[:, d, :, :], psY[:, :].rearrange("p (h n) -> p h n", h=4)).then_inc(ctx_kept, 1)

            ctx_decay(0)
            for name, i in (("nq", 0), ("nq", 1), ("nk", 0), ("nk", 1)):
                u = SPAN[name][i]
                ahead(u)
                if (name, i) == ("nk", 0):
                    keep_ctx_keys(0)
                    ctx_decay(1)
                elif (name, i) == ("nk", 1):
                    keep_states(0)
                keep(u, (naq if name == "nq" else nak)[:, 2 * i:2 * i + 2, :], SCALE if name == "nq" else None)
            keep_ctx_keys(1)
            for n, u in enumerate(SPAN["hf"] + SPAN["hb"] + SPAN["hq"]):
                ahead(u)
                if n < 4:
                    gate_sigmoid(u, 4 + n)
                else:
                    if n == 4:
                        act.wait_ge(f_set, 8)
                    else:
                        act.wait_ge(bank_free[B0[u - 1] % 2], B0[u - 1] // 2 + 1)
                    act.wait_ge(half_used, H0[u] + NH[u])
                    nc.scalar.activation(hgt[:, :, :], bank(u).rearrange("p (a b) -> p a b", a=2), ACT.Sigmoid
                                         ).then_inc(silu_e, 1)
                if n == 0:
                    keep_states(1)

            nc.scalar.preload_act_table_set(TABLES)

            def hg_exps(n):
                d = 1 - n
                act.wait_ge(f_cum, 3 + n)
                nc.scalar.activation(QE[d][:, :, :], lg[:, d, :, :], ACT.Exp)
                nc.scalar.activation(KE[d][:, :, :], lg[:, d, :, :], ACT.Exp, scale=-1.0)
                nc.scalar.activation(KD[d][:, :, :], KD[d][:, :, :], ACT.Exp).then_inc(f_exp, 1)

            for s, u in enumerate(SLOT2):
                if u is not None:
                    ahead(u)
                if s >= 2:
                    h = s - 2
                    for t in range(NT):
                        n = 2 * h + t
                        act.wait_ge(turnedP, NT0 + n + 1)
                        if h >= 2 and t == 0:
                            act.wait_ge(yed, NG + h - 1)
                        nc.scalar.copy(pnT[:, n % 4, :], psX[:, :]).then_inc(pT_kept, 1)
                        act.wait_ge(pT_kept, NT0 + n + 1)
                if s < 8:
                    if s == 0:
                        act.wait_ge(nb_set, 1)
                    exps(NG + s, [(pn[:, s % 2, t, :], psS[:, 2 * (s % 2) + t, :]) for t in range(NT)], False)
                if s < 2:
                    keep(u, nav[:, :, s * 256:(s + 1) * 256])
                elif s < 4:
                    keep(u, hv[:, :, (s - 2) * 256:(s - 1) * 256])
                elif s < 6:
                    act.wait_ge(half_used, H0[u] + NH[u])
                    nc.scalar.copy(sgh[:, 2 * (s - 4):2 * (s - 4) + 2, :], bank(u).rearrange("p (a b) -> p a b", a=2)
                                   ).then_inc(bank_free[B0[u] % 2], 1)
                    act.wait_ge(bank_free[B0[u] % 2], B0[u] // 2 + 1)
                if s == 1:
                    act.wait_ge(f_set, 8)
                    nc.scalar.activation(lg[:, :, :, :], lg[:, :, :, :], ACT.Ln).then_inc(f_ln, 1)
                elif s == 6:
                    hg_exps(0)
                elif s == 8:
                    nc.scalar.activation(hov[:, 3], sgh[:, :, :], ACT.Sigmoid).then_inc(silu_e, 1)
                    nc.scalar.preload_act_table_set(TABLES)

            for n in range(8):
                j = n % 4
                if n == 1:
                    hg_exps(1)
                if n:
                    act.wait_ge(kv_done, n)
                else:
                    act.wait_ge(masks_set, 1)
                for c in range(4):
                    a = slice(c * CH, (c + 1) * CH)
                    ins = nc.scalar.copy(vbd[a, :, c, :], hv[a, :, j * P:(j + 1) * P])
                ins.then_inc(vbd_set, 1)
                act.wait_ge(kd_turned, 2 + n + 1)
                nc.scalar.copy(kdt[:, :, :], psX[:, 0:S].rearrange("p (a b) -> p a b", a=2)).then_inc(kd_kept, 1)
            ahead(SPAN["evoA"][2])
            act.wait_ge(o_kept, 8)
            nc.scalar.activation(kd[:, :, :], oT[:, :, :], ACT.Square).then_inc(sub_sq, 1)
            act.wait_ge(sub_sum, 3)
            step(nc.scalar.activation(headr2, psS[:, 2:4, :], ACT.Ln, bias=eps[:, 0:1], scale=1.0 / P))
            nc.scalar.activation(headr2, headr2, ACT.Exp, scale=-0.5).then_inc(sub_inv, 1)
            for u in SPAN["evoA"] + SPAN["evoB"]:
                ahead(u)

            def squares_of_x(i):
                for g in range(4):
                    act.wait_ge(x_ready, XR[i] + g + 1)
                    nc.scalar.activation(sqv[:, 2 * g:2 * g + 2, :], xT[:, 2 * g:2 * g + 2, :], ACT.Square
                                         ).then_inc(squares, 1)
                inverse(F[i])


            def conv_centre(src, n, w, b, z):
                for q in range(2):
                    ins = nc.scalar.activation(z[:, q, :], src[:, q, :], ACT.Identity, scale=pcol[:, w + q:w + q + 1],
                                               bias=pcol[:, b + q:b + q + 1])
                    if q == 0:
                        step(ins)
                ins.then_inc(conv_a, 1)
                act.wait_ge(conv_a, n + 1)

            def feed_forward(layer):
                squares_of_x(f"ffn{layer}")
                highs(f"ffn{layer}", mod[:, layer, 24:32, 0])
                n0 = (FT // 2 + 4) * layer
                for i in range(FT // 2):
                    ua, uv = SPAN[f"fa{layer}.{i}"][0], SPAN[f"fv{layer}.{i}"][0]
                    ahead(ua)
                    act.wait_ge(half_used, H0[ua] + NH[ua])
                    if i >= 2:
                        act.wait_ge(G_ready, n0 + i - 1)
                    src = bank(ua).rearrange("p (a b) -> p a b", a=2)
                    nc.scalar.copy(fa[:, i % 2, :, :], src).then_inc(bank_free[B0[ua] % 2], 1)
                    act.wait_ge(bank_free[B0[ua] % 2], B0[ua] // 2 + 1)
                    conv_centre(fa[:, i % 2, :, :], n0 + i, C_FCW + P * layer + FT + 2 * i,
                                C_FCB + P * layer + 2 * i, fz[:, i % 2, :, :])
                    ahead(uv)
                    act.wait_ge(gelu_in, FT // 2 * layer + i + 1)
                    nc.scalar.activation(fz[:, i % 2, :, :], fz[:, i % 2, :, :], ACT.Gelu).then_inc(gelu_out, 1)
                    act.wait_ge(gelu_out, FT // 2 * layer + i + 1)
                for i in range(FT // 2):
                    ahead(SPAN[f"fd{layer}.{i}"][0])

            feed_forward(0)
            nc.scalar.preload_act_table_set(TABLES)
            squares_of_x("mix1")
            highs("mix1", mod[:, 1, 0:8, 0])
            for i in range(4):
                uc, uu, ub = [SPAN[f"od{q}{i}"][0] for q in "cub"]
                n = FT // 2 + i
                ahead(uc)
                act.wait_ge(half_used, H0[uc] + NH[uc])
                if i >= 2:
                    act.wait_ge(G_ready, n - 1)
                nc.scalar.copy(fa[:, i % 2, :, :], bank(uc).rearrange("p (a b) -> p a b", a=2)
                               ).then_inc(bank_free[B0[uc] % 2], 1)
                act.wait_ge(bank_free[B0[uc] % 2], B0[uc] // 2 + 1)
                act.sem_inc(c_kept, 1)
                ahead(uu)
                act.wait_ge(cu_set, i + 1)
                conv_centre(fa[:, i % 2, :, :], n, C_ODW + 8 + 2 * i, C_ODB + 2 * i, fz[:, i % 2, :, :])
                ahead(ub)
            for u in SPAN["odo"]:
                ahead(u)
            feed_forward(1)
            nc.scalar.preload_act_table_set(TABLES)
            squares_of_x("last")

            for k4 in range(2):
                for t in range(NT):
                    n = 2 * k4 + t
                    act.wait_ge(out_turned, n + 1)
                    nc.scalar.copy(tok[:, t, k4 * 512:(k4 + 1) * 512], token_bank(n)).then_inc(out_kept, 1)

        @block.vector
        def _(dve):
            steps = [0]
            half_at = [0]
            V = nc.vector

            def step(ins):
                steps[0] += 1
                ins.then_inc(dves, 1)
                dve.wait_ge(dves, steps[0])

            def then(ins, s, n):
                ins.then_inc(s, 1)
                dve.wait_ge(s, n)

            def split_through(u):
                while half_at[0] < H0[u] + NH[u]:
                    h = half_at[0]
                    v = next(w for w in split_order if H0[w] <= h < H0[w] + NH[w])
                    dve.wait_ge(hi_split, h + 1)
                    src, _ = raw_half(v, h - H0[v])
                    V.tensor_tensor(ring_half(wlo, v, h - H0[v]), src, ring_half(whi, v, h - H0[v]).bitcast(F32),
                                    ALU.subtract).then_inc(lo_split, 1)
                    half_at[0] += 1

            def ahead(u):
                if u in after:
                    split_through(after[u])

            def split_value(v, hi, lo, s, n):
                step(V.tensor_copy(hi, v))
                then(V.tensor_tensor(lo, v, hi.bitcast(F32), ALU.subtract), s, n)

            V.memset(eps[:, 0:1], EPS)
            V.memset(eps[:, 1:2], SUBLN_EPS)
            then(V.memset(ones[:, :], 1.0), ones_set, 1)
            for t in range(NT):
                dve.wait_ge(h1_inv, t + 1)
                V.tensor_scalar(xn[:, t, :], tok[:, t, :], stat[:, 2, t:t + 1], None, ALU.mult).then_inc(xn_set, 1)
            dve.wait_ge(small_mm, 1)
            then(V.tensor_copy(pcol[:, 0:125], psX[:, 0:125]), small_ev, 1)
            dve.sem_inc(c_exp, 1)
            split_through(0)
            for k in range(KT):
                dve.wait_ge(v_set, k + 1)
                step(V.tensor_copy(Hhi[:, k, :], FIRST[k % 4]))
                then(V.tensor_tensor(Hlo[:, k, :], FIRST[k % 4], Hhi[:, k, :].bitcast(F32), ALU.subtract),
                     H_ready, k + 1)

            ada_at = [0]

            def keep_ada(limit):
                while ada_at[0] < limit:
                    n = ada_at[0]
                    layer, s, who = ACCS[n]
                    c = C_ADAB + 48 * layer + 8 * s
                    dve.wait_ge(acc_summed, n + 1)
                    then(V.tensor_tensor(mod[:, layer, 8 * s:8 * s + 8, who], ada_bank(n), pcol[:, c:c + 8], ALU.add),
                         ada_kept, n + 1)
                    ada_at[0] += 1

            def normed(i, src, g0, shift=None, hi=Hhi, lo=Hlo, tiles=range(KT)):
                dve.wait_ge(rms_inv, F[i] + 1)
                n0 = KT * (H_COUNT[i] - 1)
                for k in range(tiles[0], tiles[-1] + 2):
                    if k in tiles:
                        if k >= 3:
                            dve.wait_ge(H_ready, n0 + k - 2)
                        V.scalar_tensor_tensor(VALUE[k % 3], src[:, k, :], g0[:, k:k + 1], rn[:, 1, :],
                                               ALU.mult, ALU.mult).then_inc(v_set, 1)
                    if k > tiles[0]:
                        m = k - 1
                        dve.wait_ge(vhi_set, n0 - KT + m + 1)
                        if shift is None:
                            ins = V.tensor_tensor(lo[:, m, :], VALUE[m % 3], hi[:, m, :].bitcast(F32),
                                                  ALU.subtract)
                        else:
                            ins = V.scalar_tensor_tensor(lo[:, m, :], VALUE[m % 3], shift[:, m:m + 1],
                                                         hi[:, m, :].bitcast(F32), ALU.add, ALU.subtract)
                        ins.then_inc(H_ready, 1)
                dve.wait_ge(H_ready, n0 + tiles[-1] + 1)

            dve.wait_ge(c_exp, 2)
            step(V.tensor_scalar(cse[:, :], cse[:, :], 1.0, None, ALU.add))
            step(V.reciprocal(cse[:, :], cse[:, :]))
            for i in range(2):
                step(V.tensor_tensor(cs[:, :, i], cse[:, 8 * i:8 * i + 8], pcol[:, C_C + 8 * i:C_C + 8 * i + 8],
                                     ALU.mult))
            dve.sem_inc(c_silu, 1)

            for name, i in BEFORE:
                for u in [SPAN[name][i]]:
                    ahead(u)
                    if u == 0:
                        dve.wait_ge(small_mm, 2)
                        for t, rows in ((1, 96), (2, 88), (3, 88)):
                            ins = V.tensor_copy(pcol[:, t * P:t * P + rows], psX[:, t * P:t * P + rows])
                        then(ins, small_ev, 2)
                        dve.wait_ge(consts, 1)
                        step(V.tensor_copy(dist[:, :], distI[:, :]))
                        step(V.tensor_copy(distw[:, :], distI[:, :]))
                        step(V.memset(cmask[:, :], 0.0))
                        dve.sem_inc(consts, 1)
                        dve.wait_ge(misc_in, 16 * MISC)
                        then(V.tensor_tensor(lamp[0:HD, 0:2], lam4[:, 0:4:2], lam4[:, 1:4:2], ALU.mult), small_ev, 3)
                if (name, i) == ("ka", 1):
                    dve.wait_ge(small_ex, 1)
                    step(V.tensor_tensor(lamp[:, 4:5], lamp[:, 3:4], lamp[:, 2:3], ALU.subtract))
                    step(V.tensor_scalar(lamp[:, 5:6], lamp[:, 4:5], -LAM_INIT, None, ALU.add))
                    step(V.tensor_scalar(lamp[:, 6:7], pcol[:, C_SUB:C_SUB + 1], 1.0 - LAM_INIT, None, ALU.mult))
                    for t in range(2):
                        step(V.tensor_copy(sinkb[:, :, :, t], smallr[:, 8:16].rearrange("p (i j) -> p j i", i=2)))
            def forget_log():
                u = SPAN["fc"][0]
                dve.wait_ge(half_used, H0[u] + NH[u])
                then(V.tensor_scalar(fcw[:, 0, :], bank(u)[0:8, 0:S], bfc[:, 0:1], None, ALU.add),
                     bank_free[B0[u] % 2], B0[u] // 2 + 1)
                then(V.scalar_tensor_tensor(fcw[:, 1, :], fcw[:, 0, :], -1.0, fcw[:, 0, :], ALU.mult, ALU.max),
                     forget_a, 1)
                step(V.tensor_scalar(fcw[:, 0, :], fcw[:, 0, :], 0.0, None, ALU.min))
                dve.wait_ge(forget_a, 2)
                step(V.tensor_tensor(fcw[:, 1, :], fcw[:, 1, :], fcw[:, 0, :], ALU.subtract))
                then(V.tensor_tensor_scan(negc[:, :], ones[0:8, 0:S], fcw[:, 1, :], 0.0, ALU.mult, ALU.add), forget, 1)

            def gate_first(n):
                b = n % 3
                v = sg[:, 4 * b:4 * b + 4, :]
                dve.wait_ge(sig_set, n)
                ins = V.tensor_tensor(v, v, SIG[n][:, :, :], ALU.mult)
                if b:
                    step(ins)
                    dve.wait_ge(y_kept, 4 * b + 4)
                    ins = V.tensor_tensor(v, v, (None, kaT, qaT)[b][:, :, :], ALU.mult)
                then(ins, gated, n)

            SLOPE_A = [2.0 ** (-8.0 * (h + 1) / 4) for h in range(4)]
            SLOPE_B = [2.0 ** (-8.0 * (h + 1) / 8) for h in range(8)]
            def bias_max(g):
                br, j = GROUPS[g]
                st = 3 * (g % 2)
                dve.wait_ge(scored, g + 1)
                if g == 4:
                    dve.wait_ge(consts, 3)
                if g == 0:
                    dve.wait_ge(consts, 3)
                for i in range(2):
                    o = psS[:, 2 * (g % 2) + i, 0:384]
                    if br == "A":
                        ins = V.scalar_tensor_tensor(o, dist[:, :], -SLOPE_A[j], o, ALU.mult, ALU.add)
                    elif br == "B":
                        ins = V.scalar_tensor_tensor(o, distw[:, :], -SLOPE_B[j + 4 * i], o, ALU.mult, ALU.add)
                    else:
                        ins = V.tensor_tensor(o, o, cmask[:, :], ALU.add)
                step(ins)
                for t in range(2):
                    ins = V.tensor_reduce(stat[:, st, t:4:2], psS[:, 2 * (g % 2):2 * (g % 2) + 2, COLS[t][0]:COLS[t][1]],
                                          AX.X, ALU.max, negate=(br != "B"))
                if br == "B":
                    step(ins)
                if br == "B":
                    sk = sinkb[:, j, :, :].rearrange("p i t -> p (i t)")
                    step(V.tensor_tensor(stat[:, st, :], stat[:, st, :], sk, ALU.max))
                    step(V.tensor_scalar(stat[:, st, :], stat[:, st, :], -1.0, None, ALU.mult))
                    ins = V.tensor_tensor(stat[:, st + 2, :], sk, stat[:, st, :], ALU.add)
                then(ins, biased, g + 1)

            def normalise(g):
                br, j = GROUPS[g]
                st = 3 * (g % 2)
                dve.wait_ge(exped, g + 1)
                if br == "B":
                    step(V.tensor_tensor(stat[:, st + 1, :], stat[:, st + 1, :], stat[:, st + 2, :], ALU.add))
                step(V.reciprocal(stat[:, st + 1, :], stat[:, st + 1, :]))
                if br == "A":
                    step(V.tensor_scalar(stat[:, st + 1, 2:4], stat[:, st + 1, 2:4], lamp[:, 5:6], None, ALU.mult))
                for i in range(2):
                    for t in range(2):
                        a, b = COLS[t]
                        v = pr[:, g % 2, i, a:b]
                        if br == "A" and i == 1:
                            ins = V.scalar_tensor_tensor(pr[:, g % 2, 0, a:b], v, stat[:, st + 1, 2 + t:3 + t],
                                                         pr[:, g % 2, 0, a:b], ALU.mult, ALU.add)
                        else:
                            ins = V.tensor_scalar(v, v, stat[:, st + 1, 2 * i + t:2 * i + t + 1], None, ALU.mult)
                    if i == 0 and br == "A":
                        step(ins)
                then(ins, probs, g + 1)

            def low_of(b):
                dve.wait_ge(M_high, b)
                then(V.tensor_tensor(Mlo[:, 4 * b:4 * b + 4, :], sg[:, 4 * b:4 * b + 4, :],
                                     Mhi[:, 4 * b:4 * b + 4, :].bitcast(F32), ALU.subtract), M_ready, b)

            for s, fill in enumerate(SLOT):
                if s < NG:
                    bias_max(s)
                ahead(fill[0])
                if 1 <= s <= NG:
                    normalise(s - 1)
                if s == 13:
                    gate_first(1)
                    low_of(1)
                if s == 7:
                    forget_log()
                for u in fill[1:]:
                    ahead(u)
                if s in SUM_AT:
                    keep_ada(SUM_AT[s] + 1)
            ahead(SPAN["gm_b0"][0])
            gate_first(2)
            low_of(2)
            gate_first(3)
            ahead(SPAN["up_b0"][0])
            dve.wait_ge(sub_inv, 1)
            for i in range(2):
                v = yA[:, 2 * i:2 * i + 2, :]
                step(V.scalar_tensor_tensor(v, v, lamp[:, 6:7], headr[:, i, :].rearrange("p (a b) -> p a b", a=2),
                                            ALU.mult, ALU.mult))
                step(V.tensor_tensor(v, v, sg[:, 2 * i:2 * i + 2, :], ALU.mult))
            step(V.tensor_copy(Mhi[:, 0:4, :], yA[:, :, :]))
            then(V.tensor_tensor(Mlo[:, 0:4, :], yA[:, :, :], Mhi[:, 0:4, :].bitcast(F32), ALU.subtract), M_ready, 3)

            n = 0
            for i in range(4):
                for b, br in enumerate("bca"):
                    ug, u = SPAN[f"gm_{br}{i}"][0], SPAN[f"up_{br}{i}"][0]
                    ahead(ug)
                    ahead(u)
                    dve.wait_ge(gate_e, n + 1)
                    v = gate[:, n % 2, :, :]
                    dve.wait_ge(half_used, H0[u] + NH[u])
                    dst = merged if b == 0 else mt
                    then(V.tensor_tensor(dst[:, :, :], v, bank(u).rearrange("p (a b) -> p a b", a=2), ALU.mult),
                         bank_free[B0[u] % 2], B0[u] // 2 + 1)
                    dve.sem_inc(gate_used, 1)
                    if b:
                        step(V.tensor_tensor(merged[:, :, :], merged[:, :, :], mt[:, :, :], ALU.add))
                    n += 1
                    if b == 0:
                        keep_ada((4, 5, 5, 6)[i])
                split_value(merged[:, :, :], Whi[:, 2 * i:2 * i + 2, :], Wlo[:, 2 * i:2 * i + 2, :],
                            merge_ready, i + 1)
            for m in range(2):
                step(V.scalar_tensor_tensor(cm[:, m, :], mod[:, 0, 8:16, 1 - m], 1.0, pcol[:, C_MIX:C_MIX + 8],
                                            ALU.add, ALU.mult))
            for n, u in enumerate(SPAN["wo"]):
                ahead(u)
                if n == 0:
                    u = SPAN["gm_a3"][0]
                    dve.wait_ge(half_used, H0[u] + NH[u])
                    normed("ctx", cxT, cm[:, 0, :], mod[:, 0, 0:8, 1])
                    keep_ada(7)
                    u = SPAN["wo"][0]
                dve.wait_ge(half_used, H0[u] + NH[u])
                v = xT[:, 2 * n:2 * n + 2, :]
                then(V.tensor_tensor(v, v, bank(u).rearrange("p (a b) -> p a b", a=2), ALU.add),
                     bank_free[B0[u] % 2], B0[u] // 2 + 1)
                dve.sem_inc(x_ready, 1)

            def renorm(i, gain, n):
                dve.wait_ge(rms_inv, F[i] + 1)
                for k in range(KT):
                    ins = V.scalar_tensor_tensor(xT[:, k, :], xT[:, k, :], pcol[:, gain + k:gain + k + 1], rn[:, 1, :],
                                                 ALU.mult, ALU.mult)
                    if k == 3 and i == "last":
                        ins.then_inc(norm_done, 1)
                ins.then_inc(norm_done, 1)

            keep_ada(8)
            step(V.scalar_tensor_tensor(cm[:, 2, :], mod[:, 0, 32:40, 0], 1.0, pcol[:, C_FFN:C_FFN + 8],
                                        ALU.add, ALU.mult))
            step(V.tensor_tensor(lbc[:, 0, :], pcol[:, C_LB + 8:C_LB + 16], pcol[:, C_LB:C_LB + 8], ALU.subtract))
            dve.sem_inc(lb_e, 1)
            dve.wait_ge(lb_e, 2)
            step(V.tensor_scalar(lbc[:, 0, :], lbc[:, 0, :], 1.0, None, ALU.add))
            step(V.reciprocal(lbc[:, 1, :], lbc[:, 0, :]))
            step(V.tensor_scalar(lbc[:, 2, :], lbc[:, 1, :], -1.0, 1.0, ALU.mult, ALU.add))

            def forget_gate(i):
                d, n = i // 2 % 2, i % 2
                dve.wait_ge(f_e, i + 1)
                for q in range(2):
                    c = 4 * d + 2 * n + q
                    ins = V.tensor_scalar(lg[:, d, 2 * n + q, :], hgt[:, q, :], lbc[:, 2, c:c + 1], lbc[:, 1, c:c + 1],
                                          ALU.mult, ALU.add)
                step(ins)
                then(V.tensor_scalar(kk[:, d, 2 * n:2 * n + 2, :], lg[:, d, 2 * n:2 * n + 2, :], -1.0, 1.0,
                                     ALU.mult, ALU.add), f_set, i + 1)

            def cumulate(d, factor):
                r = slice(None, None, -1) if d else slice(None)
                for j in range(4):
                    ins = V.tensor_tensor_scan(lg[:, d, j, r], factor, lg[:, d, j, r], 0.0, ALU.mult, ALU.add)
                return ins

            for i, u in enumerate(SPAN["chf"] + SPAN["chb"]):
                ahead(u)
                if i == 1:
                    renorm("fin1", C_FG, 1)
                forget_gate(i)
            for u in SPAN["cnk"]:
                ahead(u)
            dve.wait_ge(f_ln, 1)
            for d in range(2):
                then(cumulate(d, ones[:, 0:S]), f_cum, d + 1)
            for n, u in enumerate(SPAN["cnv"] + SPAN["chi"]):
                ahead(u)
                if n < 2:
                    normed("mix0", xT, cm[:, 1, :], mod[:, 0, 0:8, 0], Xhi, Xlo, range(4 * n, 4 * n + 4))

            def decayed(d):
                dve.wait_ge(f_exp, d + 1)
                then(V.tensor_tensor(kd[:, :, :], kd[:, :, :], kk[:, d, :, :], ALU.mult), f_mul, d + 1)

            decayed(0)
            for name in ("nq", "nk"):
                for u in SPAN[name]:
                    ahead(u)
                    if u == SPAN["nk"][0]:
                        decayed(1)

            for i, u in enumerate(SPAN["hf"] + SPAN["hb"] + SPAN["hq"]):
                ahead(u)
                if i < 4:
                    forget_gate(4 + i)
                else:
                    dve.wait_ge(silu_e, i - 3)
                    then(V.tensor_tensor(hq[:, 2 * i - 8:2 * i - 6, :], hgt[:, :, :],
                                         bank(u).rearrange("p (a b) -> p a b", a=2), ALU.mult),
                         bank_free[B0[u] % 2], B0[u] // 2 + 1)

            def keep_na(j):
                dve.wait_ge(yed, NG + 2 * j + 2)
                then(V.tensor_copy(vt[:, 1, :], psY[:, 0:S]), y_kept, NG + j + 1)
                split_value(vt[:, 1, :], Hhi[:, j, :], Hlo[:, j, :], M_ready, 3 + j + 1)

            b3 = [lg[:, d, :, :].rearrange("p h (c t) -> p (h c) t", t=CH) for d in range(2)]

            def to_end(n):
                d = 1 - n
                tot = (b3[d][:, :, 0:1] if d else b3[d][:, :, CH - 1:CH]).to_broadcast([P, 4 * NCH, CH])
                then(V.tensor_tensor(KD[d][:, :, :].rearrange("p h (c t) -> p (h c) t", t=CH), tot, b3[d],
                                     ALU.subtract), f_cum, 3 + n)

            def decay_products(n):
                d = 1 - n
                dve.wait_ge(f_exp, 3 + n)
                q3 = QE[d][:, :, :].rearrange("p h (c t) -> p (h c) t", t=CH)
                step(V.tensor_copy(dec[:, d, :].rearrange("p (c o) -> p c o", o=1),
                                   q3[:, :, 0:1] if d else q3[:, :, CH - 1:CH]))
                V.tensor_tensor(KD[d][:, :, :], KD[d][:, :, :], kk[:, d, :, :], ALU.mult)
                V.tensor_tensor(KE[d][:, :, :], KE[d][:, :, :], kk[:, d, :, :], ALU.mult)
                then(V.tensor_tensor(QE[d][:, :, :], QE[d][:, :, :], hq[:, :, :], ALU.mult), f_mul, 3 + n)

            dve.wait_ge(nb_set, 1)
            for s, u in enumerate(SLOT2):
                if s < 8:
                    st = 3 * (s % 2)
                    dve.wait_ge(scored, NG + s + 1)
                    for t in range(NT):
                        o = psS[:, 2 * (s % 2) + t, 0:S].rearrange("p (a b) -> p a b", a=4)
                        ins = V.tensor_tensor(o, o, nb_head(s)[:, 2 - 2 * t:6 - 2 * t, ::-1], ALU.add)
                    step(ins)
                    then(V.tensor_reduce(stat[:, st, 0:2], psS[:, 2 * (s % 2):2 * (s % 2) + 2, :], AX.X, ALU.max,
                                         negate=True), biased, NG + s + 1)
                    if s == 7:
                        dve.sem_inc(nb_used, 1)
                if u is not None:
                    ahead(u)
                if 1 <= s <= 8:
                    h = s - 1
                    st = 3 * (h % 2)
                    dve.wait_ge(exped, NG + h + 1)
                    step(V.reciprocal(stat[:, st + 1, 0:2], stat[:, st + 1, 0:2]))
                    for t in range(NT):
                        v = pn[:, h % 2, t, :]
                        ins = V.tensor_scalar(v, v, stat[:, st + 1, t:t + 1], None, ALU.mult)
                    then(ins, probs, NG + h + 1)
                if s >= 4 and s % 2 == 0:
                    keep_na((s - 4) // 2)
                if s == 3:
                    dve.wait_ge(f_ln, 2)
                    dve.wait_ge(consts, 4)
                if s in (3, 4):
                    step(cumulate(4 - s, reset[:, :]))
                elif s == 6:
                    dve.wait_ge(half_used, H0[SPAN["hg"][1]] + 2)
                    to_end(0)
                elif s == 7:
                    decay_products(0)
                elif s == 9:
                    dve.wait_ge(silu_e, 3)
                    step(V.tensor_tensor(sgh[:, :, :], sgh[:, :, :], hov[:, 3], ALU.mult))
            keep_na(3)
            to_end(1)

            def add_gated(u, n, layer, s, ready=True):
                dve.wait_ge(half_used, H0[u] + NH[u])
                for q in range(2):
                    k = 2 * n + q
                    ins = V.scalar_tensor_tensor(xT[:, k, :], bank(u)[:, q * S:(q + 1) * S],
                                                 mod[:, layer, 8 * s + k, 0:1], xT[:, k, :], ALU.mult, ALU.add)
                    if q == 0:
                        step(ins)
                then(ins, bank_free[B0[u] % 2], B0[u] // 2 + 1)
                if ready:
                    dve.sem_inc(x_ready, 1)

            def keep_o(n):
                j = n % 4
                dve.wait_ge(o_done, n + 1)
                if n < 4:
                    ins = V.tensor_copy(oT[:, j, :], psY[:, 0:S])
                else:
                    ins = V.tensor_tensor(oT[:, j, :], oT[:, j, :], psY[:, 0:S], ALU.add)
                then(ins, o_kept, n + 1)

            dve.wait_ge(masks_set, 1)
            for n in range(8):
                d, j = 1 - n // 4, n % 4
                st = SQ[n % 2]
                dve.wait_ge(att_done, n + 1)
                if n >= 2:
                    dve.wait_ge(o_done, n - 1)
                for t in range(NT):
                    ins = V.copy_predicated(ATTM[2 * (n // 4) + n % 2][:, t, :], smask[:, d, :].bitcast(U32),
                                            psG[:, n % 2, t * P:(t + 1) * P])
                then(ins, att_set, n + 1)
                first = NCH - 1 if d else 0
                step(V.tensor_copy(st[:, first, :], sctx[:, d, j, :]))
                dve.wait_ge(kv_done, n + 1)
                order = list(range(NCH - 1, -1, -1)) if d else list(range(NCH))
                for a, b in zip(order[:-1], order[1:]):
                    step(V.scalar_tensor_tensor(st[:, b, :], st[:, a, :], dec[:, d, NCH * j + a:NCH * j + a + 1],
                                                psS[:, 2 * (n % 2) + a // 4, (a % 4) * P:(a % 4 + 1) * P],
                                                ALU.mult, ALU.add))
                dve.sem_inc(st_set, 1)
                if n:
                    keep_o(n - 1)
                if n == 1:
                    decay_products(1)
            ahead(SPAN["evoA"][2])
            keep_o(7)
            add_gated(SPAN["evoA"][0], 0, 0, 2, ready=False)
            dve.wait_ge(sub_inv, 2)
            for j in range(4):
                step(V.scalar_tensor_tensor(oT[:, j, :], oT[:, j, :], pcol[:, C_HGN + j:C_HGN + j + 1],
                                            headr2[:, j // 2, (j % 2) * S:(j % 2 + 1) * S], ALU.mult, ALU.mult))
            step(V.tensor_tensor(oT[:, :, :], oT[:, :, :], sgh[:, :, :], ALU.mult))
            step(V.tensor_copy(Hhi[:, 4:8, :], oT[:, :, :]))
            then(V.tensor_tensor(Hlo[:, 4:8, :], oT[:, :, :], Hhi[:, 4:8, :].bitcast(F32), ALU.subtract),
                 M_ready, 8)
            dve.sem_inc(core_done, 1)
            for n, u in enumerate(SPAN["evoA"][1:]):
                ahead(u)
                add_gated(u, n + 1, 0, 2, ready=False)
            for n, u in enumerate(SPAN["evoB"]):
                if n < 3:
                    ahead(u)
                add_gated(u, n, 0, 2)
            ahead(SPAN["evoB"][3])

            def conv_sides(z, src, w, n):
                dve.wait_ge(conv_a, n + 1)
                for q in range(2):
                    step(V.scalar_tensor_tensor(z[:, q, 1:S], src[:, q, 0:S - 1], pcol[:, w[0] + q:w[0] + q + 1],
                                                z[:, q, 1:S], ALU.mult, ALU.add))
                    ins = V.scalar_tensor_tensor(z[:, q, 0:S - 1], src[:, q, 1:S], pcol[:, w[1] + q:w[1] + q + 1],
                                                 z[:, q, 0:S - 1], ALU.mult, ALU.add)
                    if q == 0:
                        step(ins)
                return ins

            def gains(m, s, w):
                step(V.scalar_tensor_tensor(cm[:, m, :], mod[:, 1, 8 * s:8 * s + 8, 0], 1.0, pcol[:, w:w + 8],
                                            ALU.add, ALU.mult))

            def feed_forward(layer):
                normed(f"ffn{layer}", xT, cm[:, 2 + 2 * layer, :], mod[:, layer, 24:32, 0])
                n0 = (FT // 2 + 4) * layer
                for i in range(FT // 2):
                    ua, uv = SPAN[f"fa{layer}.{i}"][0], SPAN[f"fv{layer}.{i}"][0]
                    ahead(ua)
                    z, src = fz[:, i % 2, :, :], fa[:, i % 2, :, :]
                    c = C_FCW + P * layer + 2 * i
                    then(conv_sides(z, src, (c, c + 2 * FT), n0 + i), gelu_in, FT // 2 * layer + i + 1)
                    ahead(uv)
                    dve.wait_ge(gelu_out, FT // 2 * layer + i + 1)
                    dve.wait_ge(half_used, H0[uv] + NH[uv])
                    then(V.tensor_tensor(z, z, bank(uv).rearrange("p (a b) -> p a b", a=2), ALU.mult),
                         bank_free[B0[uv] % 2], B0[uv] // 2 + 1)
                    split_value(z, Ghi[:, 2 * i:2 * i + 2, :], Glo[:, 2 * i:2 * i + 2, :], G_ready, n0 + i + 1)
                    if layer == 0 and i in (6, 10):
                        keep_ada({6: 9, 10: 10}[i])
                for i in range(FT // 2):
                    if i < FT // 2 - 1:
                        ahead(SPAN[f"fd{layer}.{i}"][0])
                    if layer == 0 and i == 6:
                        keep_ada(11)
                        gains(3, 1, C_MIX + 8)
                u = SPAN[f"fd{layer}.{FT // 2 - 1}"][0]
                for k in range(KT):
                    if k == 6:
                        dve.wait_ge(half_used, H0[u] + NH[u])
                    elif k % 2 == 0:
                        dve.wait_ge(down_part, 3 * layer + k // 2 + 1)
                    ins = V.scalar_tensor_tensor(xT[:, k, :], psS[:, k // 2, (k % 2) * S:(k % 2 + 1) * S],
                                                 mod[:, layer, 40 + k, 0:1], xT[:, k, :], ALU.mult, ALU.add)
                    if k % 2:
                        ins.then_inc(x_ready, 1)
                ahead(u)
                dve.wait_ge(x_ready, XR[f"ffn{layer}"] + 8)

            feed_forward(0)
            normed("mix1", xT, cm[:, 3, :], mod[:, 1, 0:8, 0])
            for i in range(4):
                uc, uu, ub = [SPAN[f"od{q}{i}"][0] for q in "cub"]
                n = FT // 2 + i
                z, src = fz[:, i % 2, :, :], fa[:, i % 2, :, :]
                ahead(uc)
                ahead(uu)
                dve.wait_ge(c_kept, i + 1)
                dve.wait_ge(half_used, H0[uu] + NH[uu])
                then(V.tensor_tensor(src, src, bank(uu).rearrange("p (a b) -> p a b", a=2), ALU.mult),
                     bank_free[B0[uu] % 2], B0[uu] // 2 + 1)
                dve.sem_inc(cu_set, 1)
                ahead(ub)
                step(conv_sides(z, src, (C_ODW + 2 * i, C_ODW + 16 + 2 * i), n))
                dve.wait_ge(half_used, H0[ub] + NH[ub])
                then(V.tensor_tensor(z, z, bank(ub).rearrange("p (a b) -> p a b", a=2), ALU.mult),
                     bank_free[B0[ub] % 2], B0[ub] // 2 + 1)
                split_value(z, Ghi[:, 2 * i:2 * i + 2, :], Glo[:, 2 * i:2 * i + 2, :], G_ready, n + 1)
                if i >= 1:
                    keep_ada(11 + i)
            gains(4, 4, C_FFN + 8)
            for n, u in enumerate(SPAN["odo"]):
                if n < 3:
                    ahead(u)
                add_gated(u, n, 1, 2)
            ahead(SPAN["odo"][3])
            feed_forward(1)
            renorm("last", C_FN, 2)

        @block.gpsimd
        def _(pool):
            G = nc.gpsimd
            steps = [0]

            def step(ins):
                steps[0] += 1
                ins.then_inc(pools, 1)
                pool.wait_ge(pools, steps[0])

            step(G.memset(ident[:, :], 0.0))
            step(G.affine_select(out=ident[:, :], in_=ident[:, :], compare_op=ALU.not_equal, fill=1.0, base=0,
                                 pattern=[[-1, P]], channel_multiplier=1))
            pool.sem_inc(ident_set, 1)
            step(G.memset(sel[:, :, :], 0.0))
            step(G.affine_select(out=sel[:, :, :], in_=sel[:, :, :], compare_op=ALU.not_equal, fill=1.0, base=0,
                                 pattern=[[-1, 8], [0, P]], channel_multiplier=1))
            step(G.iota(distI[:, 0:P], pattern=[[-1, P]], base=0, channel_multiplier=1))
            step(G.iota(distI[:, P:384], pattern=[[-1, S]], base=P, channel_multiplier=1))
            pool.sem_inc(consts, 1)
            pool.wait_ge(consts, 2)
            for tile_, fill in ((dist, FAR), (distw, FAR), (cmask, -FAR)):
                for a, b, base in ((0, P, 0), (P, 384, P)):
                    step(G.affine_select(out=tile_[:, a:b], in_=tile_[:, a:b], compare_op=ALU.is_ge, fill=fill,
                                         base=base, pattern=[[-1, b - a]], channel_multiplier=1))
            step(G.affine_select(out=distw[:, P:384], in_=distw[:, P:384], compare_op=ALU.is_ge, fill=FAR,
                                 base=-1, pattern=[[1, S]], channel_multiplier=-1))
            pool.sem_inc(consts, 1)

            def ada(n0, buf, acc, tmp):
                secs = [(0, s) for s in range(6)] if n0 == 0 else [(1, s) for s in range(6)]
                chunks = [(l, s, k) for l, s in secs for k in range(KT)]
                c0 = 0 if n0 == 0 else 6 * KT

                def load(c):
                    l, s, k = chunks[c]
                    pool.dma_start(buf[:, (c0 + c) % AW, :], ada_w_2[l, k * P:(k + 1) * P, s * D:(s + 1) * D]
                                   ).then_inc(adaw_landed[(c0 + c) % AW], 16)
                for c in range(AW):
                    load(c)
                n = n0
                for c, (l, s, k) in enumerate(chunks):
                    pool.wait_ge(adaw_landed[(c0 + c) % AW], 16 * ((c0 + c) // AW + 1))
                    w = buf[:, (c0 + c) % AW, :]
                    whos = [who for a, b, who in ACCS if (a, b) == (l, s)]
                    for who in whos:
                        a = acc[:, (n + who) % 2, :]
                        sc = cs[:, k, who:who + 1]
                        if k == 0:
                            if n + who - n0 >= 2:
                                pool.wait_ge(acc_summed, n + who - 1)
                            step(G.tensor_scalar(a, w, sc, 1.0, ALU.mult, ALU.mult))
                        else:
                            step(G.tensor_scalar(tmp[:, :], w, sc, 1.0, ALU.mult, ALU.mult))
                            step(G.tensor_tensor(a, a, tmp[:, :], ALU.add))
                    if k == KT - 1:
                        pool.sem_inc(acc_ready, len(whos))
                        n += len(whos)
                    if c + AW < len(chunks):
                        load(c + AW)

            pool.wait_ge(c_silu, 1)
            ada(0, adaw0, acc0, adat0)
            pool.wait_ge(norm_done, 1)
            step(G.memset(smask[:, :, :], 1.0))
            step(G.affine_select(out=smask[:, 0, :], in_=smask[:, 0, :], compare_op=ALU.is_ge, fill=0.0, base=0,
                                 pattern=[[1, P]], channel_multiplier=-1))
            step(G.affine_select(out=smask[:, 0, :], in_=smask[:, 0, :], compare_op=ALU.is_ge, fill=0.0, base=0,
                                 pattern=[[-CH, 4], [0, CH]], channel_multiplier=1))
            step(G.affine_select(out=smask[:, 1, :], in_=smask[:, 1, :], compare_op=ALU.is_ge, fill=0.0, base=0,
                                 pattern=[[-1, P]], channel_multiplier=1))
            step(G.affine_select(out=smask[:, 1, :], in_=smask[:, 1, :], compare_op=ALU.is_ge, fill=0.0, base=CH - 1,
                                 pattern=[[CH, 4], [0, CH]], channel_multiplier=-1))
            step(G.memset(reset[:, :], 1.0))
            step(G.memset(reset[:, :].rearrange("p (c t) -> p c t", t=CH)[:, :, 0:1], 0.0))
            step(G.memset(vbd[:, :, :, :], 0.0))
            pool.sem_inc(consts, 1)
            pool.wait_ge(rms_inv, F["mix0"] + 1)
            step(G.memset(rpad, 0.0))
            pool.dma_start(rpad[:, 48:79], na_rpb_2.rearrange("a h r c -> (a h r) c")).then_inc(scr_out, 16)
            pool.wait_ge(scr_out, 16)
            step(G.memset(rrev, 0.0))
            step(G.tensor_copy(rrev[:, 0:127], rpad[:, 126::-1]))
            pool.dma_start(rscr, rrev).then_inc(scr_out, 16)
            pool.wait_ge(scr_out, 32)
            for half_ in range(2):
                for h in range(8):
                    src = bass.AP(rscr.tensor, (h * 15 + 5 - half_) * P, [[1, HD], [P, 6], [1, HD]])
                    pool.dma_start(nb_head(h)[half_ * HD:(half_ + 1) * HD, :, :], src).then_inc(nb_in, 16)
            pool.wait_ge(nb_in, 16 * 16)
            for half_ in range(2):
                a = slice(half_ * HD, (half_ + 1) * HD)
                for nb in (nbA, nbB):
                    v = nb[a, :, :, :].rearrange("p h j c -> p (h j) c")
                    m = v.shape[1]
                    step(G.affine_select(out=v[:, :, 0:48], in_=v[:, :, 0:48], compare_op=ALU.is_ge, fill=-FAR,
                                         base=7 - 63, pattern=[[0, m], [1, 48]], channel_multiplier=1))
                    step(G.affine_select(out=v[:, :, 16:64], in_=v[:, :, 16:64], compare_op=ALU.is_ge, fill=-FAR,
                                         base=63 + 8 - 16, pattern=[[0, m], [-1, 48]], channel_multiplier=-1))
            pool.sem_inc(nb_set, 1)
            pool.wait_ge(nb_used, 1)
            for a in ATTM:
                step(G.memset(a, 0.0))
            pool.sem_inc(masks_set, 1)
            pool.wait_ge(core_done, 1)
            ada(8, adaw1, acc1, adat1)


_INS = ['x', 'norm_gain', 'w_in', 'b_forget', 'lambda_q1', 'lambda_k1', 'lambda_q2', 'lambda_k2', 'subln_gain',
        'sinks', 'w_up_a', 'w_up_b', 'w_up_c', 'w_o', 'final_gain', 'c_2', 'ctx_2', 'c_ctx_2', 'ada_w_2', 'ada_b_2',
        'norm_mix_w_2', 'norm_ffn_w_2', 'ev_w_in_2', 'ev_w_out_2', 'na_rpb_2', 'hg_lb_logits_2', 'hg_norm_w_2',
        'od_w_in_2', 'od_conv_w_2', 'od_conv_b_2', 'od_w_out_2', 'ffn_w_up_2', 'ffn_conv_w_2', 'ffn_conv_b_2',
        'ffn_w_down_2', 'final_norm_w_2']
_OUTS = [((1, 256, 1024), 'float32')]


def kernel(**inputs):
    import numpy as _np
    import concourse.bacc as _bacc
    from concourse import mybir as _mybir
    from concourse.bass_utils import run_bass_kernel_spmd as _run

    nc = _bacc.Bacc("TRN2", target_bir_lowering=False, num_devices=1)
    arrays, args = {}, []
    for name in _INS:
        a = _np.ascontiguousarray(inputs[name])
        arrays[f"in_{name}_dram"] = a
        args.append(nc.dram_tensor(f"in_{name}_dram", a.shape, _mybir.dt.from_np(a.dtype), kind="ExternalInput").ap())
    for i, (shape, dtype) in enumerate(_OUTS):
        dt = _mybir.dt.from_np(_np.dtype(dtype))
        args.append(nc.dram_tensor(f"out_{i}_dram", shape, dt, kind="ExternalOutput").ap())
    build(nc, *args)
    r = _run(nc, [arrays], core_ids=[0])
    return r.results[0]["out_0_dram"]
```
